# Optimizing a Trainium2 kernel written in Bass

```python
import jax, jax.numpy as jnp
from jax import lax
import numpy as np

D_MODEL = 2048
BATCH = 1
SEQ = 256
DEPTH = 1

MLA_HEADS = 8
MLA_Q_RANK = 512
MLA_KV_RANK = 256
MLA_NOPE = 128
MLA_ROPE = 64
MLA_V = 128
ROPE_THETA = 10000.0
Q_BLOCK = 128
GLA_HEADS = 4
GLA_DK = D_MODEL // 2 // GLA_HEADS
GLA_DV = D_MODEL // GLA_HEADS
GLA_GATE_RANK = 16
GLA_TAU = 16.0
GLA_CHUNK = 64
D_FF = 5632
CONV_WIDTH = 3
EPS = 1e-6

IN_SIZES = (MLA_Q_RANK, MLA_KV_RANK, MLA_ROPE,
            GLA_HEADS * GLA_DK, GLA_HEADS * GLA_DK, GLA_HEADS * GLA_DV,
            GLA_GATE_RANK, GLA_HEADS * GLA_DV,
            D_MODEL, D_MODEL)
IN_OFFSETS = tuple(int(v) for v in np.cumsum(IN_SIZES)[:-1])
D_IN = int(sum(IN_SIZES))

kernel_name = 'hybrid_mla_gla_convffn_block'

def rmsnorm(x, w):
    x32 = x.astype(jnp.float32)
    y = x32 * lax.rsqrt(jnp.mean(x32 * x32, axis=-1, keepdims=True) + EPS)
    return (y * w.astype(jnp.float32)).astype(x.dtype)

def rope_tables(positions):
    inv = 1.0 / (ROPE_THETA ** (jnp.arange(0, MLA_ROPE, 2, dtype=jnp.float32) / MLA_ROPE))
    ang = positions.astype(jnp.float32)[..., None] * inv
    return jnp.cos(ang), jnp.sin(ang)

def apply_rope(x, cos, sin):
    x32 = x.astype(jnp.float32)
    x1, x2 = jnp.split(x32, 2, axis=-1)
    out = jnp.concatenate([x1 * cos - x2 * sin, x2 * cos + x1 * sin], axis=-1)
    return out.astype(x.dtype)

def mla_branch(q_lat, kv_lat, k_rope, positions, g_q, w_q_up, g_kv, w_kv_up):
    B, S, _ = q_lat.shape
    q = (rmsnorm(q_lat, g_q) @ w_q_up).reshape(B, S, MLA_HEADS, MLA_NOPE + MLA_ROPE)
    kv = (rmsnorm(kv_lat, g_kv) @ w_kv_up).reshape(B, S, MLA_HEADS, MLA_NOPE + MLA_V)
    q_nope, q_pe = q[..., :MLA_NOPE], q[..., MLA_NOPE:]
    k_nope, v = kv[..., :MLA_NOPE], kv[..., MLA_NOPE:]
    cos, sin = rope_tables(positions)
    q_pe = apply_rope(q_pe, cos[:, :, None, :], sin[:, :, None, :])
    k_pe = apply_rope(k_rope, cos, sin)
    scale = (MLA_NOPE + MLA_ROPE) ** -0.5
    nb = S // Q_BLOCK
    key_idx = jnp.arange(S)

    def blocks(t):
        return jnp.moveaxis(t.reshape((B, nb, Q_BLOCK) + t.shape[2:]), 1, 0)

    def attend(args):
        qn, qp, start = args
        s = (jnp.einsum('bqhd,bkhd->bhqk', qn, k_nope).astype(jnp.float32)
             + jnp.einsum('bqhr,bkr->bhqk', qp, k_pe).astype(jnp.float32)) * scale
        q_idx = start + jnp.arange(Q_BLOCK)
        mask = key_idx[None, :] <= q_idx[:, None]
        s = jnp.where(mask, s, -jnp.inf)
        p = jax.nn.softmax(s, axis=-1).astype(v.dtype)
        return jnp.einsum('bhqk,bkhd->bqhd', p, v)

    starts = jnp.arange(nb) * Q_BLOCK
    o = lax.map(attend, (blocks(q_nope), blocks(q_pe), starts))
    return jnp.moveaxis(o, 0, 1).reshape(B, S, MLA_HEADS * MLA_V)

def gla_branch(q, k, v, gate_lr, out_gate, w_gate_up, b_gate, g_out):
    B, S, _ = q.shape
    dtype = q.dtype
    nc = S // GLA_CHUNK
    log_a = jax.nn.log_sigmoid((gate_lr @ w_gate_up + b_gate).astype(jnp.float32)) / GLA_TAU

    def heads(t, d):
        return t.reshape(B, nc, GLA_CHUNK, GLA_HEADS, d).transpose(1, 0, 3, 2, 4).astype(jnp.float32)

    qc = heads(q * (GLA_DK ** -0.5), GLA_DK)
    kc = heads(k, GLA_DK)
    vc = heads(v, GLA_DV)
    gc = heads(log_a, GLA_DK)
    causal = jnp.tril(jnp.ones((GLA_CHUNK, GLA_CHUNK), dtype=bool))[:, :, None]

    def step(state, inp):
        qi, ki, vi, gi = inp
        b = jnp.cumsum(gi, axis=-2)
        inter = jnp.einsum('bhcd,bhde->bhce', qi * jnp.exp(b), state)
        diff = b[:, :, :, None, :] - b[:, :, None, :, :]
        decay = jnp.where(causal, jnp.exp(jnp.where(causal, diff, 0.0)), 0.0)
        attn = jnp.einsum('bhid,bhjd,bhijd->bhij', qi, ki, decay)
        intra = jnp.einsum('bhij,bhje->bhie', attn, vi)
        b_last = b[:, :, -1:, :]
        state = (jnp.exp(b_last[:, :, 0, :])[..., None] * state
                 + jnp.einsum('bhcd,bhce->bhde', ki * jnp.exp(b_last - b), vi))
        return state, inter + intra

    s0 = jnp.zeros((B, GLA_HEADS, GLA_DK, GLA_DV), jnp.float32)
    _, o = lax.scan(step, s0, (qc, kc, vc, gc))
    o = o.transpose(1, 0, 3, 2, 4).reshape(B, S, GLA_HEADS, GLA_DV)
    o = rmsnorm(o, g_out).reshape(B, S, GLA_HEADS * GLA_DV).astype(dtype)
    return o * jax.nn.silu(out_gate)

def conv_ffn(h, w_up, conv_w, conv_b, w_down):
    S = h.shape[1]
    u = h @ w_up
    up = jnp.pad(u, ((0, 0), (CONV_WIDTH - 1, 0), (0, 0)))
    acc = up[:, 0:S] * conv_w[0]
    for i in range(1, CONV_WIDTH):
        acc = acc + up[:, i:i + S] * conv_w[i]
    acc = acc + conv_b
    a, val = jnp.split(acc, 2, axis=-1)
    return (jax.nn.gelu(a, approximate=True) * val) @ w_down

def setup_inputs(seed: int = 0) -> dict:
    key = jax.random.key(seed)
    ks = jax.random.split(key, 24)

    def dense(k, shape):
        return jax.random.normal(k, (DEPTH,) + shape, jnp.float32) * (shape[0] ** -0.5)

    def gain(k, n):
        return 1.0 + 0.02 * jax.random.normal(k, (DEPTH, n), jnp.float32)

    def bias(k, n):
        return 0.01 * jax.random.normal(k, (DEPTH, n), jnp.float32)

    return {
        'x': jax.random.normal(ks[0], (BATCH, SEQ, D_MODEL), jnp.float32),
        'c': jax.random.normal(ks[1], (BATCH, D_MODEL), jnp.float32),
        'positions': jnp.broadcast_to(jnp.arange(SEQ, dtype=jnp.int32), (BATCH, SEQ)),
        'w_ada': dense(ks[2], (D_MODEL, 6 * D_MODEL)),
        'b_ada': bias(ks[3], 6 * D_MODEL),
        'g_pre_mix': gain(ks[4], D_MODEL),
        'w_in': dense(ks[5], (D_MODEL, D_IN)),
        'g_q_lat': gain(ks[6], MLA_Q_RANK),
        'w_q_up': dense(ks[7], (MLA_Q_RANK, MLA_HEADS * (MLA_NOPE + MLA_ROPE))),
        'g_kv_lat': gain(ks[8], MLA_KV_RANK),
        'w_kv_up': dense(ks[9], (MLA_KV_RANK, MLA_HEADS * (MLA_NOPE + MLA_V))),
        'w_gla_gate_up': dense(ks[10], (GLA_GATE_RANK, GLA_HEADS * GLA_DK)),
        'b_gla_gate': bias(ks[11], GLA_HEADS * GLA_DK),
        'g_gla_out': gain(ks[12], GLA_DV),
        'w_branch_a': dense(ks[13], (MLA_HEADS * MLA_V, D_MODEL)),
        'w_branch_b': dense(ks[14], (GLA_HEADS * GLA_DV, D_MODEL)),
        'w_mix_out': dense(ks[15], (D_MODEL, D_MODEL)),
        'g_post_mix': gain(ks[16], D_MODEL),
        'g_pre_ffn': gain(ks[17], D_MODEL),
        'w_ffn_up': dense(ks[18], (D_MODEL, 2 * D_FF)),
        'conv_w': jax.random.normal(ks[19], (DEPTH, CONV_WIDTH, 2 * D_FF), jnp.float32) * (CONV_WIDTH ** -0.5),
        'conv_b': bias(ks[20], 2 * D_FF),
        'w_ffn_down': dense(ks[21], (D_FF, D_MODEL)),
        'g_post_ffn': gain(ks[22], D_MODEL),
    }

def reference(x, c, positions, w_ada, b_ada, g_pre_mix, w_in, g_q_lat, w_q_up, g_kv_lat,
              w_kv_up, w_gla_gate_up, b_gla_gate, g_gla_out, w_branch_a, w_branch_b,
              w_mix_out, g_post_mix, g_pre_ffn, w_ffn_up, conv_w, conv_b, w_ffn_down,
              g_post_ffn):
    c_act = jax.nn.silu(c)
    for l in range(DEPTH):
        mod = (c_act @ w_ada[l] + b_ada[l])[:, None, :]
        shift_m, scale_m, gate_m, shift_f, scale_f, gate_f = jnp.split(mod, 6, axis=-1)

        h = rmsnorm(x, g_pre_mix[l]) * (1 + scale_m) + shift_m
        z = h @ w_in[l]
        (q_lat, kv_lat, k_rope, gq, gk, gv, g_lr, g_og, gate_a, gate_b) = jnp.split(z, IN_OFFSETS, axis=-1)
        y_a = mla_branch(q_lat, kv_lat, k_rope, positions, g_q_lat[l], w_q_up[l],
                         g_kv_lat[l], w_kv_up[l]) @ w_branch_a[l]
        y_b = gla_branch(gq, gk, gv, g_lr, g_og, w_gla_gate_up[l], b_gla_gate[l],
                         g_gla_out[l]) @ w_branch_b[l]
        merged = jax.nn.sigmoid(gate_a) * y_a + jax.nn.sigmoid(gate_b) * y_b
        y = merged @ w_mix_out[l]
        x = x + gate_m * rmsnorm(y, g_post_mix[l])

        h = rmsnorm(x, g_pre_ffn[l]) * (1 + scale_f) + shift_f
        f = conv_ffn(h, w_ffn_up[l], conv_w[l], conv_b[l], w_ffn_down[l])
        x = x + gate_f * rmsnorm(f, g_post_ffn[l])
    return x


_drawn_inputs = setup_inputs


def setup_inputs(seed=0):
    import zlib

    import numpy as np

    out = dict(_drawn_inputs(seed))
    spreads = {}
    factors = {'g_q_lat': 8.0,
     'g_kv_lat': 8.0,
     'b_gla_gate': 8.0,
     'g_gla_out': 27.17,
     'g_post_mix': 5.118,
     'g_pre_ffn': 13.495,
     'conv_b': 31.135,
     'g_post_ffn': 22.482}
    for name, (base, spread) in spreads.items():
        noise = np.random.default_rng([zlib.crc32(name.encode()), seed]).standard_normal(out[name].shape)
        drawn = base * np.exp(spread * noise) if base else spread * noise
        out[name] = __import__('jax').numpy.asarray(drawn.astype(out[name].dtype))
    for name, factor in factors.items():
        out[name] = (out[name] * factor).astype(out[name].dtype)
    return out
```

```python
from contextlib import ExitStack

import numpy as np

import concourse.bass as bass
from concourse import mybir

P = 128
F32 = mybir.dt.float32
F32R = mybir.dt.float32r
I32 = mybir.dt.int32
U8 = mybir.dt.uint8
ALU = mybir.AluOpType
ACT = mybir.ActivationFunctionType
AX = mybir.AxisListType.X

D = 2048
S = 256
NT = S // P
H = 8
NOPE, ROPE, VD = 128, 64, 128
QR, KVR = 512, 256
GH = 4
DK, DV = D // 2 // GH, D // GH
GR = 16
TAU = 16.0
FF = 5632
KT = D // P
EPS = 1e-6
THETA = 10000.0

C_Q = 0
C_KV = C_Q + QR
C_KR = C_KV + KVR
C_GQ = C_KR + ROPE
C_GK = C_GQ + GH * DK
C_GV = C_GK + GH * DK
C_LR = C_GV + GH * DV
C_OG = C_LR + GR
C_GA = C_OG + GH * DV
C_GB = C_GA + D

UC = 512
AC = 1024
RING = 4
ADA_BLOCK = D // P * (D // AC)
MLA_SCALE = float(NOPE + ROPE) ** -0.5
GLA_SCALE = float(DK) ** -0.5
LEVELS = 9

V_BADA, V_C, V_GPRE = 0, 96, 112
V_GQ, V_GKV, V_BGLA, V_GOUT, V_GFFN, V_CB = 128, 132, 134, 142, 146, 162
V_CW = 256
V_END = V_CW + 3 * 2 * FF // P

GROUPS = ([("misc", 8, 4), ("qlat", 8, 4)] + [("gq", 8, 4)] * 2
          + [("qup", 2, 4)] * 3 + [("kup", 2, 8)] + [("vup", 2, 4)]
          + [("gk", 8, 4)] * 2 + [("gv", 8, 2)] * 4 + [("og", 8, 4)] * 4
          + [("ga", 8, 4)] * 4 + [("gb", 8, 4)] * 4 + [("ba", 4, 4)] * 4 + [("bb", 8, 4)] * 4
          + [("mix", 8, 2)] * 4 + [("ffn", 8, 4)] * 22 + [("down", 22, 2)] * 4)


def starts(name):
    u = t = p = 0
    a = 2 * ADA_BLOCK
    for kind, nu, nt in GROUPS:
        if kind == name:
            return u, t, p, a
        u, t, p = u + nu, t + nt, p + nu // 2 - 1
        if nu in (4, 8) and a < 6 * ADA_BLOCK:
            a += nu // 2
    return u, t, p, a


UNITS = starts("end")[0]
FIRST_OF = {g[0]: starts(g[0]) for g in GROUPS}


def level_masks():
    j, i = np.arange(P)[:, None], np.arange(P)[None, :]
    out = [i == j]
    for lv in range(1, LEVELS - 1):
        h = 1 << (lv - 1)
        out.append((i // (2 * h) == j // (2 * h)) & (j % (2 * h) < h) & (i % (2 * h) >= h))
    return np.concatenate(out, axis=1).astype(np.int32)


def constants():
    ident = np.eye(P, dtype=np.float32)
    rot = np.zeros((P, P), np.float32)
    for b in (0, ROPE):
        for m in range(ROPE // 2):
            rot[b + m + ROPE // 2, b + m] = -1.0
            rot[b + m, b + m + ROPE // 2] = 1.0
    q, k = np.arange(P)[:, None], np.arange(P)[None, :]
    causal = np.where(k <= q, 0.0, -1e30).astype(np.float32)
    inv = 1.0 / (np.float32(THETA) ** (np.arange(0, ROPE, 2, dtype=np.float32) / np.float32(ROPE)))
    inv = np.tile(inv.astype(np.float32), 4)[:, None]
    return np.ascontiguousarray(np.concatenate([ident, rot, causal, inv], axis=1))


def build(nc, ap, out):
    (x, c, positions, w_ada, b_ada, g_pre_mix, w_in, g_q_lat, w_q_up, g_kv_lat, w_kv_up, w_gla_gate_up,
     b_gla_gate, g_gla_out, w_branch_a, w_branch_b, w_mix_out, g_post_mix, g_pre_ffn, w_ffn_up, conv_w,
     conv_b, w_ffn_down, g_post_ffn, const_f, const_m) = ap
    ctx = ExitStack()
    with ctx:
        def sb(name, shape, dt):
            return ctx.enter_context(nc.sbuf_tensor(name, shape, dt))

        def sem(name):
            return ctx.enter_context(nc.semaphore(name))

        raw = sb("raw", [P, RING, 2, UC], F32)
        w_hi = sb("w_hi", [P, RING, 2, UC], F32R)
        w_lo = sb("w_lo", [P, RING, 2, UC], F32R)
        acc = sb("acc", [P, D], F32)
        fixed = sb("fixed", [P, 3 * P + 1], F32)
        ident, rot, causal = (fixed[:, i * P:(i + 1) * P] for i in range(3))
        inv_freq = fixed[:, 3 * P:3 * P + 1]
        ones = sb("ones", [P, P], F32)
        masks = sb("masks", [P, LEVELS - 1, P], U8)
        cos_t = sb("cos_t", [P, S], F32)
        sin_t = sb("sin_t", [P, S], F32)
        vec = sb("vec", [P, V_END], F32)
        c_act = sb("c_act", [P, KT], F32)
        mod = sb("mod", [P, 6, KT], F32)
        cross = sb("cross", [P, 2, S], F32)
        ytmp = sb("ytmp", [P, 2, S], F32)
        eps_t = sb("eps_t", [P, 1], F32)
        stat = sb("stat", [P, 32], F32)
        cap_kb = 139 * 1024

        def at(kb, name, shape, dt, size_kb):
            words = 1
            for n in shape[1:]:
                words *= n
            assert words * 4 <= size_kb * 1024 and (kb + size_kb) * 1024 <= cap_kb, name
            with nc.sbuf_tensor(name + "_before", [P, max(kb, 0) * 256 + 8], F32):
                with nc.sbuf_tensor(name, shape, dt) as t:
                    pass
            return t

        ada = at(0, "ada", [P, RING, AC], F32, 16)
        conv_in = at(0, "conv_in", [P, 4, S + 2], F32, 5)
        conv_a = at(5, "conv_a", [P, 4, S], F32, 4)
        conv_v = at(9, "conv_v", [P, 2, S], F32, 2)
        hid_f = at(11, "hid_f", [P, 2, S], F32, 2)
        B = 16
        cap_kb = (B + 137) * 1024
        ht = at(B + 0, "ht", [P, KT, 2, S], F32R, 32)
        ot = at(B + 32, "ot", [P, H, 2, S], F32R, 16)
        og = at(B + 48, "og", [P, KT, S], F32, 16)
        v_gla = at(B + 64, "v_gla", [P, NT, GH * DV], F32, 16)
        q_gla = at(B + 80, "q_gla", [P, 8, S], F32, 8)
        k_gla = at(B + 88, "k_gla", [P, 8, S], F32, 8)
        x_tok = at(B + 96, "x_tok", [P, NT, D], F32, 16)
        xn_tok = at(B + 112, "xn_tok", [P, NT, D], F32, 16)
        xn_t = at(B + 48, "xn_t", [P, KT, S], F32, 16)
        h_f = at(B + 64, "h_f", [P, KT, S], F32, 16)
        junk = at(B + 80, "junk", [P, D], F32, 8)
        rows = at(B + 88, "rows", [P, 5, P], F32, 3)
        pos_i = at(B + 32, "pos_i", [P, S], I32, 1)
        pos_f = at(B + 33, "pos_f", [P, S], F32, 1)
        ang = at(B + 34, "ang", [P, S], F32, 1)
        turn = at(B + 35, "turn", [P, 2, S], F32, 2)
        red = at(B + 37, "red", [P, 2, S], F32, 2)
        masks_i = at(B + 39, "masks_i", [P, LEVELS - 1, P], I32, 4)
        lat = at(B + 48, "lat", [P, 6, S], F32, 6)
        lat_s = at(B + 54, "lat_s", [P, 6, 2, S], F32R, 12)
        lat_sq = at(B + 66, "lat_sq", [P, 6, S], F32, 6)
        q_rope_in = at(B + 72, "q_rope_in", [P, 4, S], F32, 4)
        rope_tmp = at(B + 76, "rope_tmp", [P, 2, S], F32, 2)
        lat_r = at(B + 78, "lat_r", [P, 2, S], F32, 2)
        q_nope = at(B + 96, "q_nope", [P, H, S], F32, 8)
        k_nope = at(B + 104, "k_nope", [P, H, S], F32, 8)
        v_mla = at(B + 112, "v_mla", [P, NT, H * VD], F32, 8)
        q_rope = at(B + 120, "q_rope", [P, 4, S], F32, 4)
        k_rope = at(B + 124, "k_rope", [P, S], F32, 1)
        probs = at(B + 125, "probs", [P, 3, 4 * P], F32, 6)
        probs_t = at(B + 131, "probs_t", [P, 2, 3 * P], F32, 3)
        k_rope_in = at(B + 134, "k_rope_in", [P, S], F32, 1)
        lr_t = at(B + 135, "lr_t", [P, S], F32, 1)
        soft = at(B + 136, "soft", [P, 3, 8], F32, 1)
        w_gate = at(B + 48, "w_gate", [P, GH * DK], F32, 4)
        pre = at(B + 96, "pre", [P, 8, S], F32, 8)
        suf = at(B + 104, "suf", [P, 8, S], F32, 8)
        dec = at(B + 112, "dec", [P, 8, S], F32, 8)
        qk = at(B + 120, "qk", [P, 8, S], F32, 8)
        attn0 = at(B + 128, "attn0", [P, GH, S], F32, 4)
        attn1 = at(B + 132, "attn1", [P, GH, P], F32, 2)
        o_gla = at(B + 96, "o_gla", [P, KT, S], F32, 16)
        o_sq = at(B + 112, "o_sq", [P, 4, S], F32, 4)
        o_r = at(B + 128, "o_r", [P, GH, S], F32, 4)
        og_s = at(B + 0, "og_s", [P, KT, 2, S], F32R, 32)
        gate_a = at(B + 80, "gate_a", [P, KT, S], F32, 16)
        gate_b = at(B + 112, "gate_b", [P, KT, S], F32, 16)
        merged = at(B + 32, "merged", [P, KT, 2, S], F32R, 32)
        gg_m = at(B + 64, "gg_m", [P, D], F32, 8)
        gpost_m = at(B + 72, "gpost_m", [P, D], F32, 8)
        brow_m = at(B + 128, "brow_m", [P, UC], F32, 2)
        x_again = at(B + 96, "x_again", [P, NT, D], F32, 16)
        x1 = at(B + 121, "x1", [P, NT, D], F32, 16)
        xn1 = at(B + 80, "xn1", [P, NT, D], F32, 16)
        h2_f = at(B + 32, "h2_f", [P, KT, S], F32, 16)
        junk_m = at(B + 112, "junk_m", [P, D], F32, 8)
        h2t = at(B + 0, "h2t", [P, KT, 2, S], F32R, 32)
        hid = at(B + 32, "hid", [P, FF // P, 2, S], F32R, 88)
        f_tok = at(B + 0, "f_tok", [P, NT, D], F32, 16)
        gg_f = at(B + 16, "gg_f", [P, D], F32, 8)
        gpost_f = at(B + 24, "gpost_f", [P, D], F32, 8)
        junk_f = at(5, "junk_f", [P, UC], F32, 2)
        brow_f = at(13, "brow_f", [P, UC], F32, 2)

        ps = ctx.enter_context(nc.psum_tensor("ps", [P, 8, UC], F32))

        x_loaded, rows_loaded, const_loaded = sem("x_loaded"), sem("rows_loaded"), sem("const_loaded")
        gate_w_loaded, post_loaded, x_again_loaded = sem("gate_w_loaded"), sem("post_loaded"), sem("x_again_loaded")
        post_f_loaded, bias_f_loaded, stored = sem("post_f_loaded"), sem("bias_f_loaded"), sem("stored")
        raw_loaded = [sem(f"raw_loaded{r}") for r in range(RING)]
        ada_loaded = [sem(f"ada_loaded{r}") for r in range(RING)]
        hi_done, lo_done = sem("hi_done"), sem("lo_done")
        pairs_used = sem("pairs_used")
        tile_ready = sem("tile_ready")
        tile_half = sem("tile_half")
        tile_empty = sem("tile_empty")
        ada_used = sem("ada_used")
        acc_zero, acc_read = sem("acc_zero"), sem("acc_read")
        mod_ready, mod_psum = sem("mod_ready"), sem("mod_psum")
        dve_step, act_step, pool_step = sem("dve_step"), sem("act_step"), sem("pool_step")
        setup_done = sem("setup_done")
        rows_t, vec_ready, c_ready = sem("rows_t"), sem("vec_ready"), sem("c_ready")
        ssq_x, rms_x, norm_x, xt_psum, xt_copied = (sem("ssq_x"), sem("rms_x"), sem("norm_x"), sem("xt_psum"),
                                                    sem("xt_copied"))
        h_ready, h_hi, h_lo = sem("h_ready"), sem("h_hi"), sem("h_lo")
        angle_ready, table_ready = sem("angle_ready"), sem("table_ready")
        lat_squared, lat_summed, lat_rms, lat_normed, lat_hi, lat_lo = (
            sem("lat_squared"), sem("lat_summed"), sem("lat_rms"), sem("lat_normed"), sem("lat_hi"), sem("lat_lo"))
        rot_ready, rope_done = sem("rot_ready"), sem("rope_done")
        scores_ready, max_ready, exp_done, probs_ready = (sem("scores_ready"), sem("max_ready"), sem("exp_done"),
                                                          sem("probs_ready"))
        pt_ready, pt_copied, ctx_ready, ctx_hi, ctx_lo = (sem("pt_ready"), sem("pt_copied"), sem("ctx_ready"),
                                                          sem("ctx_hi"), sem("ctx_lo"))
        gate_psum, gate_pre, gate_soft, decay_ready = (sem("gate_psum"), sem("gate_pre"), sem("gate_soft"),
                                                       sem("decay_ready"))
        dec_ready, qk_ready, scan_ready, level_ready, level_taken = (
            sem("dec_ready"), sem("qk_ready"), sem("scan_ready"), sem("level_ready"), sem("level_taken"))
        og_psum, og_copied, og_squared, og_summed, og_rms, og_silu, og_gated, og_hi, og_lo = (
            sem("og_psum"), sem("og_copied"), sem("og_squared"), sem("og_summed"), sem("og_rms"), sem("og_silu"),
            sem("og_gated"), sem("og_hi"), sem("og_lo"))
        sig_done, mul_done, merged_ready, merged_hi, merged_lo = (
            sem("sig_done"), sem("mul_done"), sem("merged_ready"), sem("merged_hi"), sem("merged_lo"))
        gate_row, gg_ready = sem("gate_row"), sem("gg_ready")
        rms_y, x1_ready, ssq_1, rms_1, norm_1, x1t_psum, h2_ready, h2_hi, h2_lo = (
            sem("rms_y"), sem("x1_ready"), sem("ssq_1"), sem("rms_1"), sem("norm_1"), sem("x1t_psum"),
            sem("h2_ready"), sem("h2_hi"), sem("h2_lo"))
        conv_first, conv_done, gelu_done, hid_ready, hid_hi, hid_lo = (
            sem("conv_first"), sem("conv_done"), sem("gelu_done"), sem("hid_ready"), sem("hid_hi"), sem("hid_lo"))
        sum_f, rms_f, out_ready = sem("sum_f"), sem("rms_f"), sem("out_ready")

        def halves(t, h):
            v = t[:, :, :].rearrange("p d (b s h) -> p (d b) s h", s=2, h=h)
            return v[:, :, 0, :], v[:, :, 1, :]

        def spread(col, like):
            return col.to_broadcast(list(like.shape))

        class Steps:

            def __init__(self, eng, s):
                self.eng, self.s, self.n = eng, s, 0

            def mark(self, ins):
                ins.then_inc(self.s, 1)
                self.n = self.n + 1

            def wait(self):
                self.eng.wait_ge(self.s, self.n)

        block = ctx.enter_context(nc.Block())

        @block.sync
        def _(sp):
            def load_unit(u, r, src):
                if not isinstance(u, int) or u >= RING:
                    sp.wait_ge(lo_done, u - (RING - 1))
                sp.dma_start(raw[:, r], src).then_inc(raw_loaded[r], 16)

            def load_ada(a, r, src):
                if not isinstance(a, int) or a >= RING:
                    sp.wait_ge(ada_used, a - (RING - 1))
                sp.dma_start(ada[:, r], src).then_inc(ada_loaded[r], 16)

            def two_kt(w, row0, col0):
                return w[bass.ds(row0, 2 * P), bass.ds(col0, UC)].rearrange("(k p) n -> p k n", p=P)

            def ada_src(block_no, kt, half):
                return w_ada[bass.ds(kt * P, P), bass.ds(block_no * D + half * AC, AC)]

            def group(u0, nu, src, a0=None, a_block=None, a_kt=None, slot0=0):
                for j in range(nu):
                    load_unit(u0 + j, (slot0 + j) % RING, src(j))
                    if a0 is not None and j % 2 == 1:
                        n = j // 2
                        load_ada(a0 + n, n % RING, ada_src(a_block, a_kt + n // 2, n % 2))

            sp.dma_start(x_tok[:], x[0].rearrange("(t p) d -> p t d", p=P)).then_inc(x_loaded, 16)
            n_small = 0

            def small(dst, src):
                sp.dma_start(dst, src).then_inc(rows_loaded, 16)

            def as_rows(v):
                return v.rearrange("(r c) -> r c", c=P)

            for dst0, v in ((0, b_ada[0]), (96, c[0]), (112, g_pre_mix[0])):
                n = v.shape[0] // P
                small(rows[dst0:dst0 + n, 0, :], as_rows(v))
            for v0, v in ((V_GQ, g_q_lat[0]), (V_GKV, g_kv_lat[0]), (V_BGLA, b_gla_gate[0]), (V_GOUT, g_gla_out[0]),
                          (V_GFFN, g_pre_ffn[0]), (V_CB, conv_b[0])):
                n = v.shape[0] // P
                small(rows[v0 - P:v0 - P + n, 1, :], as_rows(v))
            cw = conv_w[0].rearrange("i (r c) -> (i r) c", c=P)
            for k in range(3):
                n = min(P, cw.shape[0] - k * P)
                small(rows[0:n, 2 + k, :], cw[k * P:k * P + n, :])
            sp.dma_start(fixed[:], const_f).then_inc(const_loaded, 16)
            sp.dma_start(masks_i[:, :, :].rearrange("p l n -> p (l n)"), const_m).then_inc(const_loaded, 16)
            sp.dma_start(pos_i[:], positions[0:1, :].to_broadcast([P, S])).then_inc(const_loaded, 16)

            for a in range(RING):
                load_ada(a, a, ada_src(0, a // 2, a % 2))
            with sp.Fori(1, KT // 2) as i:
                for r in range(RING):
                    load_ada(4 * i + r, r, ada_src(0, 2 * i + r // 2, r % 2))
            with sp.Fori(0, KT // 2) as i:
                for r in range(RING):
                    load_ada(ADA_BLOCK + 4 * i + r, r, ada_src(1, 2 * i + r // 2, r % 2))

            u0, _, _, a0 = FIRST_OF["misc"]
            for j in range(8):
                r = j % RING
                rs = w_in[j * 2 * P:(j + 1) * 2 * P, :].rearrange("(k p) n -> p k n", p=P)
                if j >= RING:
                    sp.wait_ge(lo_done, j - (RING - 1))
                sp.dma_start(raw[:, r, :, 0:320], rs[:, :, C_KV:C_KV + 320]).then_inc(raw_loaded[r], 16)
                sp.dma_start(raw[:, r, :, 320:384], rs[:, :, C_KR:C_KR + ROPE]).then_inc(raw_loaded[r], 16)
                sp.dma_start(raw[:, r, :, 384:512], rs[:, :, C_LR:C_LR + P]).then_inc(raw_loaded[r], 16)
                if j % 2 == 1:
                    n = j // 2
                    load_ada(a0 + n, n, ada_src(3, n // 2, n % 2))
            u0, _, _, a0 = FIRST_OF["qlat"]
            group(u0, 8, lambda j: two_kt(w_in, 256 * j, C_Q), a0, 3, 2)
            u0, _, _, a0 = FIRST_OF["gq"]
            with sp.Fori(0, 2) as g:
                group(u0 + 8 * g, 8, lambda j: two_kt(w_in, 256 * j, C_GQ + UC * g), a0 + 4 * g, 3, 4 + 2 * g)
            u0 = FIRST_OF["qup"][0]
            qv = w_q_up.rearrange("(k p) (h e) -> p k h e", p=P, e=NOPE + ROPE)
            for n in range(6):
                g, j = n // 2, n % 2
                r = (u0 + n) % RING
                sp.wait_ge(lo_done, u0 + n - (RING - 1))
                for k in range(2):
                    if g < 2:
                        dst = raw[:, r, k, :].rearrange("p (h e) -> p h e", h=4)
                        sp.dma_start(dst, qv[:, 2 * j + k, 4 * g:4 * g + 4, 0:NOPE]).then_inc(raw_loaded[r], 8 * 2)
                    else:
                        dst = raw[:, r, k, :].rearrange("p (h e) -> p h e", h=H)
                        sp.dma_start(dst, qv[:, 2 * j + k, :, NOPE:NOPE + ROPE]).then_inc(raw_loaded[r], 8 * 2)
            u0 = FIRST_OF["kup"][0]
            kvv = w_kv_up.rearrange("(k p) (h e) -> p k h e", p=P, e=NOPE + VD)
            for n in range(4):
                part, hh = n // 2, n % 2
                r = (u0 + n) % RING
                sp.wait_ge(lo_done, u0 + n - (RING - 1))
                for k in range(2):
                    dst = raw[:, r, k, :].rearrange("p (h e) -> p h e", h=4)
                    sp.dma_start(dst, kvv[:, k, 4 * hh:4 * hh + 4, part * NOPE:part * NOPE + P])\
                        .then_inc(raw_loaded[r], 16)
            s0 = FIRST_OF["gk"][0] % RING
            u0, _, _, a0 = FIRST_OF["gk"]
            with sp.Fori(0, 2) as g:
                group(u0 + 8 * g, 8, lambda j: two_kt(w_in, 256 * j, C_GK + UC * g), a0 + 4 * g, 3, 8 + 2 * g, s0)
            sp.wait_ge(tile_ready, FIRST_OF["gk"][1])
            sp.dma_start(w_gate[0:GR, :], w_gla_gate_up).then_inc(gate_w_loaded, 16)
            u0, _, _, a0 = FIRST_OF["gv"]
            with sp.Fori(0, 2) as g:
                group(u0 + 8 * g, 8, lambda j: two_kt(w_in, 256 * j, C_GV + UC * g), a0 + 4 * g, 3, 12 + 2 * g, s0)
            with sp.Fori(2, 4) as g:
                group(u0 + 8 * g, 8, lambda j: two_kt(w_in, 256 * j, C_GV + UC * g), a0 + 4 * g, 4, 2 * g - 4, s0)
            u0, _, _, a0 = FIRST_OF["og"]
            with sp.Fori(0, 6) as g:
                group(u0 + 8 * g, 8, lambda j: two_kt(w_in, 256 * j, C_OG + UC * g), a0 + 4 * g, 4, 4 + 2 * g, s0)
            with sp.Fori(6, 12) as g:
                group(u0 + 8 * g, 8, lambda j: two_kt(w_in, 256 * j, C_OG + UC * g), a0 + 4 * g, 2, 2 * g - 12, s0)
            sp.wait_ge(og_psum, 8)
            sp.dma_start(gpost_m[:], g_post_mix[0:1, :].to_broadcast([P, D])).then_inc(post_loaded, 16)
            u0, _, _, a0 = FIRST_OF["ba"]
            with sp.Fori(0, 2) as g:
                for n in range(2):
                    group(u0 + 8 * g + 4 * n, 4, lambda j: two_kt(w_branch_a, 256 * j, 2 * UC * g + UC * n),
                          None, None, None, s0)
                    for m in range(2):
                        load_ada(a0 + 4 * g + 2 * n + m, 2 * n + m, ada_src(2, 12 + 2 * g + n, m))
            sp.wait_ge(og_gated, 4)
            for b in range(4):
                c0 = 2 * D + b * UC
                sp.dma_start(brow_m[32 * b:32 * b + 1, :], b_ada[0:1, c0:c0 + UC]).then_inc(post_loaded, 16)
            u0, _, _, a0 = FIRST_OF["bb"]
            with sp.Fori(0, 4) as g:
                group(u0 + 8 * g, 8, lambda j: two_kt(w_branch_b, 256 * j, UC * g), a0 + 4 * g, 5, 2 * g, s0)
            sp.wait_ge(og_lo, 4)
            sp.dma_start(x_again[:], x[0].rearrange("(t p) d -> p t d", p=P)).then_inc(x_again_loaded, 16)
            u0, _, _, a0 = FIRST_OF["mix"]
            with sp.Fori(0, 4) as g:
                group(u0 + 8 * g, 8, lambda j: two_kt(w_mix_out, 256 * j, UC * g), a0 + 4 * g, 5, 8 + 2 * g, s0)
            u0 = FIRST_OF["ffn"][0]
            with sp.Fori(0, 11) as g:
                for part in range(2):
                    group(u0 + 16 * g + 8 * part, 8,
                          lambda j: two_kt(w_ffn_up, 256 * j, part * FF + UC * g), None, None, None, s0)
            for b in range(4):
                c0 = 5 * D + b * UC
                sp.dma_start(brow_f[32 * b:32 * b + 1, :], b_ada[0:1, c0:c0 + UC]).then_inc(bias_f_loaded, 16)
            u0, t0, _, _ = FIRST_OF["down"]
            for n in range(4):
                for j in range(22):
                    load_unit(u0 + 22 * n + j, (s0 + 22 * n + j) % RING, two_kt(w_ffn_down, 256 * j, UC * n))
                    if n == 0 and j == RING:
                        sp.wait_ge(tile_ready, t0)
                        sp.dma_start(gpost_f[:], g_post_ffn[0:1, :].to_broadcast([P, D])).then_inc(post_f_loaded, 16)
            for n in range(4):
                t, c0 = n // 2, (n % 2) * (D // 2)
                sp.wait_ge(out_ready, n + 1)
                sp.dma_start(out[0, t * P:(t + 1) * P, c0:c0 + D // 2], f_tok[:, t, c0:c0 + D // 2])\
                    .then_inc(stored, 16)
            sp.wait_ge(stored, 64)

        @block.tensor
        def _(pe):
            mm = nc.tensor.matmul

            def tile_free(t):
                if not isinstance(t, int) or t >= 4:
                    pe.wait_ge(tile_empty, t - 3)

            def feature_pair(u, t0, kt0, pairs, last, moving, slot, first):
                pe.wait_ge(lo_done, u + 2)
                for f in range(4):
                    if first:
                        tile_free(t0 + f)
                    for j in range(2):
                        s = (slot + j) % RING
                        for k in range(2):
                            kt = kt0 + 2 * j + k
                            start = first and j == 0 and k == 0
                            stop = last and j == 1 and k == 1
                            cols = slice(f * P, (f + 1) * P)
                            mm(ps[:, f, :], w_hi[:, s, k, cols], moving[:, kt].rearrange("p a t -> p (a t)"),
                               start=start, stop=False)
                            ins = mm(ps[:, f, 0:S], w_lo[:, s, k, cols], moving[:, kt, 0], start=False, stop=stop)
                    if last:
                        ins.then_inc(tile_ready, 1)
                if not last:
                    ins.then_inc(pairs_used, 1)

            def feature_group(u0, t0, nu, moving, slot, kt0=0):
                for j in range(0, nu, 2):
                    feature_pair(u0 + j, t0, kt0 + 2 * j, nu // 2, j == nu - 2, moving, (slot + j) % RING, j == 0)

            def token_group(u0, t0, nu, still, slot, bank0):
                for j in range(0, nu, 2):
                    first, last = j == 0, j == nu - 2
                    pe.wait_ge(lo_done, u0 + j + 2)
                    for t in range(NT):
                        if first:
                            tile_free(t0 + t)
                        o = ps[:, bank0 + t, :]
                        for i in range(2):
                            s = (slot + j + i) % RING
                            for k in range(2):
                                kt = 2 * (j + i) + k
                                tok = slice(t * P, (t + 1) * P)
                                start = first and i == 0 and k == 0
                                mm(o, still[:, kt, 0, tok], w_hi[:, s, k, :], start=start, stop=False)
                                mm(o, still[:, kt, 0, tok], w_lo[:, s, k, :], start=False, stop=False)
                                ins = mm(o, still[:, kt, 1, tok], w_hi[:, s, k, :], start=False,
                                         stop=last and i == 1 and k == 1)
                        if last:
                            ins.then_inc(tile_ready, 1)
                    if not last:
                        ins.then_inc(pairs_used, 1)

            def mod_columns(n_block, used):
                pe.wait_ge(ada_used, used)
                if n_block:
                    pe.wait_ge(mod_ready, n_block)
                for i in range(KT):
                    ins = mm(ps[:, 4, i:i + 1], acc[:, i * P:(i + 1) * P], ones[:, 0:1], start=True, stop=True)
                ins.then_inc(mod_psum, 1)

            pe.wait_ge(rows_loaded, 12 * 16)
            pe.wait_ge(const_loaded, 3 * 16)
            for k in range(5):
                n = (P, P - 6, P, P, V_END - V_CW - 2 * P)[k]
                ins = nc.tensor.transpose(ps[:, 4 + k // 4, (k % 4) * P:(k % 4) * P + n], rows[0:n, k, :],
                                          ident[0:n, 0:n])
            ins.then_inc(rows_t, 1)
            pe.wait_ge(norm_x, 2)
            pe.wait_ge(vec_ready, 1)
            for b in range(8):
                for q in range(4):
                    kt, t = 2 * b + q // 2, q % 2
                    ins = nc.tensor.transpose(ps[:, b, q * P:(q + 1) * P], xn_tok[:, t, kt * P:(kt + 1) * P], ident[:])
                ins.then_inc(xt_psum, 1)
            pe.wait_ge(xt_copied, 8)
            pe.wait_ge(setup_done, 2)
            mod_columns(0, ADA_BLOCK)
            mod_columns(1, 2 * ADA_BLOCK)
            pe.wait_ge(h_lo, 4)
            feature_group(0, 0, 8, ht, 0)
            feature_group(8, 4, 8, ht, 0)
            u0, t0, _, _ = FIRST_OF["gq"]
            feature_group(u0, t0, 8, ht, 0)
            pe.wait_ge(lat_squared, 1)
            pe.wait_ge(mod_ready, 2)
            for n, (f0, nf) in enumerate(((0, 2), (2, 4))):
                for i in range(nf):
                    ins = mm(ps[:, 4, n * S:(n + 1) * S], ones[:], lat_sq[:, f0 + i, :], start=i == 0, stop=i == nf - 1)
            ins.then_inc(lat_summed, 1)
            feature_group(u0 + 8, t0 + 4, 8, ht, 0)
            pe.wait_ge(lat_lo, 1)
            u0, t0, _, _ = FIRST_OF["qup"]
            for g in range(3):
                feature_group(u0 + 2 * g, t0 + 4 * g, 2, lat_s, (u0 + 2 * g) % RING, 2)
            u0, t0, _, _ = FIRST_OF["kup"]
            pe.wait_ge(lo_done, u0 + 2)
            for n in range(8):
                f, s = n % 4, (u0 + n // 4) % RING
                tile_free(t0 + n)
                for k in range(2):
                    cols = slice(f * P, (f + 1) * P)
                    mm(ps[:, f, :], w_hi[:, s, k, cols], lat_s[:, k].rearrange("p a t -> p (a t)"), start=k == 0,
                       stop=False)
                    ins = mm(ps[:, f, 0:S], w_lo[:, s, k, cols], lat_s[:, k, 0], start=False, stop=k == 1)
                ins.then_inc(tile_ready, 1)
            u0, t0, _, _ = FIRST_OF["vup"]
            pe.wait_ge(lo_done, u0 + 2)
            for n in range(4):
                half, t = n // 2, n % 2
                s = (u0 + half) % RING
                tile_free(t0 + n)
                tok = slice(t * P, (t + 1) * P)
                for k in range(2):
                    mm(ps[:, n, :], lat_s[:, k, 0, tok], w_hi[:, s, k, :], start=k == 0, stop=False)
                    mm(ps[:, n, :], lat_s[:, k, 0, tok], w_lo[:, s, k, :], start=False, stop=False)
                    ins = mm(ps[:, n, :], lat_s[:, k, 1, tok], w_hi[:, s, k, :], start=False, stop=k == 1)
                ins.then_inc(tile_ready, 1)

            def rope_rotate():
                pe.wait_ge(tile_empty, FIRST_OF["kup"][1])
                pe.wait_ge(lat_rms, 1)
                for i in range(4):
                    mm(ps[:, 4 + i // 2, (i % 2) * S:(i % 2 + 1) * S], rot[:], q_rope_in[:, i, :], start=True, stop=True)
                mm(ps[:, 6, 0:S], rot[:], k_rope_in[:], start=True, stop=True).then_inc(rot_ready, 1)

            def scores(h):
                if h == 0:
                    pe.wait_ge(rope_done, 5)
                    pe.wait_ge(tile_empty, FIRST_OF["vup"][1])
                else:
                    pe.wait_ge(max_ready, h)
                p0 = ROPE * (h % 2)
                for t in range(NT):
                    o = ps[:, 4, t * P:t * P + (t + 1) * P]
                    tok, keys = slice(t * P, (t + 1) * P), slice(0, (t + 1) * P)
                    mm(o, q_nope[:, h, tok], k_nope[:, h, keys], start=True, stop=False)
                    ins = mm(o, q_rope[p0:p0 + ROPE, h // 2, tok], k_rope[p0:p0 + ROPE, keys], start=False, stop=True)
                ins.then_inc(scores_ready, 1)

            def transpose_probs(h):
                pe.wait_ge(probs_ready, h + 1)
                if h:
                    pe.wait_ge(pt_copied, h)
                for i in range(3):
                    ins = nc.tensor.transpose(ps[:, 5, i * P:(i + 1) * P], probs[:, h % 3, i * P:(i + 1) * P], ident[:])
                ins.then_inc(pt_ready, 1)

            def context(h):
                pe.wait_ge(pt_copied, h + 1)
                if h:
                    pe.wait_ge(ctx_lo, h)
                else:
                    pe.wait_ge(tile_empty, FIRST_OF["gk"][1])
                hv = slice(h * VD, (h + 1) * VD)
                mm(ps[:, 6, 0:S], v_mla[:, 0, hv], probs_t[:, h % 2, 0:S], start=True, stop=False)
                mm(ps[:, 6, P:S], v_mla[:, 1, hv], probs_t[:, h % 2, S:3 * P], start=False, stop=True)\
                    .then_inc(ctx_ready, 1)

            def mla_at(step):
                h, odd = step // 2, step % 2
                if not odd:
                    if h < H:
                        scores(h)
                    if 0 <= h - 2 < H:
                        context(h - 2)
                elif 0 <= h - 1 < H:
                    transpose_probs(h - 1)

            def gate_preact(n):
                if n == 0:
                    pe.wait_ge(ctx_lo, H)
                    pe.wait_ge(gate_w_loaded, 16)
                else:
                    pe.wait_ge(gate_pre, 4)
                for i in range(4):
                    ft = 4 * n + i
                    ins = mm(ps[:, 6 + i // 2, (i % 2) * S:(i % 2 + 1) * S], w_gate[0:GR, ft * P:(ft + 1) * P],
                             lr_t[0:GR, :], start=True, stop=True)
                ins.then_inc(gate_psum, 1)

            def level(lv):
                pe.wait_ge(qk_ready, lv) if lv else pe.wait_ge(gate_pre, 8)
                if lv:
                    pe.wait_ge(level_taken, lv)
                else:
                    pe.wait_ge(tile_empty, FIRST_OF["gv"][1])
                for t in range(NT if lv < LEVELS - 1 else 1):
                    for hd in range(GH):
                        o = ps[:, 6 + t, hd * P:(hd + 1) * P]
                        for i in range(2):
                            d = 2 * hd + i
                            tok = slice(t * P, (t + 1) * P)
                            qtok = tok if lv < LEVELS - 1 else slice(P, 2 * P)
                            lhs, rhs = (k_gla, q_gla) if lv == 0 else (qk, qk)
                            ins = mm(o, lhs[:, d, tok], rhs[:, d, qtok], start=i == 0, stop=i == 1)
                ins.then_inc(level_ready, 1)

            def gla_out(pr):
                if pr < 2:
                    pe.wait_ge(level_taken, LEVELS)
                    pe.wait_ge(tile_empty, FIRST_OF["og"][1])
                else:
                    pe.wait_ge(og_copied, pr - 1)
                for i in range(2):
                    ft = 2 * pr + i
                    hd = ft // 4
                    fv = slice(ft * P, (ft + 1) * P)
                    o = ps[:, 6 + pr % 2, i * S:(i + 1) * S]
                    mm(o, v_gla[:, 0, fv], attn0[:, hd, :], start=True, stop=False)
                    ins = mm(ps[:, 6 + pr % 2, i * S + P:(i + 1) * S], v_gla[:, 1, fv], attn1[:, hd, :], start=False,
                             stop=True)
                ins.then_inc(og_psum, 1)

            def gla_norm_sum(hd):
                pe.wait_ge(og_squared, hd + 1)
                for i in range(4):
                    ins = mm(ps[:, 4 + hd // 2, (hd % 2) * S:(hd % 2 + 1) * S], ones[:], o_sq[:, i, :],
                             start=i == 0, stop=i == 3)
                ins.then_inc(og_summed, 1)

            rope_rotate()
            s0 = FIRST_OF["gk"][0] % RING
            step = 0
            for g in range(2):
                u0, t0, _, _ = FIRST_OF["gk"]
                for j in range(0, 8, 2):
                    feature_pair(u0 + 8 * g + j, t0 + 4 * g, 2 * j, 4, j == 6, ht, (s0 + j) % RING, j == 0)
                    mla_at(step)
                    step += 1
            u0, t0, _, _ = FIRST_OF["gv"]
            for g in range(4):
                for j in range(0, 8, 2):
                    first, last = j == 0, j == 6
                    pe.wait_ge(lo_done, u0 + 8 * g + j + 2)
                    for t in range(NT):
                        if first:
                            tile_free(t0 + 2 * g + t)
                        o = ps[:, (2 * g + t) % 4, :]
                        for i in range(2):
                            s = (s0 + j + i) % RING
                            for k in range(2):
                                kt = 2 * (j + i) + k
                                tok = slice(t * P, (t + 1) * P)
                                mm(o, ht[:, kt, 0, tok], w_hi[:, s, k, :], start=first and i == 0 and k == 0, stop=False)
                                mm(o, ht[:, kt, 0, tok], w_lo[:, s, k, :], start=False, stop=False)
                                ins = mm(o, ht[:, kt, 1, tok], w_hi[:, s, k, :], start=False,
                                         stop=last and i == 1 and k == 1)
                        if last:
                            ins.then_inc(tile_ready, 1)
                    if not last:
                        ins.then_inc(pairs_used, 1)
                    mla_at(step)
                    if step in (19, 20):
                        gate_preact(step - 19)
                    if step == 22:
                        level(0)
                    if g == 1 and last:
                        pe.wait_ge(max_ready, H)
                        mod_columns(2, 3 * ADA_BLOCK)
                    step += 1
            u0, t0, _, _ = FIRST_OF["og"]
            for g in range(4):
                for j in range(0, 8, 2):
                    feature_pair(u0 + 8 * g + j, t0 + 4 * g, 2 * j, 4, j == 6, ht, (s0 + j) % RING, j == 0)
                    if step % 2 == 1 and 1 <= (step - 23) // 2 <= LEVELS - 1:
                        level((step - 23) // 2)
                    step += 1
            pe.wait_ge(mod_ready, 3)
            for hd in range(GH + 1):
                if hd < GH:
                    gla_out(2 * hd)
                    gla_out(2 * hd + 1)
                if hd:
                    gla_norm_sum(hd - 1)
            u0, t0, _, _ = FIRST_OF["ga"]
            with pe.Fori(0, 2) as g:
                feature_group(u0 + 8 * g, t0 + 4 * g, 8, ht, s0)
            pe.wait_ge(og_rms, 1)
            mod_columns(3, 4 * ADA_BLOCK)
            with pe.Fori(2, 8) as g:
                feature_group(u0 + 8 * g, t0 + 4 * g, 8, ht, s0)
            pe.wait_ge(ctx_lo, H)
            u0, t0, _, _ = FIRST_OF["ba"]
            with pe.Fori(0, 4) as g:
                feature_group(u0 + 4 * g, t0 + 4 * g, 4, ot, s0)

            def gate_rows(used, brow):
                pe.wait_ge(ada_used, used)
                for b in range(4):
                    cols = slice(b * UC, (b + 1) * UC)
                    mm(ps[:, 4 + b, :], ones[:], acc[:, cols], start=True, stop=False)
                    row = slice(32 * b, 32 * b + 1)
                    ins = mm(ps[:, 4 + b, :], ones[row, :], brow[row, :], start=False, stop=True)
                ins.then_inc(gate_row, 1)

            pe.wait_ge(mod_ready, 4)
            pe.wait_ge(og_copied, 8)
            pe.wait_ge(post_loaded, 16 * 5)
            gate_rows(5 * ADA_BLOCK, brow_m)
            u0, t0, _, _ = FIRST_OF["bb"]
            pe.wait_ge(og_lo, 4)
            with pe.Fori(0, 4) as g:
                feature_group(u0 + 8 * g, t0 + 4 * g, 8, og_s, s0)
            u0, t0, _, _ = FIRST_OF["mix"]
            pe.wait_ge(merged_lo, 4)
            with pe.Fori(0, 2) as g:
                for n in range(2):
                    token_group(u0 + 16 * g + 8 * n, t0 + 4 * g + 2 * n, 8, merged, s0, 2 * n)
            pe.wait_ge(tile_empty, FIRST_OF["ffn"][1])
            pe.wait_ge(gg_ready, 1)
            pe.wait_ge(norm_1, 2)
            for b in range(8):
                for q in range(4):
                    kt, t = 2 * b + q // 2, q % 2
                    ins = nc.tensor.transpose(ps[:, b, q * P:(q + 1) * P], xn1[:, t, kt * P:(kt + 1) * P], ident[:])
                ins.then_inc(x1t_psum, 1)
            u0, t0, _, _ = FIRST_OF["ffn"]
            pe.wait_ge(h2_lo, 4)
            with pe.Fori(0, 11) as g:
                for part in range(2):
                    feature_group(u0 + 16 * g + 8 * part, t0 + 8 * g + 4 * part, 8, h2t, s0)
            pe.wait_ge(bias_f_loaded, 16 * 4)
            gate_rows(6 * ADA_BLOCK, brow_f)
            u0, t0, _, _ = FIRST_OF["down"]
            pe.wait_ge(hid_lo, FF // P + 1)
            with pe.Fori(0, 2) as g:
                for n in range(2):
                    token_group(u0 + 44 * g + 22 * n, t0 + 4 * g + 2 * n, 22, hid, (s0 + 22 * n) % RING, 2 * n)

        @block.scalar
        def _(act):
            A = nc.scalar.activation
            own = Steps(act, act_step)

            def split(u, slot, loaded, free_sem, free_at):
                act.wait_ge(raw_loaded[slot], loaded)
                if free_sem is not None:
                    act.wait_ge(free_sem, free_at)
                A(w_hi[:, slot], raw[:, slot], ACT.Copy).then_inc(hi_done, 1)

            def loads(u):
                u_q, u_k = FIRST_OF["qup"][0], FIRST_OF["gk"][0]
                return 3 if u < 8 else 2 if u_q <= u < u_k else 1

            total = [0] * (UNITS + 1)
            for u in range(UNITS):
                total[u] = loads(u) * 16 + (total[u - RING] if u >= RING else 0)

            def split_at(u0, j, t0, p0, g=None, nu=8, t_step=0):
                u = u0 + 2 + j
                if u >= UNITS:
                    return
                loaded = total[u] if g is None else total[u] + g * (16 * nu // RING)
                if j < 2:
                    free = (None, 0) if isinstance(t0, int) and t0 == 0 else (tile_ready, t0)
                else:
                    free = (pairs_used, p0 + (j - 2) // 2 + 1)
                split(u, u % RING, loaded, *free)

            def half_tile(t, bank, scale=1.0):
                act.wait_ge(tile_ready, t + 1)
                if not isinstance(t, int) or t >= 2:
                    act.wait_ge(tile_empty, t - 1)
                A(cross[:, bank % 2], ps[:, bank, S:2 * S], ACT.Copy, scale=scale).then_inc(tile_half, 1)

            act.wait_ge(x_loaded, 16)
            for t in range(NT):
                A(junk[:], x_tok[:, t], ACT.Square, accum_out=stat[:, t:t + 1]).then_inc(ssq_x, 1)
                act.wait_ge(ssq_x, t + 1)
            act.wait_ge(setup_done, 2)
            A(stat[:, 2:4], stat[:, 0:2], ACT.Sqrt, bias=eps_t[:], scale=1.0 / D).then_inc(rms_x, 1)
            act.wait_ge(rows_t, 1)
            own.mark(A(vec[:, 0:2 * P - 6], ps[:, 4, 0:2 * P - 6], ACT.Copy))
            A(vec[:, V_CW:UC], ps[:, 4, V_CW:UC], ACT.Copy)
            A(vec[:, UC:V_END], ps[:, 5, 0:V_END - UC], ACT.Copy).then_inc(vec_ready, 1)
            own.wait()
            A(c_act[:], vec[:, V_C:V_C + KT], ACT.Silu).then_inc(c_ready, 1)
            act.wait_ge(angle_ready, 1)
            A(cos_t[:], red[:, 0], ACT.Sin).then_inc(table_ready, 1)
            A(sin_t[:], red[:, 1], ACT.Sin).then_inc(table_ready, 1)
            for b in range(8):
                act.wait_ge(xt_psum, b + 1)
                A(xn_t[:, 2 * b:2 * b + 2, :], ps[:, b, :].rearrange("p (k t) -> p k t", k=2), ACT.Copy)\
                    .then_inc(xt_copied, 1)
            split(0, 0, total[0], None, 0)
            split(1, 1, total[1], None, 0)
            for q in range(4):
                act.wait_ge(h_ready, q + 1)
                A(ht[:, 4 * q:4 * q + 4, 0], h_f[:, 4 * q:4 * q + 4], ACT.Copy).then_inc(h_hi, 1)
            for name in ("misc", "qlat"):
                u0, t0, p0, _ = FIRST_OF[name]
                for j in range(8):
                    split_at(u0, j, t0, p0)
                for f in range(4):
                    half_tile(t0 + f, f)
            act.wait_ge(tile_empty, 8)
            A(lat_sq[:], lat[:], ACT.Square).then_inc(lat_squared, 1)
            u0, t0, p0, _ = FIRST_OF["gq"]
            for g in range(2):
                for j in range(8):
                    split_at(u0 + 8 * g, j, t0 + 4 * g, p0 + 3 * g)
                    if g == 1 and j == 0:
                        act.wait_ge(lat_summed, 1)
                        A(lat_r[:, 0], ps[:, 4, 0:S], ACT.Sqrt, bias=eps_t[:], scale=1.0 / KVR)
                        A(lat_r[:, 1], ps[:, 4, S:2 * S], ACT.Sqrt, bias=eps_t[:], scale=1.0 / QR)\
                            .then_inc(lat_rms, 1)
                    if g == 1 and j == 6:
                        act.wait_ge(lat_normed, 1)
                        A(lat_s[:, :, 0], lat[:], ACT.Copy).then_inc(lat_hi, 1)
                for f in range(4):
                    half_tile(t0 + 4 * g + f, f, GLA_SCALE)
            u0, t0, p0, _ = FIRST_OF["qup"]
            for g in range(3):
                for j in range(2):
                    split_at(u0 + 2 * g, j, t0 + 4 * g, p0)
                for f in range(4):
                    half_tile(t0 + 4 * g + f, f)
            u0, t0, p0, _ = FIRST_OF["kup"]
            for j in range(2):
                split_at(u0, j, t0, p0)
            for f in range(8):
                half_tile(t0 + f, f % 4)
            u0, t0, p0, _ = FIRST_OF["vup"]
            for j in range(2):
                split_at(u0, j, t0, p0)
            for n in range(4):
                half, t = n // 2, n % 2
                act.wait_ge(tile_ready, t0 + n + 1)
                A(v_mla[:, t, half * UC + S:(half + 1) * UC], ps[:, n, S:UC], ACT.Copy).then_inc(tile_half, 1)

            def exps(h):
                act.wait_ge(max_ready, h + 1)
                k = h % 3
                for t in range(NT):
                    part = probs[:, k, t * P:t * P + (t + 1) * P]
                    ins = A(part, part, ACT.Exp, bias=soft[:, k, t:t + 1], scale=MLA_SCALE,
                            accum_out=soft[:, k, 2 + t:3 + t])
                    ins.then_inc(exp_done, 1)

            def copy_probs(h):
                act.wait_ge(pt_ready, h + 1)
                if h >= 2:
                    act.wait_ge(ctx_ready, h - 1)
                A(probs_t[:, h % 2], ps[:, 5, 0:3 * P], ACT.Copy).then_inc(pt_copied, 1)

            def context_hi(h):
                act.wait_ge(ctx_ready, h + 1)
                A(ot[:, h, 0], ps[:, 6, 0:S], ACT.Copy).then_inc(ctx_hi, 1)

            def mla_at(step):
                h, odd = step // 2, step % 2
                if odd:
                    if h < H:
                        exps(h)
                    if 0 <= h - 2 < H:
                        context_hi(h - 2)
                elif 0 <= h - 2 < H:
                    copy_probs(h - 2)

            def log_gate():
                act.wait_ge(gate_pre, 8)
                own.mark(A(dec[:], suf[:], ACT.Abs))
                own.wait()
                own.mark(A(dec[:], dec[:], ACT.Exp, scale=-1.0))
                own.wait()
                A(dec[:], dec[:], ACT.Ln, bias=ones[:, 0:1]).then_inc(gate_soft, 1)

            def decays(lv):
                h = 1 << (lv - 1)
                if lv > 1:
                    act.wait_ge(scan_ready, lv - 1)
                else:
                    act.wait_ge(decay_ready, 1)
                d0, d1 = halves(dec, h)
                A(d1, halves(pre, h)[1], ACT.Exp)
                A(d0, halves(suf, h)[0], ACT.Exp).then_inc(dec_ready, 1)

            s0 = FIRST_OF["gk"][0] % RING
            step = 0
            for g in range(2):
                u0, t0, p0, _ = FIRST_OF["gk"]
                for j in range(8):
                    split_at(u0 + 8 * g, j, t0 + 4 * g, p0 + 3 * g)
                    if j % 2 == 1:
                        mla_at(step)
                        step += 1
                for f in range(4):
                    half_tile(t0 + 4 * g + f, f)
            for g in range(4):
                u0, t0, p0, _ = FIRST_OF["gv"]
                for j in range(8):
                    split_at(u0 + 8 * g, j, t0 + 2 * g, p0 + 3 * g)
                    if j % 2 == 1:
                        mla_at(step)
                        if step == 21:
                            log_gate()
                        if step == 23:
                            decays(1)
                        step += 1
                for t in range(NT):
                    n = t0 + 2 * g + t
                    act.wait_ge(tile_ready, n + 1)
                    A(v_gla[:, t, g * UC + S:(g + 1) * UC], ps[:, n % 4, S:UC], ACT.Copy).then_inc(tile_half, 1)
            for g in range(4):
                u0, t0, p0, _ = FIRST_OF["og"]
                for j in range(8):
                    split_at(u0 + 8 * g, j, t0 + 4 * g, p0 + 3 * g)
                    if j % 2 == 1:
                        if step % 2 == 1 and 2 <= (step - 21) // 2 <= LEVELS - 1:
                            decays((step - 21) // 2)
                        step += 1
                for f in range(4):
                    half_tile(t0 + 4 * g + f, f)
            for pr in range(8):
                act.wait_ge(og_psum, pr + 1)
                A(o_gla[:, 2 * pr:2 * pr + 2, :], ps[:, 6 + pr % 2, :].rearrange("p (k t) -> p k t", k=2), ACT.Copy)\
                    .then_inc(og_copied, 1)
                if pr % 2 == 1:
                    hd = pr // 2
                    act.wait_ge(og_copied, pr + 1)
                    if hd:
                        act.wait_ge(og_summed, hd)
                    A(o_sq[:], o_gla[:, 4 * hd:4 * hd + 4], ACT.Square).then_inc(og_squared, 1)
            act.wait_ge(og_summed, GH)
            A(o_r[:].rearrange("p (b h) t -> p b (h t)", b=2), ps[:, 4:6, :], ACT.Sqrt, bias=eps_t[:], scale=1.0 / DV)\
                .then_inc(og_rms, 1)
            act.wait_ge(tile_empty, FIRST_OF["ga"][1])
            A(og[:], og[:], ACT.Silu).then_inc(og_silu, 1)
            u0, t0, p0, _ = FIRST_OF["ga"]
            nc.scalar.preload_act_table(ACT.Sigmoid)
            for first, gate in ((0, gate_a), (4, gate_b)):
                with act.Fori(first, first + 4) as g:
                    for j in range(8):
                        split_at(u0, j, t0 + 4 * g, p0 + 3 * g, g)
                    for f in range(4):
                        half_tile(t0 + 4 * g + f, f)
                    act.wait_ge(tile_empty, t0 + 4 * g + 4)
                    tiles = gate[:, bass.ds(4 * g - 4 * first, 4)]
                    A(tiles, tiles, ACT.Sigmoid).then_inc(sig_done, 1)
            act.wait_ge(og_gated, 4)
            act.wait_ge(tile_ready, FIRST_OF["ba"][1])
            for q in range(4):
                A(og_s[:, 4 * q:4 * q + 4, 0], o_gla[:, 4 * q:4 * q + 4], ACT.Copy).then_inc(og_hi, 1)
            u0, t0, p0, _ = FIRST_OF["ba"]
            with act.Fori(0, 2) as g:
                for n in range(2):
                    for j in range(4):
                        split_at(u0 + 4 * n, j, t0 + 8 * g + 4 * n, p0 + 2 * g + n, g)
                    for f in range(4):
                        half_tile(t0 + 8 * g + 4 * n + f, f)
            u0, t0, p0, _ = FIRST_OF["bb"]
            with act.Fori(0, 4) as g:
                for j in range(8):
                    split_at(u0, j, t0 + 4 * g, p0 + 3 * g, g)
                for f in range(4):
                    half_tile(t0 + 4 * g + f, f)
                act.wait_ge(merged_ready, g + 1)
                A(merged[:, bass.ds(4 * g, 4), 0], gate_b[:, bass.ds(4 * g, 4)], ACT.Copy).then_inc(merged_hi, 1)
            nc.scalar.preload_act_table(ACT.Sqrt)
            u0, t0, p0, _ = FIRST_OF["mix"]
            act.wait_ge(tile_empty, t0)
            act.wait_ge(merged_lo, 4)
            with act.Fori(0, 2) as g:
                for n in range(2):
                    for j in range(8):
                        split_at(u0 + 8 * n, j, t0 + 4 * g + 2 * n, p0 + 6 * g + 3 * n, g, nu=16)
                    for t in range(NT):
                        bank = 2 * n + t
                        act.wait_ge(tile_ready, t0 + 4 * g + bank + 1)
                        act.wait_ge(tile_half, t0 + 4 * g + bank)
                        A(junk_m[:, 0:UC], ps[:, bank, :], ACT.Square,
                          accum_out=stat[:, bass.ds(8 + 4 * t + 2 * g + n, 1)]).then_inc(tile_half, 1)
            act.wait_ge(sum_f, 1)
            A(stat[:, 18:20], stat[:, 16:18], ACT.Sqrt, bias=eps_t[:], scale=1.0 / D).then_inc(rms_y, 1)
            for t in range(NT):
                act.wait_ge(x1_ready, t + 1)
                if t:
                    act.wait_ge(ssq_1, t)
                A(junk_m[:], x1[:, t], ACT.Square, accum_out=stat[:, 4 + t:5 + t]).then_inc(ssq_1, 1)
            act.wait_ge(ssq_1, 2)
            A(stat[:, 6:8], stat[:, 4:6], ACT.Sqrt, bias=eps_t[:], scale=1.0 / D).then_inc(rms_1, 1)
            nc.scalar.preload_act_table(ACT.Gelu_apprx_tanh)
            for b in range(0, 8, 2):
                act.wait_ge(x1t_psum, b + 1)
                for k in range(2):
                    kt = 2 * b + k
                    ins = A(h2_f[:, kt], ps[:, b, k * S:(k + 1) * S], ACT.Identity, bias=mod[:, 3, kt:kt + 1],
                            scale=mod[:, 4, kt:kt + 1])
                own.mark(ins)
                act.wait_ge(h2_ready, b // 2 + 1)
                own.wait()
                A(h2t[:, 2 * b:2 * b + 4, 0], h2_f[:, 2 * b:2 * b + 4], ACT.Copy).then_inc(h2_hi, 1)
            u0, t0, p0, _ = FIRST_OF["ffn"]
            with act.Fori(0, 11) as g:
                for part in range(2):
                    for j in range(8):
                        split_at(u0 + 8 * part, j, t0 + 8 * g + 4 * part, p0 + 6 * g + 3 * part, g, nu=16)
                    for f in range(6):
                        if f < 4:
                            half_tile(t0 + 8 * g + 4 * part + f, f)
                        if 0 <= f - 1 < 4:
                            n = f - 1
                            ft = part * (FF // P) + 4 * g + n
                            act.wait_ge(tile_empty, t0 + 8 * g + 4 * part + n + 1)
                            dst = conv_a[:, n] if part == 0 else conv_v[:, n % 2]
                            if part == 0 and n == 0:
                                act.wait_ge(hid_ready, 4 * g + 1)
                            if part == 1 and n >= 2:
                                act.wait_ge(hid_ready, 4 * g + n)
                            A(dst, conv_in[:, n, 2:S + 2], ACT.Identity,
                              bias=vec[:, bass.ds(V_CB + ft, 1)], scale=vec[:, bass.ds(V_CW + 2 * (2 * FF // P) + ft, 1)])\
                                .then_inc(conv_first, 1)
                        if 0 <= f - 2 < 4:
                            n = f - 2
                            if part == 0:
                                act.wait_ge(conv_done, 8 * g + n + 2)
                                A(conv_a[:, n], conv_a[:, n], ACT.Gelu_apprx_tanh).then_inc(gelu_done, 1)
                            else:
                                act.wait_ge(hid_ready, 4 * g + n + 2)
                                A(hid[:, bass.ds(4 * g + n, 1), 0].rearrange("p o t -> p (o t)"), hid_f[:, n % 2],
                                  ACT.Copy).then_inc(hid_hi, 1)
            nc.scalar.preload_act_table(ACT.Sqrt)
            u0, t0, p0, _ = FIRST_OF["down"]
            for g in range(2):
                for n in range(2):
                    for j in range(22):
                        split_at(u0 + 44 * g + 22 * n, j, t0 + 4 * g + 2 * n, p0 + 20 * g + 10 * n)
                    for t in range(NT):
                        bank = 2 * n + t
                        act.wait_ge(tile_ready, t0 + 4 * g + bank + 1)
                        act.wait_ge(tile_half, t0 + 4 * g + bank)
                        A(junk_f[:], ps[:, bank, :], ACT.Square,
                          accum_out=stat[:, 8 + 4 * t + 2 * g + n:9 + 4 * t + 2 * g + n]).then_inc(tile_half, 1)
            act.wait_ge(sum_f, 2)
            A(stat[:, 22:24], stat[:, 20:22], ACT.Sqrt, bias=eps_t[:], scale=1.0 / D).then_inc(rms_f, 1)

        @block.vector
        def _(dve):
            V = nc.vector
            own = Steps(dve, dve_step)

            def chain(ins):
                own.mark(ins)
                own.wait()

            def split(u, slot):
                dve.wait_ge(hi_done, u + 1)
                V.tensor_tensor(w_lo[:, slot], raw[:, slot], w_hi[:, slot].bitcast(F32), ALU.subtract)\
                    .then_inc(lo_done, 1)

            def clear_acc(n):
                if 1 <= n <= 4:
                    dve.wait_ge(mod_psum, n)
                if n == 5:
                    dve.wait_ge(gate_row, 1)
                V.memset(acc[:], 0.0).then_inc(acc_zero, 1)
                dve.wait_ge(acc_zero, n + 1)

            def ada_unit(a, slot, kt, half, loaded, guard=True):
                dve.wait_ge(ada_loaded[slot], loaded)
                if guard:
                    dve.wait_ge(ada_used, a - 1)
                part = acc[:, half * AC:(half + 1) * AC]
                V.scalar_tensor_tensor(part, ada[:, slot], c_act[:, bass.ds(kt, 1)], part, ALU.mult, ALU.add)\
                    .then_inc(ada_used, 1)

            def split_pairs(u0, nu, a=None, kt=None, g=None, per=8, extra=None):
                for j in range(nu):
                    u = u0 + 2 + j
                    if u < UNITS:
                        split(u if g is None else u + per * g, u % RING)
                    if j % 2 == 1:
                        if a is not None:
                            n = j // 2
                            av = a + n if g is None else a + n + (per // 2) * g
                            loaded = 16 * ((a + n) // RING + 1)
                            if g is not None:
                                loaded = loaded + 16 * (per // 2 // RING) * g
                            ada_unit(av, (a + n) % RING, kt + n // 2, n % 2, loaded)
                        if extra is not None:
                            extra()

            def sum_tile(t, bank, dst, scale=None):
                dve.wait_ge(tile_half, t + 1)
                if scale is None:
                    ins = V.tensor_tensor(dst, ps[:, bank, 0:S], cross[:, bank % 2], ALU.add)
                else:
                    ins = V.scalar_tensor_tensor(dst, ps[:, bank, 0:S], scale, cross[:, bank % 2], ALU.mult, ALU.add)
                ins.then_inc(tile_empty, 1)

            dve.wait_ge(const_loaded, 3 * 16)
            chain(V.tensor_copy(pos_f[:], pos_i[:]))
            chain(V.tensor_scalar(ang[:], pos_f[:], inv_freq[:, 0:1], None, ALU.mult))
            round_c = 12582912.0
            V.tensor_scalar(turn[:, 0], ang[:], float(0.5 / np.pi), 0.25, ALU.mult, ALU.add)
            chain(V.tensor_scalar(turn[:, 1], ang[:], float(0.5 / np.pi), None, ALU.mult))
            chain(V.tensor_scalar(turn[:], turn[:], round_c, None, ALU.add))
            chain(V.tensor_scalar(turn[:], turn[:], -round_c, None, ALU.add))
            for n in range(2):
                own.mark(V.scalar_tensor_tensor(red[:, n], turn[:, n], -6.28125, ang[:], ALU.mult, ALU.add))
            own.wait()
            for part in (-0.0019350051879882812, -3.019916050561733e-07):
                chain(V.scalar_tensor_tensor(red[:], turn[:], part, red[:], ALU.mult, ALU.add))
            chain(V.tensor_scalar(red[:, 0], red[:, 0], float(np.pi / 2), None, ALU.add))
            V.tensor_scalar(red[:], red[:], 3.1415925, -3.1415925, ALU.min, ALU.max).then_inc(angle_ready, 1)

            V.tensor_copy(masks[:], masks_i[:])

            dve.wait_ge(rms_x, 1)
            chain(V.reciprocal(stat[:, 2:4], stat[:, 2:4]))
            for t in range(NT):
                V.tensor_scalar(xn_tok[:, t], x_tok[:, t], stat[:, 2 + t:3 + t], None, ALU.mult).then_inc(norm_x, 1)

            dve.wait_ge(c_ready, 1)

            def take_mod(n, dst, base):
                dve.wait_ge(mod_psum, n + 1)
                return V.tensor_tensor(mod[:, dst], ps[:, 4, 0:KT], vec[:, base:base + KT], ALU.add)

            def one_plus_times(dst, gain):
                return V.scalar_tensor_tensor(mod[:, dst], mod[:, dst], 1.0, vec[:, gain:gain + KT], ALU.add, ALU.mult)

            for n in range(2):
                clear_acc(n)
                if n == 1:
                    take_mod(0, 0, V_BADA).then_inc(mod_ready, 1)
                a0 = ADA_BLOCK * n
                for r in range(RING):
                    ada_unit(a0 + r, r, r // 2, r % 2, 16 * (a0 // RING + 1), guard=r >= 2)
                with dve.Fori(1, KT // 2) as i:
                    for r in range(RING):
                        ada_unit(a0 + 4 * i + r, r, 2 * i + r // 2, r % 2, 16 * (a0 // RING) + 16 * i + 16)
            split(0, 0)
            split(1, 1)
            chain(take_mod(1, 1, V_BADA + KT))
            one_plus_times(1, V_GPRE).then_inc(mod_ready, 1)
            dve.wait_ge(mod_ready, 2)
            dve.wait_ge(xt_copied, 8)
            for q in range(4):
                for i in range(4):
                    kt = 4 * q + i
                    ins = V.tensor_scalar(h_f[:, kt], xn_t[:, kt], mod[:, 1, kt:kt + 1], mod[:, 0, kt:kt + 1],
                                          ALU.mult, ALU.add)
                ins.then_inc(h_ready, 1)
            for q in range(4):
                dve.wait_ge(h_hi, q + 1)
                ks = slice(4 * q, 4 * q + 4)
                V.tensor_tensor(ht[:, ks, 1], h_f[:, ks], ht[:, ks, 0].bitcast(F32), ALU.subtract).then_inc(h_lo, 1)
            clear_acc(2)
            for name, kt in (("misc", 0), ("qlat", 2)):
                u0, t0, _, a0 = FIRST_OF[name]
                split_pairs(u0, 8, a0, kt)
                dsts = ([lat[:, 0], lat[:, 1], k_rope_in[:], lr_t[:]] if name == "misc"
                        else [lat[:, 2 + f] for f in range(4)])
                for f in range(4):
                    sum_tile(t0 + f, f, dsts[f])

            def latents_at(step):
                if step == 0:
                    dve.wait_ge(lat_rms, 1)
                    chain(V.reciprocal(lat_r[:], lat_r[:]))
                if step == 1:
                    for i in range(6):
                        gain = V_GKV + i if i < 2 else V_GQ + i - 2
                        ins = V.scalar_tensor_tensor(lat[:, i], lat[:, i], vec[:, gain:gain + 1],
                                                     lat_r[:, 0 if i < 2 else 1], ALU.mult, ALU.mult)
                    ins.then_inc(lat_normed, 1)
                if step == 3:
                    dve.wait_ge(lat_hi, 1)
                    V.tensor_tensor(lat_s[:, :, 1], lat[:], lat_s[:, :, 0].bitcast(F32), ALU.subtract)\
                        .then_inc(lat_lo, 1)

            u0, t0, _, a0 = FIRST_OF["gq"]
            for g in range(2):
                for j in range(4):
                    split_pairs(u0 + 8 * g + 2 * j, 2)
                    ada_unit(a0 + 4 * g + j, j, 4 + 2 * g + j // 2, j % 2, 16 * ((a0 + 4 * g) // RING + 1))
                    if g:
                        latents_at(j)
                for f in range(4):
                    sum_tile(t0 + 4 * g + f, f, q_gla[:, 4 * g + f], GLA_SCALE)
            u0, t0, _, _ = FIRST_OF["qup"]
            for g in range(3):
                split_pairs(u0 + 2 * g, 2)
                for f in range(4):
                    sum_tile(t0 + 4 * g + f, f, q_nope[:, 4 * g + f] if g < 2 else q_rope_in[:, f])
            u0, t0, _, _ = FIRST_OF["kup"]
            split_pairs(u0, 2)
            for n in range(8):
                sum_tile(t0 + n, n % 4, k_nope[:, n])
            u0, t0, _, _ = FIRST_OF["vup"]
            split_pairs(u0, 2)
            for n in range(4):
                half, t = n // 2, n % 2
                dve.wait_ge(tile_half, t0 + n + 1)
                V.tensor_copy(v_mla[:, t, half * UC:half * UC + S], ps[:, n, 0:S]).then_inc(tile_empty, 1)
            dve.wait_ge(table_ready, 2)
            dve.wait_ge(rot_ready, 1)
            for i in range(4):
                V.tensor_tensor(rope_tmp[:, i % 2], ps[:, 4 + i // 2, (i % 2) * S:(i % 2 + 1) * S], sin_t[:], ALU.mult)
                chain(V.tensor_tensor(q_rope[:, i], q_rope_in[:, i], cos_t[:], ALU.mult))
                V.tensor_tensor(q_rope[:, i], q_rope[:, i], rope_tmp[:, i % 2], ALU.add).then_inc(rope_done, 1)
            V.tensor_tensor(rope_tmp[:, 0], ps[:, 6, 0:S], sin_t[:], ALU.mult)
            chain(V.tensor_tensor(k_rope[:], k_rope_in[:], cos_t[:], ALU.mult))
            V.tensor_tensor(k_rope[:], k_rope[:], rope_tmp[:, 0], ALU.add).then_inc(rope_done, 1)

            def mask_and_max(h):
                dve.wait_ge(scores_ready, h + 1)
                if h >= 3:
                    dve.wait_ge(pt_ready, h - 2)
                k = h % 3

                def diagonal(v):
                    return v.rearrange("p (a b) -> p a b", b=2 * P)[:, :, 0:P]

                V.tensor_copy(probs[:, k, P:2 * P], ps[:, 4, P:2 * P])
                bias = causal[:].rearrange("p (o n) -> p o n", o=1).to_broadcast([P, 2, P])
                chain(V.tensor_tensor(diagonal(probs[:, k]), diagonal(ps[:, 4]), bias, ALU.add))
                V.tensor_reduce(soft[:, k, 0:1], probs[:, k, 0:P], AX, ALU.max)
                chain(V.tensor_reduce(soft[:, k, 1:2], probs[:, k, P:3 * P], AX, ALU.max))
                V.tensor_scalar(soft[:, k, 0:2], soft[:, k, 0:2], -MLA_SCALE, None, ALU.mult).then_inc(max_ready, 1)

            def normalise(h):
                dve.wait_ge(exp_done, 2 * h + 2)
                k = h % 3
                chain(V.reciprocal(soft[:, k, 4:6], soft[:, k, 2:4]))
                V.tensor_scalar(probs[:, k, 0:P], probs[:, k, 0:P], soft[:, k, 4:5], None, ALU.mult)
                V.tensor_scalar(probs[:, k, P:3 * P], probs[:, k, P:3 * P], soft[:, k, 5:6], None, ALU.mult)\
                    .then_inc(probs_ready, 1)

            def context_lo(h):
                dve.wait_ge(ctx_hi, h + 1)
                V.tensor_tensor(ot[:, h, 1], ps[:, 6, 0:S], ot[:, h, 0].bitcast(F32), ALU.subtract).then_inc(ctx_lo, 1)

            def mla_at(step):
                h, odd = step // 2, step % 2
                if odd:
                    if h < H:
                        mask_and_max(h)
                    if 0 <= h - 2 < H:
                        context_lo(h - 2)
                elif 0 <= h - 1 < H:
                    normalise(h - 1)

            def gate_bias(n):
                dve.wait_ge(gate_psum, n + 1)
                for i in range(4):
                    ft = 4 * n + i
                    V.tensor_scalar(suf[:, ft], ps[:, 6 + i // 2, (i % 2) * S:(i % 2 + 1) * S],
                                    vec[:, V_BGLA + ft:V_BGLA + ft + 1], None, ALU.add).then_inc(gate_pre, 1)

            def log_decay():
                dve.wait_ge(gate_soft, 1)
                chain(V.scalar_tensor_tensor(pre[:], suf[:], 0.0, dec[:], ALU.min, ALU.subtract))
                V.tensor_scalar(pre[:], pre[:], 1.0 / TAU, None, ALU.mult)
                V.memset(attn0[:], 0.0)
                V.memset(attn1[:], 0.0)
                V.memset(suf[:], 0.0).then_inc(decay_ready, 1)
                dve.wait_ge(decay_ready, 1)

            def products(lv):
                h = 1 << (lv - 1)
                dve.wait_ge(dec_ready, lv)
                dve.wait_ge(level_ready, lv)
                V.tensor_tensor(halves(qk, h)[1], halves(q_gla, h)[1], halves(dec, h)[1], ALU.mult)
                V.tensor_tensor(halves(qk, h)[0], halves(k_gla, h)[0], halves(dec, h)[0], ALU.mult).then_inc(qk_ready, 1)

            def scan(lv):
                h = 1 << (lv - 1)
                p0, p1 = halves(pre, h)
                s0_, _ = halves(suf, h)
                chain(V.tensor_tensor(s0_, s0_, spread(p1[:, :, h - 1:h], s0_), ALU.add))
                V.tensor_tensor(p1, p1, spread(p0[:, :, h - 1:h], p1), ALU.add).then_inc(scan_ready, 1)
                dve.wait_ge(scan_ready, lv)

            def select(lv):
                dve.wait_ge(level_ready, lv + 1)

                def by_head(b):
                    return ps[:, b, :].rearrange("p (h n) -> p h n", h=GH)

                if lv < LEVELS - 1:
                    m = masks[:, lv:lv + 1, :].to_broadcast([P, GH, P])
                    V.copy_predicated(attn0[:, :, 0:P], m, by_head(6))
                    V.copy_predicated(attn1[:], m, by_head(7)).then_inc(level_taken, 1)
                else:
                    V.tensor_copy(attn0[:, :, P:S], by_head(6)).then_inc(level_taken, 1)
                dve.wait_ge(level_taken, lv + 1)

            step = 0
            for g in range(2):
                u0, t0, _, a0 = FIRST_OF["gk"]
                for j in range(4):
                    split_pairs(u0 + 8 * g + 2 * j, 2)
                    ada_unit(a0 + 4 * g + j, j, 8 + 2 * g + j // 2, j % 2, 16 * ((a0 + 4 * g) // RING + 1))
                    mla_at(step)
                    step += 1
                for f in range(4):
                    sum_tile(t0 + 4 * g + f, f, k_gla[:, 4 * g + f])
            for g in range(4):
                u0, t0, _, a0 = FIRST_OF["gv"]
                if g == 2:
                    clear_acc(3)
                    chain(take_mod(2, 3, V_BADA + 3 * KT))
                    V.tensor_copy(mod[:, 3], mod[:, 3]).then_inc(mod_ready, 1)
                for j in range(4):
                    split_pairs(u0 + 8 * g + 2 * j, 2)
                    kt = (12 + 2 * g if g < 2 else 2 * g - 4) + j // 2
                    ada_unit(a0 + 4 * g + j, j, kt, j % 2, 16 * ((a0 + 4 * g) // RING + 1))
                    mla_at(step)
                    if step in (20, 21):
                        gate_bias(step - 20)
                    if step == 22:
                        log_decay()
                    step += 1
                for t in range(NT):
                    n = t0 + 2 * g + t
                    dve.wait_ge(tile_half, n + 1)
                    V.tensor_copy(v_gla[:, t, g * UC:g * UC + S], ps[:, n % 4, 0:S]).then_inc(tile_empty, 1)
            for g in range(4):
                u0, t0, _, a0 = FIRST_OF["og"]
                for j in range(4):
                    split_pairs(u0 + 8 * g + 2 * j, 2)
                    ada_unit(a0 + 4 * g + j, j, 4 + 2 * g + j // 2, j % 2, 16 * ((a0 + 4 * g) // RING + 1))
                    if step % 2 == 0:
                        lv = (step - 22) // 2
                        products(lv)
                        if lv < LEVELS - 1:
                            scan(lv)
                    else:
                        select((step - 25) // 2)
                    step += 1
                for f in range(4):
                    sum_tile(t0 + 4 * g + f, f, og[:, 4 * g + f])
            select(LEVELS - 1)

            u0, t0, _, a0 = FIRST_OF["ga"]

            def gate_loop(g_from, g_to, dst, u, t, a, kt0):
                with dve.Fori(g_from, g_to) as g:
                    split_pairs(u, 8, a, 2 * g + kt0, g)
                    for f in range(4):
                        sum_tile(t + 4 * g + f, f, dst(g, f))

            def column(buf, n):
                return buf[:, bass.ds(n, 1)].rearrange("p o t -> p (o t)")

            gate_loop(0, 2, lambda g, f: column(gate_a, 4 * g + f), u0, t0, a0, 12)
            dve.wait_ge(og_rms, 1)
            chain(V.reciprocal(o_r[:], o_r[:]))
            for hd in range(GH):
                part = o_gla[:, 4 * hd:4 * hd + 4]
                own.mark(V.tensor_tensor(part, part, o_r[:, hd:hd + 1].to_broadcast([P, 4, S]), ALU.mult))
            own.wait()
            dve.wait_ge(og_silu, 1)
            for i in range(4):
                part, gate = (b[:].rearrange("p (h i) t -> p h i t", i=4)[:, :, i] for b in (o_gla, og))
                V.scalar_tensor_tensor(part, part, vec[:, V_GOUT + i:V_GOUT + i + 1], gate, ALU.mult, ALU.mult)\
                    .then_inc(og_gated, 1)
            clear_acc(4)
            chain(take_mod(3, 4, V_BADA + 4 * KT))
            one_plus_times(4, V_GFFN).then_inc(mod_ready, 1)
            gate_loop(2, 4, lambda g, f: column(gate_a, 4 * g + f), u0, t0, a0, -4)
            gate_loop(4, 8, lambda g, f: column(gate_b, 4 * g + f - 16), u0, t0, a0, -4)
            for q in range(4):
                dve.wait_ge(og_hi, q + 1)
                ks = slice(4 * q, 4 * q + 4)
                V.tensor_tensor(og_s[:, ks, 1], o_gla[:, ks], og_s[:, ks, 0].bitcast(F32), ALU.subtract)\
                    .then_inc(og_lo, 1)
            u0, t0, _, a0 = FIRST_OF["ba"]
            dve.wait_ge(sig_done, 8)
            n0 = own.n
            with dve.Fori(0, 2) as g:
                own.n = n0 + 8 * g
                for n in range(2):
                    split_pairs(u0 + 4 * n, 4, a0 + 2 * n, 12 + 2 * g + n, g)
                    for f in range(4):
                        sum_tile(t0 + 8 * g + 4 * n + f, f, ytmp[:, f % 2])
                        dve.wait_ge(tile_empty, t0 + 8 * g + 4 * n + f + 1)
                        dst = column(gate_a, 8 * g + 4 * n + f)
                        own.mark(V.tensor_tensor(dst, dst, ytmp[:, f % 2], ALU.mult))
            own.n = n0 + 16
            own.wait()

            def gate_gain(n, dst, gpost):
                dve.wait_ge(gate_row, n + 1)
                for b in range(4):
                    cols = slice(b * UC, (b + 1) * UC)
                    ins = V.tensor_tensor(dst[:, cols], ps[:, 4 + b, :], gpost[:, cols], ALU.mult)
                ins.then_inc(gg_ready, 1)

            dve.wait_ge(post_loaded, 16 * 5)
            clear_acc(5)
            gate_gain(0, gg_m, gpost_m)
            u0, t0, _, a0 = FIRST_OF["bb"]
            n0 = own.n
            with dve.Fori(0, 4) as g:
                own.n = n0 + 4 * g
                split_pairs(u0, 8, a0, 2 * g, g)
                for f in range(4):
                    sum_tile(t0 + 4 * g + f, f, ytmp[:, f % 2])
                    dve.wait_ge(tile_empty, t0 + 4 * g + f + 1)
                    y, gb = ytmp[:, f % 2], column(gate_b, 4 * g + f)
                    chain(V.tensor_tensor(y, y, gb, ALU.mult))
                    ins = V.tensor_tensor(gb, y, column(gate_a, 4 * g + f), ALU.add)
                ins.then_inc(merged_ready, 1)
                dve.wait_ge(merged_hi, g + 1)
                ks = bass.ds(4 * g, 4)
                V.tensor_tensor(merged[:, ks, 1], gate_b[:, ks], merged[:, ks, 0].bitcast(F32), ALU.subtract)\
                    .then_inc(merged_lo, 1)
            own.n = n0 + 16
            u0, t0, _, a0 = FIRST_OF["mix"]
            with dve.Fori(0, 2) as g:
                for n in range(2):
                    split_pairs(u0 + 8 * n, 8, a0 + 4 * n, 8 + 4 * g + 2 * n, g, per=16)
                    for t in range(NT):
                        bank = 2 * n + t
                        dve.wait_ge(tile_half, t0 + 4 * g + bank + 1)
                        cols = bass.ds(2 * UC * g + UC * n, UC)
                        V.tensor_tensor(x1[:, t, cols], ps[:, bank, :], gg_m[:, cols], ALU.mult).then_inc(tile_empty, 1)
            V.tensor_reduce(stat[:, 16:18], stat[:, 8:16].rearrange("p (t n) -> p t n", t=2), AX, ALU.add)\
                .then_inc(sum_f, 1)
            dve.wait_ge(rms_y, 1)
            chain(V.reciprocal(stat[:, 18:20], stat[:, 18:20]))
            dve.wait_ge(x_again_loaded, 16)
            dve.wait_ge(tile_empty, FIRST_OF["ffn"][1])
            for t in range(NT):
                V.scalar_tensor_tensor(x1[:, t], x1[:, t], stat[:, 18 + t:19 + t], x_again[:, t], ALU.mult, ALU.add)\
                    .then_inc(x1_ready, 1)
            dve.wait_ge(x1_ready, 2)
            dve.wait_ge(rms_1, 1)
            chain(V.reciprocal(stat[:, 6:8], stat[:, 6:8]))
            for t in range(NT):
                V.tensor_scalar(xn1[:, t], x1[:, t], stat[:, 6 + t:7 + t], None, ALU.mult).then_inc(norm_1, 1)
            for b in range(1, 8, 2):
                dve.wait_ge(x1t_psum, b + 1)
                for k in range(2):
                    kt = 2 * b + k
                    ins = V.tensor_scalar(h2_f[:, kt], ps[:, b, k * S:(k + 1) * S], mod[:, 4, kt:kt + 1],
                                          mod[:, 3, kt:kt + 1], ALU.mult, ALU.add)
                ins.then_inc(h2_ready, 1)
            for q in range(4):
                dve.wait_ge(h2_hi, q + 1)
                ks = slice(4 * q, 4 * q + 4)
                V.tensor_tensor(h2t[:, ks, 1], h2_f[:, ks], h2t[:, ks, 0].bitcast(F32), ALU.subtract).then_inc(h2_lo, 1)
            dve.wait_ge(ada_used, 6 * ADA_BLOCK)
            chain(V.memset(conv_in[:, :, 0:2], 0.0))
            for n, s in enumerate((conv_done, hid_ready, hid_lo)):
                V.memset(hid_f[:, 0, n:n + 1], 0.0).then_inc(s, 1)
            dve.wait_ge(hid_lo, 1)
            u0, t0, _, _ = FIRST_OF["ffn"]
            n0 = own.n
            with dve.Fori(0, FF // UC) as g:
                own.n = n0 + 8 * g
                for part in range(2):
                    split_pairs(u0 + 8 * part, 8, g=g, per=16)
                    for f in range(7 if part else 5):
                        if f < 4:
                            if part or f == 0:
                                dve.wait_ge(conv_done, 8 * g + (f + 2 if part else 1))
                            sum_tile(t0 + 8 * g + 4 * part + f, f, conv_in[:, f, 2:S + 2])
                        if 0 <= f - 1 < 4:
                            n = f - 1
                            ft = part * (FF // P) + 4 * g + n
                            dve.wait_ge(conv_first, 8 * g + 4 * part + n + 1)
                            dst = conv_a[:, n] if part == 0 else conv_v[:, n % 2]
                            chain(V.scalar_tensor_tensor(dst, conv_in[:, n, 1:S + 1],
                                                         vec[:, bass.ds(V_CW + 2 * FF // P + ft, 1)], dst,
                                                         ALU.mult, ALU.add))
                            V.scalar_tensor_tensor(dst, conv_in[:, n, 0:S], vec[:, bass.ds(V_CW + ft, 1)], dst,
                                                   ALU.mult, ALU.add).then_inc(conv_done, 1)
                        if part and 0 <= f - 2 < 4:
                            n = f - 2
                            dve.wait_ge(gelu_done, 4 * g + n + 1)
                            dve.wait_ge(hid_lo, 4 * g + max(n, 1))
                            dve.wait_ge(conv_done, 8 * g + 4 + n + 2)
                            V.tensor_tensor(hid_f[:, n % 2], conv_a[:, n], conv_v[:, n % 2], ALU.mult)\
                                .then_inc(hid_ready, 1)
                        if part and 0 <= f - 3 < 4:
                            n = f - 3
                            dve.wait_ge(hid_hi, 4 * g + n + 1)
                            V.tensor_tensor(column(hid[:, :, 1], 4 * g + n), hid_f[:, n % 2],
                                            column(hid[:, :, 0], 4 * g + n).bitcast(F32), ALU.subtract)\
                                .then_inc(hid_lo, 1)
            own.n = n0 + 8 * (FF // UC)
            u0, t0, _, _ = FIRST_OF["down"]
            for g in range(2):
                for n in range(2):
                    split_pairs(u0 + 44 * g + 22 * n, 2)
                    if g == 0 and n == 0:
                        dve.wait_ge(post_f_loaded, 16)
                        gate_gain(1, gg_f, gpost_f)
                    split_pairs(u0 + 44 * g + 22 * n + 2, 20)
                    for t in range(NT):
                        bank = 2 * n + t
                        dve.wait_ge(tile_half, t0 + 4 * g + bank + 1)
                        cols = slice((2 * g + n) * UC, (2 * g + n + 1) * UC)
                        V.tensor_tensor(f_tok[:, t, cols], ps[:, bank, :], gg_f[:, cols], ALU.mult)\
                            .then_inc(tile_empty, 1)
            V.tensor_reduce(stat[:, 20:22], stat[:, 8:16].rearrange("p (t n) -> p t n", t=2), AX, ALU.add)\
                .then_inc(sum_f, 1)
            dve.wait_ge(rms_f, 1)
            chain(V.reciprocal(stat[:, 22:24], stat[:, 22:24]))
            dve.wait_ge(tile_empty, FIRST_OF["down"][1] + 8)
            for n in range(4):
                t, c0 = n // 2, (n % 2) * (D // 2)
                part = f_tok[:, t, c0:c0 + D // 2]
                V.scalar_tensor_tensor(part, part, stat[:, 22 + t:23 + t], x1[:, t, c0:c0 + D // 2], ALU.mult, ALU.add)\
                    .then_inc(out_ready, 1)

        @block.gpsimd
        def _(pool):
            nc.gpsimd.memset(eps_t[:], EPS).then_inc(setup_done, 1)
            nc.gpsimd.memset(ones[:], 1.0).then_inc(setup_done, 1)


def kernel(**inputs):
    import concourse.bacc as bacc
    from concourse.bass_utils import run_bass_kernel_spmd

    names = ["x", "c", "positions", "w_ada", "b_ada", "g_pre_mix", "w_in", "g_q_lat", "w_q_up", "g_kv_lat",
             "w_kv_up", "w_gla_gate_up", "b_gla_gate", "g_gla_out", "w_branch_a", "w_branch_b", "w_mix_out",
             "g_post_mix", "g_pre_ffn", "w_ffn_up", "conv_w", "conv_b", "w_ffn_down", "g_post_ffn"]
    nc = bacc.Bacc("TRN2", target_bir_lowering=False, num_devices=1, dynamic_dma_scratch_size=1024)
    arrays = {f"in_{n}": np.ascontiguousarray(inputs[n]) for n in names}
    arrays["in_constants"] = constants()
    arrays["in_masks"] = level_masks()
    args = []
    for n, a in arrays.items():
        t = nc.dram_tensor(n, a.shape, mybir.dt.from_np(a.dtype), kind="ExternalInput").ap()
        args.append(t[0] if n[3:].startswith("w_") else t)
    out = nc.dram_tensor("out", (1, S, D), F32, kind="ExternalOutput").ap()
    build(nc, args, out)
    r = run_bass_kernel_spmd(nc, [arrays], core_ids=[0])
    return r.results[0]["out"]
```

```python
from contextlib import ExitStack

import numpy as np

import concourse.bass as bass
from concourse import mybir

P = 128
F32 = mybir.dt.float32
F32R = mybir.dt.float32r
I32 = mybir.dt.int32
U8 = mybir.dt.uint8
ALU = mybir.AluOpType
ACT = mybir.ActivationFunctionType
AX = mybir.AxisListType.X

D = 2048
S = 256
NT = S // P
H = 8
NOPE, ROPE, VD = 128, 64, 128
QR, KVR = 512, 256
GH = 4
DK, DV = D // 2 // GH, D // GH
GR = 16
TAU = 16.0
FF = 5632
KT = D // P
EPS = 1e-6
THETA = 10000.0

C_Q = 0
C_KV = C_Q + QR
C_KR = C_KV + KVR
C_GQ = C_KR + ROPE
C_GK = C_GQ + GH * DK
C_GV = C_GK + GH * DK
C_LR = C_GV + GH * DV
C_OG = C_LR + GR
C_GA = C_OG + GH * DV
C_GB = C_GA + D

UC = 512
AC = 1024
RING = 4
ADA_BLOCK = D // P * (D // AC)
MLA_SCALE = float(NOPE + ROPE) ** -0.5
GLA_SCALE = float(DK) ** -0.5
LEVELS = 9

V_BADA, V_C, V_GPRE = 0, 96, 112
V_GQ, V_GKV, V_BGLA, V_GOUT, V_GFFN, V_CB = 128, 132, 134, 142, 146, 162
V_CW = 256
V_END = V_CW + 3 * 2 * FF // P

GROUPS = ([("misc", 8, 4), ("qlat", 8, 4)] + [("gq", 8, 4)] * 2
          + [("qup", 2, 4)] * 3 + [("kup", 2, 8)] + [("vup", 2, 4)]
          + [("gk", 8, 4)] * 2 + [("gv", 8, 2)] * 4 + [("og", 8, 4)] * 4
          + [("ga", 8, 4)] * 4 + [("gb", 8, 4)] * 4 + [("ba", 4, 4)] * 4 + [("bb", 8, 4)] * 4
          + [("mix", 8, 2)] * 4 + [("ffn", 8, 4)] * 22 + [("down", 22, 2)] * 4)


def starts(name):
    u = t = p = 0
    a = 2 * ADA_BLOCK
    for kind, nu, nt in GROUPS:
        if kind == name:
            return u, t, p, a
        u, t, p = u + nu, t + nt, p + nu // 2 - 1
        if nu in (4, 8) and a < 6 * ADA_BLOCK:
            a += nu // 2
    return u, t, p, a


UNITS = starts("end")[0]
FIRST_OF = {g[0]: starts(g[0]) for g in GROUPS}


def level_masks():
    j, i = np.arange(P)[:, None], np.arange(P)[None, :]
    out = [i == j]
    for lv in range(1, LEVELS - 1):
        h = 1 << (lv - 1)
        out.append((i // (2 * h) == j // (2 * h)) & (j % (2 * h) < h) & (i % (2 * h) >= h))
    return np.concatenate(out, axis=1).astype(np.int32)


def constants():
    ident = np.eye(P, dtype=np.float32)
    rot = np.zeros((P, P), np.float32)
    for b in (0, ROPE):
        for m in range(ROPE // 2):
            rot[b + m + ROPE // 2, b + m] = -1.0
            rot[b + m, b + m + ROPE // 2] = 1.0
    q, k = np.arange(P)[:, None], np.arange(P)[None, :]
    causal = np.where(k <= q, 0.0, -1e30).astype(np.float32)
    inv = 1.0 / (np.float32(THETA) ** (np.arange(0, ROPE, 2, dtype=np.float32) / np.float32(ROPE)))
    inv = np.tile(inv.astype(np.float32), 4)[:, None]
    return np.ascontiguousarray(np.concatenate([ident, rot, causal, inv], axis=1))


def build(nc, ap, out):
    (x, c, positions, w_ada, b_ada, g_pre_mix, w_in, g_q_lat, w_q_up, g_kv_lat, w_kv_up, w_gla_gate_up,
     b_gla_gate, g_gla_out, w_branch_a, w_branch_b, w_mix_out, g_post_mix, g_pre_ffn, w_ffn_up, conv_w,
     conv_b, w_ffn_down, g_post_ffn, const_f, const_m) = ap
    ctx = ExitStack()
    with ctx:
        def sb(name, shape, dt):
            return ctx.enter_context(nc.sbuf_tensor(name, shape, dt))

        def sem(name):
            return ctx.enter_context(nc.semaphore(name))

        raw = sb("raw", [P, RING, 2, UC], F32)
        w_hi = sb("w_hi", [P, RING, 2, UC], F32R)
        w_lo = sb("w_lo", [P, RING, 2, UC], F32R)
        acc = sb("acc", [P, D], F32)
        fixed = sb("fixed", [P, 3 * P + 1], F32)
        ident, rot, causal = (fixed[:, i * P:(i + 1) * P] for i in range(3))
        inv_freq = fixed[:, 3 * P:3 * P + 1]
        ones = sb("ones", [P, P], F32)
        masks = sb("masks", [P, LEVELS - 1, P], U8)
        cos_t = sb("cos_t", [P, S], F32)
        sin_t = sb("sin_t", [P, S], F32)
        vec = sb("vec", [P, V_END], F32)
        c_act = sb("c_act", [P, KT], F32)
        mod = sb("mod", [P, 6, KT], F32)
        cross = sb("cross", [P, 2, S], F32)
        ytmp = sb("ytmp", [P, 2, S], F32)
        eps_t = sb("eps_t", [P, 1], F32)
        stat = sb("stat", [P, 32], F32)
        cap_kb = 139 * 1024

        def at(kb, name, shape, dt, size_kb):
            words = 1
            for n in shape[1:]:
                words *= n
            assert words * 4 <= size_kb * 1024 and (kb + size_kb) * 1024 <= cap_kb, name
            with nc.sbuf_tensor(name + "_before", [P, max(kb, 0) * 256 + 8], F32):
                with nc.sbuf_tensor(name, shape, dt) as t:
                    pass
            return t

        ada = at(0, "ada", [P, RING, AC], F32, 16)
        conv_in = at(0, "conv_in", [P, 4, S + 2], F32, 5)
        conv_a = at(5, "conv_a", [P, 4, S], F32, 4)
        conv_v = at(9, "conv_v", [P, 2, S], F32, 2)
        hid_f = at(11, "hid_f", [P, 2, S], F32, 2)
        B = 16
        cap_kb = (B + 137) * 1024
        ht = at(B + 0, "ht", [P, KT, 2, S], F32R, 32)
        ot = at(B + 32, "ot", [P, H, 2, S], F32R, 16)
        og = at(B + 48, "og", [P, KT, S], F32, 16)
        v_gla = at(B + 64, "v_gla", [P, NT, GH * DV], F32, 16)
        q_gla = at(B + 80, "q_gla", [P, 8, S], F32, 8)
        k_gla = at(B + 88, "k_gla", [P, 8, S], F32, 8)
        x_tok = at(B + 96, "x_tok", [P, NT, D], F32, 16)
        xn_tok = at(B + 112, "xn_tok", [P, NT, D], F32, 16)
        xn_t = at(B + 48, "xn_t", [P, KT, S], F32, 16)
        h_f = at(B + 64, "h_f", [P, KT, S], F32, 16)
        junk = at(B + 80, "junk", [P, D], F32, 8)
        rows = at(B + 88, "rows", [P, 5, P], F32, 3)
        pos_i = at(B + 32, "pos_i", [P, S], I32, 1)
        pos_f = at(B + 33, "pos_f", [P, S], F32, 1)
        ang = at(B + 34, "ang", [P, S], F32, 1)
        turn = at(B + 35, "turn", [P, 2, S], F32, 2)
        red = at(B + 37, "red", [P, 2, S], F32, 2)
        masks_i = at(B + 39, "masks_i", [P, LEVELS - 1, P], I32, 4)
        lat = at(B + 48, "lat", [P, 6, S], F32, 6)
        lat_s = at(B + 54, "lat_s", [P, 6, 2, S], F32R, 12)
        lat_sq = at(B + 66, "lat_sq", [P, 6, S], F32, 6)
        q_rope_in = at(B + 72, "q_rope_in", [P, 4, S], F32, 4)
        rope_tmp = at(B + 76, "rope_tmp", [P, 2, S], F32, 2)
        lat_r = at(B + 78, "lat_r", [P, 2, S], F32, 2)
        q_nope = at(B + 96, "q_nope", [P, H, S], F32, 8)
        k_nope = at(B + 104, "k_nope", [P, H, S], F32, 8)
        v_mla = at(B + 112, "v_mla", [P, NT, H * VD], F32, 8)
        q_rope = at(B + 120, "q_rope", [P, 4, S], F32, 4)
        k_rope = at(B + 124, "k_rope", [P, S], F32, 1)
        probs = at(B + 125, "probs", [P, 3, 4 * P], F32, 6)
        probs_t = at(B + 131, "probs_t", [P, 2, 3 * P], F32, 3)
        k_rope_in = at(B + 134, "k_rope_in", [P, S], F32, 1)
        lr_t = at(B + 135, "lr_t", [P, S], F32, 1)
        soft = at(B + 136, "soft", [P, 3, 8], F32, 1)
        w_gate = at(B + 48, "w_gate", [P, GH * DK], F32, 4)
        pre = at(B + 96, "pre", [P, 8, S], F32, 8)
        suf = at(B + 104, "suf", [P, 8, S], F32, 8)
        dec = at(B + 112, "dec", [P, 8, S], F32, 8)
        qk = at(B + 120, "qk", [P, 8, S], F32, 8)
        attn0 = at(B + 128, "attn0", [P, GH, S], F32, 4)
        attn1 = at(B + 132, "attn1", [P, GH, P], F32, 2)
        o_gla = at(B + 96, "o_gla", [P, KT, S], F32, 16)
        o_sq = at(B + 112, "o_sq", [P, 4, S], F32, 4)
        o_r = at(B + 128, "o_r", [P, GH, S], F32, 4)
        og_s = at(B + 0, "og_s", [P, KT, 2, S], F32R, 32)
        gate_a = at(B + 80, "gate_a", [P, KT, S], F32, 16)
        gate_b = at(B + 112, "gate_b", [P, KT, S], F32, 16)
        merged = at(B + 32, "merged", [P, KT, 2, S], F32R, 32)
        gg_m = at(B + 64, "gg_m", [P, D], F32, 8)
        gpost_m = at(B + 72, "gpost_m", [P, D], F32, 8)
        brow_m = at(B + 128, "brow_m", [P, UC], F32, 2)
        x_again = at(B + 96, "x_again", [P, NT, D], F32, 16)
        x1 = at(B + 121, "x1", [P, NT, D], F32, 16)
        xn1 = at(B + 80, "xn1", [P, NT, D], F32, 16)
        h2_f = at(B + 32, "h2_f", [P, KT, S], F32, 16)
        junk_m = at(B + 112, "junk_m", [P, D], F32, 8)
        h2t = at(B + 0, "h2t", [P, KT, 2, S], F32R, 32)
        hid = at(B + 32, "hid", [P, FF // P, 2, S], F32R, 88)
        f_tok = at(B + 0, "f_tok", [P, NT, D], F32, 16)
        gg_f = at(B + 16, "gg_f", [P, D], F32, 8)
        gpost_f = at(B + 24, "gpost_f", [P, D], F32, 8)
        junk_f = at(5, "junk_f", [P, UC], F32, 2)
        brow_f = at(13, "brow_f", [P, UC], F32, 2)

        ps = ctx.enter_context(nc.psum_tensor("ps", [P, 8, UC], F32))

        x_loaded, rows_loaded, const_loaded = sem("x_loaded"), sem("rows_loaded"), sem("const_loaded")
        gate_w_loaded, post_loaded, x_again_loaded = sem("gate_w_loaded"), sem("post_loaded"), sem("x_again_loaded")
        post_f_loaded, bias_f_loaded, stored = sem("post_f_loaded"), sem("bias_f_loaded"), sem("stored")
        raw_loaded = [sem(f"raw_loaded{r}") for r in range(RING)]
        ada_loaded = [sem(f"ada_loaded{r}") for r in range(RING)]
        hi_done, lo_done = sem("hi_done"), sem("lo_done")
        pairs_used = sem("pairs_used")
        tile_ready = sem("tile_ready")
        tile_half = sem("tile_half")
        tile_empty = sem("tile_empty")
        ada_used = sem("ada_used")
        acc_zero, acc_read = sem("acc_zero"), sem("acc_read")
        mod_ready, mod_psum = sem("mod_ready"), sem("mod_psum")
        dve_step, act_step, pool_step = sem("dve_step"), sem("act_step"), sem("pool_step")
        setup_done = sem("setup_done")
        rows_t, vec_ready, c_ready = sem("rows_t"), sem("vec_ready"), sem("c_ready")
        ssq_x, rms_x, norm_x, xt_psum, xt_copied = (sem("ssq_x"), sem("rms_x"), sem("norm_x"), sem("xt_psum"),
                                                    sem("xt_copied"))
        h_ready, h_hi, h_lo = sem("h_ready"), sem("h_hi"), sem("h_lo")
        angle_ready, table_ready = sem("angle_ready"), sem("table_ready")
        lat_squared, lat_summed, lat_rms, lat_normed, lat_hi, lat_lo = (
            sem("lat_squared"), sem("lat_summed"), sem("lat_rms"), sem("lat_normed"), sem("lat_hi"), sem("lat_lo"))
        rot_ready, rope_done = sem("rot_ready"), sem("rope_done")
        scores_ready, max_ready, exp_done, probs_ready = (sem("scores_ready"), sem("max_ready"), sem("exp_done"),
                                                          sem("probs_ready"))
        pt_ready, pt_copied, ctx_ready, ctx_hi, ctx_lo = (sem("pt_ready"), sem("pt_copied"), sem("ctx_ready"),
                                                          sem("ctx_hi"), sem("ctx_lo"))
        gate_psum, gate_pre, gate_soft, decay_ready = (sem("gate_psum"), sem("gate_pre"), sem("gate_soft"),
                                                       sem("decay_ready"))
        dec_ready, qk_ready, scan_ready, level_ready, level_taken = (
            sem("dec_ready"), sem("qk_ready"), sem("scan_ready"), sem("level_ready"), sem("level_taken"))
        og_psum, og_copied, og_squared, og_summed, og_rms, og_silu, og_gated, og_hi, og_lo = (
            sem("og_psum"), sem("og_copied"), sem("og_squared"), sem("og_summed"), sem("og_rms"), sem("og_silu"),
            sem("og_gated"), sem("og_hi"), sem("og_lo"))
        sig_done, mul_done, merged_ready, merged_hi, merged_lo = (
            sem("sig_done"), sem("mul_done"), sem("merged_ready"), sem("merged_hi"), sem("merged_lo"))
        gate_row, gg_ready = sem("gate_row"), sem("gg_ready")
        rms_y, x1_ready, ssq_1, rms_1, norm_1, x1t_psum, h2_ready, h2_hi, h2_lo = (
            sem("rms_y"), sem("x1_ready"), sem("ssq_1"), sem("rms_1"), sem("norm_1"), sem("x1t_psum"),
            sem("h2_ready"), sem("h2_hi"), sem("h2_lo"))
        conv_first, conv_done, gelu_done, hid_ready, hid_hi, hid_lo = (
            sem("conv_first"), sem("conv_done"), sem("gelu_done"), sem("hid_ready"), sem("hid_hi"), sem("hid_lo"))
        sum_f, rms_f, out_ready = sem("sum_f"), sem("rms_f"), sem("out_ready")

        def halves(t, h):
            v = t[:, :, :].rearrange("p d (b s h) -> p (d b) s h", s=2, h=h)
            return v[:, :, 0, :], v[:, :, 1, :]

        def spread(col, like):
            return col.to_broadcast(list(like.shape))

        class Steps:

            def __init__(self, eng, s):
                self.eng, self.s, self.n = eng, s, 0

            def mark(self, ins):
                ins.then_inc(self.s, 1)
                self.n = self.n + 1

            def wait(self):
                self.eng.wait_ge(self.s, self.n)

        block = ctx.enter_context(nc.Block())

        @block.sync
        def _(sp):
            def load_unit(u, r, src):
                if not isinstance(u, int) or u >= RING:
                    sp.wait_ge(lo_done, u - (RING - 1))
                sp.dma_start(raw[:, r], src).then_inc(raw_loaded[r], 16)

            def load_ada(a, r, src):
                if not isinstance(a, int) or a >= RING:
                    sp.wait_ge(ada_used, a - (RING - 1))
                sp.dma_start(ada[:, r], src).then_inc(ada_loaded[r], 16)

            def two_kt(w, row0, col0):
                return w[bass.ds(row0, 2 * P), bass.ds(col0, UC)].rearrange("(k p) n -> p k n", p=P)

            def ada_src(block_no, kt, half):
                return w_ada[bass.ds(kt * P, P), bass.ds(block_no * D + half * AC, AC)]

            def group(u0, nu, src, a0=None, a_block=None, a_kt=None, slot0=0):
                for j in range(nu):
                    load_unit(u0 + j, (slot0 + j) % RING, src(j))
                    if a0 is not None and j % 2 == 1:
                        n = j // 2
                        load_ada(a0 + n, n % RING, ada_src(a_block, a_kt + n // 2, n % 2))

            sp.dma_start(x_tok[:], x[0].rearrange("(t p) d -> p t d", p=P)).then_inc(x_loaded, 16)
            n_small = 0

            def small(dst, src):
                sp.dma_start(dst, src).then_inc(rows_loaded, 16)

            def as_rows(v):
                return v.rearrange("(r c) -> r c", c=P)

            for dst0, v in ((0, b_ada[0]), (96, c[0]), (112, g_pre_mix[0])):
                n = v.shape[0] // P
                small(rows[dst0:dst0 + n, 0, :], as_rows(v))
            for v0, v in ((V_GQ, g_q_lat[0]), (V_GKV, g_kv_lat[0]), (V_BGLA, b_gla_gate[0]), (V_GOUT, g_gla_out[0]),
                          (V_GFFN, g_pre_ffn[0]), (V_CB, conv_b[0])):
                n = v.shape[0] // P
                small(rows[v0 - P:v0 - P + n, 1, :], as_rows(v))
            cw = conv_w[0].rearrange("i (r c) -> (i r) c", c=P)
            for k in range(3):
                n = min(P, cw.shape[0] - k * P)
                small(rows[0:n, 2 + k, :], cw[k * P:k * P + n, :])
            sp.dma_start(fixed[:], const_f).then_inc(const_loaded, 16)
            sp.dma_start(masks_i[:, :, :].rearrange("p l n -> p (l n)"), const_m).then_inc(const_loaded, 16)
            sp.dma_start(pos_i[:], positions[0:1, :].to_broadcast([P, S])).then_inc(const_loaded, 16)

            for a in range(RING):
                load_ada(a, a, ada_src(0, a // 2, a % 2))
            with sp.Fori(1, KT // 2) as i:
                for r in range(RING):
                    load_ada(4 * i + r, r, ada_src(0, 2 * i + r // 2, r % 2))
            with sp.Fori(0, KT // 2) as i:
                for r in range(RING):
                    load_ada(ADA_BLOCK + 4 * i + r, r, ada_src(1, 2 * i + r // 2, r % 2))

            u0, _, _, a0 = FIRST_OF["misc"]
            for j in range(8):
                r = j % RING
                rs = w_in[j * 2 * P:(j + 1) * 2 * P, :].rearrange("(k p) n -> p k n", p=P)
                if j >= RING:
                    sp.wait_ge(lo_done, j - (RING - 1))
                sp.dma_start(raw[:, r, :, 0:320], rs[:, :, C_KV:C_KV + 320]).then_inc(raw_loaded[r], 16)
                sp.dma_start(raw[:, r, :, 320:384], rs[:, :, C_KR:C_KR + ROPE]).then_inc(raw_loaded[r], 16)
                sp.dma_start(raw[:, r, :, 384:512], rs[:, :, C_LR:C_LR + P]).then_inc(raw_loaded[r], 16)
                if j % 2 == 1:
                    n = j // 2
                    load_ada(a0 + n, n, ada_src(3, n // 2, n % 2))
            u0, _, _, a0 = FIRST_OF["qlat"]
            group(u0, 8, lambda j: two_kt(w_in, 256 * j, C_Q), a0, 3, 2)
            u0, _, _, a0 = FIRST_OF["gq"]
            with sp.Fori(0, 2) as g:
                group(u0 + 8 * g, 8, lambda j: two_kt(w_in, 256 * j, C_GQ + UC * g), a0 + 4 * g, 3, 4 + 2 * g)
            u0 = FIRST_OF["qup"][0]
            qv = w_q_up.rearrange("(k p) (h e) -> p k h e", p=P, e=NOPE + ROPE)
            for n in range(6):
                g, j = n // 2, n % 2
                r = (u0 + n) % RING
                sp.wait_ge(lo_done, u0 + n - (RING - 1))
                for k in range(2):
                    if g < 2:
                        dst = raw[:, r, k, :].rearrange("p (h e) -> p h e", h=4)
                        sp.dma_start(dst, qv[:, 2 * j + k, 4 * g:4 * g + 4, 0:NOPE]).then_inc(raw_loaded[r], 8 * 2)
                    else:
                        dst = raw[:, r, k, :].rearrange("p (h e) -> p h e", h=H)
                        sp.dma_start(dst, qv[:, 2 * j + k, :, NOPE:NOPE + ROPE]).then_inc(raw_loaded[r], 8 * 2)
            u0 = FIRST_OF["kup"][0]
            kvv = w_kv_up.rearrange("(k p) (h e) -> p k h e", p=P, e=NOPE + VD)
            for n in range(4):
                part, hh = n // 2, n % 2
                r = (u0 + n) % RING
                sp.wait_ge(lo_done, u0 + n - (RING - 1))
                for k in range(2):
                    dst = raw[:, r, k, :].rearrange("p (h e) -> p h e", h=4)
                    sp.dma_start(dst, kvv[:, k, 4 * hh:4 * hh + 4, part * NOPE:part * NOPE + P])\
                        .then_inc(raw_loaded[r], 16)
            s0 = FIRST_OF["gk"][0] % RING
            u0, _, _, a0 = FIRST_OF["gk"]
            with sp.Fori(0, 2) as g:
                group(u0 + 8 * g, 8, lambda j: two_kt(w_in, 256 * j, C_GK + UC * g), a0 + 4 * g, 3, 8 + 2 * g, s0)
            sp.wait_ge(tile_ready, FIRST_OF["gk"][1])
            sp.dma_start(w_gate[0:GR, :], w_gla_gate_up).then_inc(gate_w_loaded, 16)
            u0, _, _, a0 = FIRST_OF["gv"]
            with sp.Fori(0, 2) as g:
                group(u0 + 8 * g, 8, lambda j: two_kt(w_in, 256 * j, C_GV + UC * g), a0 + 4 * g, 3, 12 + 2 * g, s0)
            with sp.Fori(2, 4) as g:
                group(u0 + 8 * g, 8, lambda j: two_kt(w_in, 256 * j, C_GV + UC * g), a0 + 4 * g, 4, 2 * g - 4, s0)
            u0, _, _, a0 = FIRST_OF["og"]
            with sp.Fori(0, 6) as g:
                group(u0 + 8 * g, 8, lambda j: two_kt(w_in, 256 * j, C_OG + UC * g), a0 + 4 * g, 4, 4 + 2 * g, s0)
            with sp.Fori(6, 12) as g:
                group(u0 + 8 * g, 8, lambda j: two_kt(w_in, 256 * j, C_OG + UC * g), a0 + 4 * g, 2, 2 * g - 12, s0)
            sp.wait_ge(og_psum, 8)
            sp.dma_start(gpost_m[:], g_post_mix[0:1, :].to_broadcast([P, D])).then_inc(post_loaded, 16)
            u0, _, _, a0 = FIRST_OF["ba"]
            with sp.Fori(0, 2) as g:
                for n in range(2):
                    group(u0 + 8 * g + 4 * n, 4, lambda j: two_kt(w_branch_a, 256 * j, 2 * UC * g + UC * n),
                          None, None, None, s0)
                    for m in range(2):
                        load_ada(a0 + 4 * g + 2 * n + m, 2 * n + m, ada_src(2, 12 + 2 * g + n, m))
            sp.wait_ge(og_gated, 4)
            for b in range(4):
                c0 = 2 * D + b * UC
                sp.dma_start(brow_m[32 * b:32 * b + 1, :], b_ada[0:1, c0:c0 + UC]).then_inc(post_loaded, 16)
            u0, _, _, a0 = FIRST_OF["bb"]
            with sp.Fori(0, 4) as g:
                group(u0 + 8 * g, 8, lambda j: two_kt(w_branch_b, 256 * j, UC * g), a0 + 4 * g, 5, 2 * g, s0)
            sp.wait_ge(og_lo, 4)
            sp.dma_start(x_again[:], x[0].rearrange("(t p) d -> p t d", p=P)).then_inc(x_again_loaded, 16)
            u0, _, _, a0 = FIRST_OF["mix"]
            with sp.Fori(0, 4) as g:
                group(u0 + 8 * g, 8, lambda j: two_kt(w_mix_out, 256 * j, UC * g), a0 + 4 * g, 5, 8 + 2 * g, s0)
            u0 = FIRST_OF["ffn"][0]
            with sp.Fori(0, 11) as g:
                for part in range(2):
                    group(u0 + 16 * g + 8 * part, 8,
                          lambda j: two_kt(w_ffn_up, 256 * j, part * FF + UC * g), None, None, None, s0)
            for b in range(4):
                c0 = 5 * D + b * UC
                sp.dma_start(brow_f[32 * b:32 * b + 1, :], b_ada[0:1, c0:c0 + UC]).then_inc(bias_f_loaded, 16)
            u0, t0, _, _ = FIRST_OF["down"]
            for n in range(4):
                for j in range(22):
                    load_unit(u0 + 22 * n + j, (s0 + 22 * n + j) % RING, two_kt(w_ffn_down, 256 * j, UC * n))
                    if n == 0 and j == RING:
                        sp.wait_ge(tile_ready, t0)
                        sp.dma_start(gpost_f[:], g_post_ffn[0:1, :].to_broadcast([P, D])).then_inc(post_f_loaded, 16)
            for n in range(4):
                t, c0 = n // 2, (n % 2) * (D // 2)
                sp.wait_ge(out_ready, n + 1)
                sp.dma_start(out[0, t * P:(t + 1) * P, c0:c0 + D // 2], f_tok[:, t, c0:c0 + D // 2])\
                    .then_inc(stored, 16)
            sp.wait_ge(stored, 64)

        @block.tensor
        def _(pe):
            mm = nc.tensor.matmul

            def tile_free(t):
                if not isinstance(t, int) or t >= 4:
                    pe.wait_ge(tile_empty, t - 3)

            def feature_pair(u, t0, kt0, last, moving, slot, first, moving_ready=None):
                pe.wait_ge(lo_done, u + 2)
                if moving_ready is not None:
                    pe.wait_ge(moving_ready, kt0 // 4 + 1)
                for f in range(4):
                    if first:
                        tile_free(t0 + f)
                    for j in range(2):
                        s = (slot + j) % RING
                        for k in range(2):
                            kt = kt0 + 2 * j + k
                            start = first and j == 0 and k == 0
                            stop = last and j == 1 and k == 1
                            cols = slice(f * P, (f + 1) * P)
                            mm(ps[:, f, :], w_hi[:, s, k, cols], moving[:, kt].rearrange("p a t -> p (a t)"),
                               start=start, stop=False)
                            ins = mm(ps[:, f, 0:S], w_lo[:, s, k, cols], moving[:, kt, 0], start=False, stop=stop)
                    if last:
                        ins.then_inc(tile_ready, 1)
                if not last:
                    ins.then_inc(pairs_used, 1)

            def feature_group(u0, t0, nu, moving, slot, kt0=0, moving_ready=None):
                for j in range(0, nu, 2):
                    feature_pair(u0 + j, t0, kt0 + 2 * j, j == nu - 2, moving, (slot + j) % RING, j == 0, moving_ready)

            def token_group(u0, t0, nu, still, slot, bank0):
                for j in range(0, nu, 2):
                    first, last = j == 0, j == nu - 2
                    pe.wait_ge(lo_done, u0 + j + 2)
                    for t in range(NT):
                        if first:
                            tile_free(t0 + t)
                        o = ps[:, bank0 + t, :]
                        for i in range(2):
                            s = (slot + j + i) % RING
                            for k in range(2):
                                kt = 2 * (j + i) + k
                                tok = slice(t * P, (t + 1) * P)
                                start = first and i == 0 and k == 0
                                mm(o, still[:, kt, 0, tok], w_hi[:, s, k, :], start=start, stop=False)
                                mm(o, still[:, kt, 0, tok], w_lo[:, s, k, :], start=False, stop=False)
                                ins = mm(o, still[:, kt, 1, tok], w_hi[:, s, k, :], start=False,
                                         stop=last and i == 1 and k == 1)
                        if last:
                            ins.then_inc(tile_ready, 1)
                    if not last:
                        ins.then_inc(pairs_used, 1)

            def mod_columns(n_block, used, bank=4):
                pe.wait_ge(ada_used, used)
                if n_block:
                    pe.wait_ge(mod_ready, n_block)
                for i in range(KT):
                    ins = mm(ps[:, bank, i:i + 1], acc[:, i * P:(i + 1) * P], ones[:, 0:1], start=True, stop=True)
                ins.then_inc(mod_psum, 1)

            pe.wait_ge(rows_loaded, 12 * 16)
            pe.wait_ge(const_loaded, 3 * 16)
            for k in range(5):
                n = (P, P - 6, P, P, V_END - V_CW - 2 * P)[k]
                ins = nc.tensor.transpose(ps[:, 4 + k // 4, (k % 4) * P:(k % 4) * P + n], rows[0:n, k, :],
                                          ident[0:n, 0:n])
            ins.then_inc(rows_t, 1)
            pe.wait_ge(norm_x, 2)
            pe.wait_ge(vec_ready, 1)
            for b in range(8):
                for q in range(4):
                    kt, t = 2 * b + q // 2, q % 2
                    ins = nc.tensor.transpose(ps[:, b, q * P:(q + 1) * P], xn_tok[:, t, kt * P:(kt + 1) * P], ident[:])
                ins.then_inc(xt_psum, 1)
            pe.wait_ge(xt_copied, 8)
            pe.wait_ge(setup_done, 2)
            mod_columns(0, ADA_BLOCK)
            mod_columns(1, 2 * ADA_BLOCK)
            feature_group(0, 0, 8, ht, 0, moving_ready=h_lo)
            feature_group(8, 4, 8, ht, 0)
            u0, t0, _, _ = FIRST_OF["gq"]
            feature_group(u0, t0, 8, ht, 0)
            pe.wait_ge(lat_squared, 1)
            pe.wait_ge(mod_ready, 2)
            for n, (f0, nf) in enumerate(((0, 2), (2, 4))):
                for i in range(nf):
                    ins = mm(ps[:, 4, n * S:(n + 1) * S], ones[:], lat_sq[:, f0 + i, :], start=i == 0, stop=i == nf - 1)
            ins.then_inc(lat_summed, 1)
            feature_group(u0 + 8, t0 + 4, 8, ht, 0)
            pe.wait_ge(lat_lo, 1)
            u0, t0, _, _ = FIRST_OF["qup"]
            for g in range(3):
                feature_group(u0 + 2 * g, t0 + 4 * g, 2, lat_s, (u0 + 2 * g) % RING, 2)
            u0, t0, _, _ = FIRST_OF["kup"]
            pe.wait_ge(lo_done, u0 + 2)
            for n in range(8):
                f, s = n % 4, (u0 + n // 4) % RING
                tile_free(t0 + n)
                for k in range(2):
                    cols = slice(f * P, (f + 1) * P)
                    mm(ps[:, f, :], w_hi[:, s, k, cols], lat_s[:, k].rearrange("p a t -> p (a t)"), start=k == 0,
                       stop=False)
                    ins = mm(ps[:, f, 0:S], w_lo[:, s, k, cols], lat_s[:, k, 0], start=False, stop=k == 1)
                ins.then_inc(tile_ready, 1)
            u0, t0, _, _ = FIRST_OF["vup"]
            pe.wait_ge(lo_done, u0 + 2)
            for n in range(4):
                half, t = n // 2, n % 2
                s = (u0 + half) % RING
                tile_free(t0 + n)
                tok = slice(t * P, (t + 1) * P)
                for k in range(2):
                    mm(ps[:, n, :], lat_s[:, k, 0, tok], w_hi[:, s, k, :], start=k == 0, stop=False)
                    mm(ps[:, n, :], lat_s[:, k, 0, tok], w_lo[:, s, k, :], start=False, stop=False)
                    ins = mm(ps[:, n, :], lat_s[:, k, 1, tok], w_hi[:, s, k, :], start=False, stop=k == 1)
                ins.then_inc(tile_ready, 1)

            def rope_rotate():
                pe.wait_ge(tile_empty, FIRST_OF["kup"][1])
                pe.wait_ge(lat_rms, 1)
                for i in range(4):
                    mm(ps[:, 4 + i // 2, (i % 2) * S:(i % 2 + 1) * S], rot[:], q_rope_in[:, i, :], start=True, stop=True)
                mm(ps[:, 6, 0:S], rot[:], k_rope_in[:], start=True, stop=True).then_inc(rot_ready, 1)

            def scores(h):
                if h == 0:
                    pe.wait_ge(rope_done, 5)
                    pe.wait_ge(tile_empty, FIRST_OF["vup"][1])
                else:
                    pe.wait_ge(max_ready, h)
                p0 = ROPE * (h % 2)
                for t in range(NT):
                    o = ps[:, 4, t * P:t * P + (t + 1) * P]
                    tok, keys = slice(t * P, (t + 1) * P), slice(0, (t + 1) * P)
                    mm(o, q_nope[:, h, tok], k_nope[:, h, keys], start=True, stop=False)
                    ins = mm(o, q_rope[p0:p0 + ROPE, h // 2, tok], k_rope[p0:p0 + ROPE, keys], start=False, stop=True)
                ins.then_inc(scores_ready, 1)

            def transpose_probs(h):
                pe.wait_ge(probs_ready, h + 1)
                if h:
                    pe.wait_ge(pt_copied, h)
                for i in range(3):
                    ins = nc.tensor.transpose(ps[:, 5, i * P:(i + 1) * P], probs[:, h % 3, i * P:(i + 1) * P], ident[:])
                ins.then_inc(pt_ready, 1)

            def context(h):
                pe.wait_ge(pt_copied, h + 1)
                if h:
                    pe.wait_ge(ctx_lo, h)
                else:
                    pe.wait_ge(tile_empty, FIRST_OF["gk"][1])
                hv = slice(h * VD, (h + 1) * VD)
                mm(ps[:, 6, 0:S], v_mla[:, 0, hv], probs_t[:, h % 2, 0:S], start=True, stop=False)
                mm(ps[:, 6, P:S], v_mla[:, 1, hv], probs_t[:, h % 2, S:3 * P], start=False, stop=True)\
                    .then_inc(ctx_ready, 1)

            def mla_at(step):
                h, odd = step // 2, step % 2
                if not odd:
                    if h < H:
                        scores(h)
                    if 0 <= h - 2 < H:
                        context(h - 2)
                elif 0 <= h - 1 < H:
                    transpose_probs(h - 1)

            def gate_preact(n):
                if n == 0:
                    pe.wait_ge(ctx_lo, H)
                    pe.wait_ge(gate_w_loaded, 16)
                else:
                    pe.wait_ge(gate_pre, 4)
                for i in range(4):
                    ft = 4 * n + i
                    ins = mm(ps[:, 6 + i // 2, (i % 2) * S:(i % 2 + 1) * S], w_gate[0:GR, ft * P:(ft + 1) * P],
                             lr_t[0:GR, :], start=True, stop=True)
                ins.then_inc(gate_psum, 1)

            def level(lv):
                pe.wait_ge(qk_ready, lv) if lv else pe.wait_ge(gate_pre, 8)
                if lv:
                    pe.wait_ge(level_taken, lv)
                else:
                    pe.wait_ge(tile_empty, FIRST_OF["gv"][1])
                n_q = P if lv in (0, LEVELS - 1) else P // 2
                for t in range(NT if lv < LEVELS - 1 else 1):
                    for hd in range(GH):
                        o = ps[:, 6 + t, hd * n_q:(hd + 1) * n_q]
                        for i in range(2):
                            d = 2 * hd + i
                            keys = slice(t * P, (t + 1) * P)
                            if lv == 0:
                                lhs, rhs = k_gla, q_gla[:, d, keys]
                            elif lv == LEVELS - 1:
                                lhs, rhs = qk, qk[:, d, P:2 * P]
                            else:
                                lhs = qk
                                rhs = qk[:, d, keys].rearrange("p (b s h) -> p b s h", s=2, h=1 << (lv - 1))[:, :, 1]
                            ins = mm(o, lhs[:, d, keys], rhs, start=i == 0, stop=i == 1)
                ins.then_inc(level_ready, 1)

            def gla_out(pr):
                if pr < 2:
                    pe.wait_ge(level_taken, LEVELS)
                    pe.wait_ge(tile_empty, FIRST_OF["og"][1])
                else:
                    pe.wait_ge(og_copied, pr - 1)
                for i in range(2):
                    ft = 2 * pr + i
                    hd = ft // 4
                    fv = slice(ft * P, (ft + 1) * P)
                    o = ps[:, 6 + pr % 2, i * S:(i + 1) * S]
                    mm(o, v_gla[:, 0, fv], attn0[:, hd, :], start=True, stop=False)
                    ins = mm(ps[:, 6 + pr % 2, i * S + P:(i + 1) * S], v_gla[:, 1, fv], attn1[:, hd, :], start=False,
                             stop=True)
                ins.then_inc(og_psum, 1)

            def gla_norm_sum(hd):
                pe.wait_ge(og_squared, hd + 1)
                for i in range(4):
                    ins = mm(ps[:, 4 + hd // 2, (hd % 2) * S:(hd % 2 + 1) * S], ones[:], o_sq[:, i, :],
                             start=i == 0, stop=i == 3)
                ins.then_inc(og_summed, 1)

            rope_rotate()
            s0 = FIRST_OF["gk"][0] % RING
            step = 0
            for g in range(2):
                u0, t0, _, _ = FIRST_OF["gk"]
                for j in range(0, 8, 2):
                    feature_pair(u0 + 8 * g + j, t0 + 4 * g, 2 * j, j == 6, ht, (s0 + j) % RING, j == 0)
                    mla_at(step)
                    step += 1
            u0, t0, _, _ = FIRST_OF["gv"]
            for g in range(4):
                for j in range(0, 8, 2):
                    first, last = j == 0, j == 6
                    pe.wait_ge(lo_done, u0 + 8 * g + j + 2)
                    for t in range(NT):
                        if first:
                            tile_free(t0 + 2 * g + t)
                        o = ps[:, (2 * g + t) % 4, :]
                        for i in range(2):
                            s = (s0 + j + i) % RING
                            for k in range(2):
                                kt = 2 * (j + i) + k
                                tok = slice(t * P, (t + 1) * P)
                                mm(o, ht[:, kt, 0, tok], w_hi[:, s, k, :], start=first and i == 0 and k == 0, stop=False)
                                mm(o, ht[:, kt, 0, tok], w_lo[:, s, k, :], start=False, stop=False)
                                ins = mm(o, ht[:, kt, 1, tok], w_hi[:, s, k, :], start=False,
                                         stop=last and i == 1 and k == 1)
                        if last:
                            ins.then_inc(tile_ready, 1)
                    if not last:
                        ins.then_inc(pairs_used, 1)
                    mla_at(step)
                    if step in (19, 20):
                        gate_preact(step - 19)
                    if step == 22:
                        level(0)
                    if g == 2 and first:
                        pe.wait_ge(max_ready, H)
                        mod_columns(2, 3 * ADA_BLOCK)
                    step += 1
            u0, t0, _, _ = FIRST_OF["og"]
            for g in range(4):
                for j in range(0, 8, 2):
                    feature_pair(u0 + 8 * g + j, t0 + 4 * g, 2 * j, j == 6, ht, (s0 + j) % RING, j == 0)
                    if step % 2 == 1 and 1 <= (step - 23) // 2 <= LEVELS - 1:
                        level((step - 23) // 2)
                    step += 1
            u0, t0, _, _ = FIRST_OF["ga"]
            for g in range(4):
                for j in range(0, 8, 2):
                    feature_pair(u0 + 8 * g + j, t0 + 4 * g, 2 * j, j == 6, ht, (s0 + j) % RING, j == 0)
                    n = step - 40
                    if n < 8:
                        gla_out(n)
                    if n % 2 == 1 and 3 <= n <= 9:
                        if n == 3:
                            pe.wait_ge(mod_ready, 3)
                        gla_norm_sum((n - 3) // 2)
                    if g == 2 and j == 0:
                        pe.wait_ge(og_copied, 7)
                        mod_columns(3, 4 * ADA_BLOCK, 6)
                    step += 1
            pe.wait_ge(og_rms, 1)
            with pe.Fori(4, 8) as g:
                feature_group(u0 + 8 * g, t0 + 4 * g, 8, ht, s0)
            pe.wait_ge(ctx_lo, H)
            u0, t0, _, _ = FIRST_OF["ba"]
            with pe.Fori(0, 4) as g:
                feature_group(u0 + 4 * g, t0 + 4 * g, 4, ot, s0)

            def gate_rows(used, brow):
                pe.wait_ge(ada_used, used)
                for b in range(4):
                    cols = slice(b * UC, (b + 1) * UC)
                    mm(ps[:, 4 + b, :], ones[:], acc[:, cols], start=True, stop=False)
                    row = slice(32 * b, 32 * b + 1)
                    ins = mm(ps[:, 4 + b, :], ones[row, :], brow[row, :], start=False, stop=True)
                ins.then_inc(gate_row, 1)

            pe.wait_ge(mod_ready, 4)
            pe.wait_ge(og_copied, 8)
            pe.wait_ge(post_loaded, 16 * 5)
            gate_rows(5 * ADA_BLOCK, brow_m)
            u0, t0, _, _ = FIRST_OF["bb"]
            with pe.Fori(0, 4) as g:
                feature_group(u0 + 8 * g, t0 + 4 * g, 8, og_s, s0, moving_ready=og_lo)
            u0, t0, _, _ = FIRST_OF["mix"]
            pe.wait_ge(merged_lo, KT)
            with pe.Fori(0, 2) as g:
                for n in range(2):
                    token_group(u0 + 16 * g + 8 * n, t0 + 4 * g + 2 * n, 8, merged, s0, 2 * n)
            pe.wait_ge(tile_empty, FIRST_OF["ffn"][1])
            pe.wait_ge(gg_ready, 1)
            pe.wait_ge(norm_1, 2)
            for b in range(8):
                for q in range(4):
                    kt, t = 2 * b + q // 2, q % 2
                    ins = nc.tensor.transpose(ps[:, b, q * P:(q + 1) * P], xn1[:, t, kt * P:(kt + 1) * P], ident[:])
                ins.then_inc(x1t_psum, 1)
            pe.wait_ge(h2_lo, 2)
            u0, t0, _, _ = FIRST_OF["ffn"]
            with pe.Fori(0, 11) as g:
                for part in range(2):
                    feature_group(u0 + 16 * g + 8 * part, t0 + 8 * g + 4 * part, 8, h2t, s0, moving_ready=h2_lo)
            pe.wait_ge(bias_f_loaded, 16 * 4)
            gate_rows(6 * ADA_BLOCK, brow_f)
            u0, t0, _, _ = FIRST_OF["down"]
            pe.wait_ge(hid_lo, FF // P + 1)
            with pe.Fori(0, 2) as g:
                for n in range(2):
                    token_group(u0 + 44 * g + 22 * n, t0 + 4 * g + 2 * n, 22, hid, (s0 + 22 * n) % RING, 2 * n)

        @block.scalar
        def _(act):
            A = nc.scalar.activation
            own = Steps(act, act_step)

            def split(u, slot, loaded, free_sem, free_at):
                act.wait_ge(raw_loaded[slot], loaded)
                if free_sem is not None:
                    act.wait_ge(free_sem, free_at)
                A(w_hi[:, slot], raw[:, slot], ACT.Copy).then_inc(hi_done, 1)

            def loads(u):
                u_q, u_k = FIRST_OF["qup"][0], FIRST_OF["gk"][0]
                return 3 if u < 8 else 2 if u_q <= u < u_k else 1

            total = [0] * (UNITS + 1)
            for u in range(UNITS):
                total[u] = loads(u) * 16 + (total[u - RING] if u >= RING else 0)

            def split_at(u0, j, t0, p0, nu=8, nt=4, g=None, per=8):
                u = u0 + 2 + j
                if u >= UNITS:
                    return
                loaded = total[u] if g is None else total[u] + g * (16 * per // RING)
                free = (tile_ready, t0 + nt) if j >= nu else (pairs_used, p0 + (j - 2) // 2 + 1)
                split(u, u % RING, loaded, *free)

            def half_tile(t, bank, scale=1.0):
                act.wait_ge(tile_ready, t + 1)
                if not isinstance(t, int) or t >= 2:
                    act.wait_ge(tile_empty, t - 1)
                A(cross[:, bank % 2], ps[:, bank, S:2 * S], ACT.Copy, scale=scale).then_inc(tile_half, 1)

            act.wait_ge(x_loaded, 16)
            for t in range(NT):
                A(junk[:], x_tok[:, t], ACT.Square, accum_out=stat[:, t:t + 1]).then_inc(ssq_x, 1)
                act.wait_ge(ssq_x, t + 1)
            act.wait_ge(setup_done, 2)
            A(stat[:, 2:4], stat[:, 0:2], ACT.Sqrt, bias=eps_t[:], scale=1.0 / D).then_inc(rms_x, 1)
            act.wait_ge(rows_t, 1)
            own.mark(A(vec[:, 0:2 * P - 6], ps[:, 4, 0:2 * P - 6], ACT.Copy))
            A(vec[:, V_CW:UC], ps[:, 4, V_CW:UC], ACT.Copy)
            A(vec[:, UC:V_END], ps[:, 5, 0:V_END - UC], ACT.Copy).then_inc(vec_ready, 1)
            own.wait()
            A(c_act[:], vec[:, V_C:V_C + KT], ACT.Silu).then_inc(c_ready, 1)
            act.wait_ge(angle_ready, 1)
            A(cos_t[:], red[:, 0], ACT.Sin).then_inc(table_ready, 1)
            A(sin_t[:], red[:, 1], ACT.Sin).then_inc(table_ready, 1)
            for b in range(8):
                act.wait_ge(xt_psum, b + 1)
                A(xn_t[:, 2 * b:2 * b + 2, :], ps[:, b, :].rearrange("p (k t) -> p k t", k=2), ACT.Copy)\
                    .then_inc(xt_copied, 1)
            for r in range(RING):
                split(r, r, total[r], None, 0)
            for q in range(4):
                act.wait_ge(h_ready, q + 1)
                A(ht[:, 4 * q:4 * q + 4, 0], h_f[:, 4 * q:4 * q + 4], ACT.Copy).then_inc(h_hi, 1)

            def features(u0, t0, p0, nu=8, g=None, per=8, scale=1.0, beside=None):
                for j in range(2, nu):
                    split_at(u0, j, t0, p0, nu, 4, g, per)
                    if beside is not None and j % 2 == 1:
                        beside()
                for f in range(3):
                    half_tile(t0 + f, f, scale)
                split_at(u0, nu, t0, p0, nu, 4, g, per)
                half_tile(t0 + 3, 3, scale)
                split_at(u0, nu + 1, t0, p0, nu, 4, g, per)
                if beside is not None:
                    beside()

            for name in ("misc", "qlat"):
                u0, t0, p0, _ = FIRST_OF[name]
                features(u0, t0, p0)
            act.wait_ge(tile_empty, 8)
            A(lat_sq[:], lat[:], ACT.Square).then_inc(lat_squared, 1)
            u0, t0, p0, _ = FIRST_OF["gq"]
            features(u0, t0, p0, scale=GLA_SCALE)
            act.wait_ge(lat_summed, 1)
            A(lat_r[:, 0], ps[:, 4, 0:S], ACT.Sqrt, bias=eps_t[:], scale=1.0 / KVR)
            A(lat_r[:, 1], ps[:, 4, S:2 * S], ACT.Sqrt, bias=eps_t[:], scale=1.0 / QR).then_inc(lat_rms, 1)
            for j in range(2, 8):
                split_at(u0 + 8, j, t0 + 4, p0 + 3)
                if j == 5:
                    act.wait_ge(lat_normed, 1)
                    A(lat_s[:, :, 0], lat[:], ACT.Copy).then_inc(lat_hi, 1)
            for f in range(4):
                half_tile(t0 + 4 + f, f, GLA_SCALE)
                if f >= 2:
                    split_at(u0 + 8, 6 + f, t0 + 4, p0 + 3)
            u0, t0, p0, _ = FIRST_OF["qup"]
            for g in range(3):
                features(u0 + 2 * g, t0 + 4 * g, p0, 2)
            u0, t0, p0, _ = FIRST_OF["kup"]
            for f in range(8):
                half_tile(t0 + f, f % 4)
                if f >= 6:
                    split_at(u0, f - 4, t0, p0, 2, 8)
            u0, t0, p0, _ = FIRST_OF["vup"]
            for n in range(4):
                half, t = n // 2, n % 2
                act.wait_ge(tile_ready, t0 + n + 1)
                A(v_mla[:, t, half * UC + S:(half + 1) * UC], ps[:, n, S:UC], ACT.Copy).then_inc(tile_half, 1)
                if n >= 2:
                    split_at(u0, n, t0, p0, 2, 4)

            def exps(h):
                act.wait_ge(max_ready, h + 1)
                k = h % 3
                for t in range(NT):
                    part = probs[:, k, t * P:t * P + (t + 1) * P]
                    ins = A(part, part, ACT.Exp, bias=soft[:, k, t:t + 1], scale=MLA_SCALE,
                            accum_out=soft[:, k, 2 + t:3 + t])
                    ins.then_inc(exp_done, 1)

            def copy_probs(h):
                act.wait_ge(pt_ready, h + 1)
                if h >= 2:
                    act.wait_ge(ctx_ready, h - 1)
                A(probs_t[:, h % 2], ps[:, 5, 0:3 * P], ACT.Copy).then_inc(pt_copied, 1)

            def context_hi(h):
                act.wait_ge(ctx_ready, h + 1)
                A(ot[:, h, 0], ps[:, 6, 0:S], ACT.Copy).then_inc(ctx_hi, 1)

            def mla_at(step):
                h, odd = step // 2, step % 2
                if odd:
                    if h < H:
                        exps(h)
                    if 0 <= h - 2 < H:
                        context_hi(h - 2)
                elif 0 <= h - 2 < H:
                    copy_probs(h - 2)

            def log_gate():
                act.wait_ge(gate_pre, 8)
                own.mark(A(dec[:], suf[:], ACT.Abs))
                own.wait()
                own.mark(A(dec[:], dec[:], ACT.Exp, scale=-1.0))
                own.wait()
                A(dec[:], dec[:], ACT.Ln, bias=ones[:, 0:1]).then_inc(gate_soft, 1)

            def decays(lv):
                h = 1 << (lv - 1)
                if lv > 1:
                    act.wait_ge(scan_ready, lv - 1)
                else:
                    act.wait_ge(decay_ready, 1)
                d0, d1 = halves(dec, h)
                A(d1, halves(pre, h)[1], ACT.Exp)
                A(d0, halves(suf, h)[0], ACT.Exp).then_inc(dec_ready, 1)

            def gla_copy(pr):
                act.wait_ge(og_psum, pr + 1)
                A(o_gla[:, 2 * pr:2 * pr + 2, :], ps[:, 6 + pr % 2, :].rearrange("p (k t) -> p k t", k=2), ACT.Copy)\
                    .then_inc(og_copied, 1)

            def gla_square(hd):
                act.wait_ge(og_copied, 2 * hd + 2)
                if hd:
                    act.wait_ge(og_summed, hd)
                A(o_sq[:], o_gla[:, 4 * hd:4 * hd + 4], ACT.Square).then_inc(og_squared, 1)

            steps = [0]

            def beside():
                step = steps[0]
                steps[0] += 1
                mla_at(step)
                if step == 21:
                    log_gate()
                if step % 2 == 1 and 1 <= (step - 21) // 2 <= LEVELS - 1:
                    decays((step - 21) // 2)
                n = step - 40
                if 1 <= n <= 8:
                    gla_copy(n - 1)
                    if n % 2 == 0:
                        gla_square(n // 2 - 1)
                if n == 10:
                    act.wait_ge(og_summed, GH)
                    A(o_r[:].rearrange("p (b h) t -> p b (h t)", b=2), ps[:, 4:6, :], ACT.Sqrt, bias=eps_t[:],
                      scale=1.0 / DV).then_inc(og_rms, 1)
                if n == 11:
                    A(og[:], og[:], ACT.Silu).then_inc(og_silu, 1)

            beside()
            u0, t0, p0, _ = FIRST_OF["gk"]
            for g in range(2):
                features(u0 + 8 * g, t0 + 4 * g, p0 + 3 * g, beside=beside)
            u0, t0, p0, _ = FIRST_OF["gv"]
            for g in range(4):
                for j in range(2, 8):
                    split_at(u0 + 8 * g, j, t0 + 2 * g, p0 + 3 * g, 8, 2)
                    if j % 2 == 1:
                        beside()
                for t in range(NT):
                    n = t0 + 2 * g + t
                    if t == 1:
                        for j in (8, 9):
                            split_at(u0 + 8 * g, j, t0 + 2 * g, p0 + 3 * g, 8, 2)
                    act.wait_ge(tile_ready, n + 1)
                    A(v_gla[:, t, g * UC + S:(g + 1) * UC], ps[:, n % 4, S:UC], ACT.Copy).then_inc(tile_half, 1)
                beside()
            u0, t0, p0, _ = FIRST_OF["og"]
            for g in range(4):
                features(u0 + 8 * g, t0 + 4 * g, p0 + 3 * g, beside=beside)
            u0, t0, p0, _ = FIRST_OF["ga"]
            for g in range(4):
                features(u0 + 8 * g, t0 + 4 * g, p0 + 3 * g, beside=beside)
                act.wait_ge(tile_empty, t0 + 4 * g + 4)
                tiles = gate_a[:, 4 * g:4 * g + 4]
                A(tiles, tiles, ACT.Sigmoid).then_inc(sig_done, 1)
            nc.scalar.preload_act_table(ACT.Sigmoid)
            with act.Fori(4, 8) as g:
                features(u0, t0 + 4 * g, p0 + 3 * g, g=g)
                act.wait_ge(tile_empty, t0 + 4 * g + 4)
                tiles = gate_b[:, bass.ds(4 * g - 16, 4)]
                A(tiles, tiles, ACT.Sigmoid).then_inc(sig_done, 1)
            act.wait_ge(og_gated, 4)
            act.wait_ge(tile_ready, FIRST_OF["ba"][1])
            for q in range(4):
                A(og_s[:, 4 * q:4 * q + 4, 0], o_gla[:, 4 * q:4 * q + 4], ACT.Copy).then_inc(og_hi, 1)
            u0, t0, p0, _ = FIRST_OF["ba"]
            with act.Fori(0, 2) as g:
                for n in range(2):
                    features(u0 + 4 * n, t0 + 8 * g + 4 * n, p0 + 2 * g + n, 4, g)
            u0, t0, p0, _ = FIRST_OF["bb"]
            with act.Fori(0, 4) as g:
                for j in range(2, 8):
                    split_at(u0, j, t0 + 4 * g, p0 + 3 * g, g=g)
                for f in range(6):
                    if f == 3:
                        split_at(u0, 8, t0 + 4 * g, p0 + 3 * g, g=g)
                    if f < 4:
                        half_tile(t0 + 4 * g + f, f)
                    if f == 3:
                        split_at(u0, 9, t0 + 4 * g, p0 + 3 * g, g=g)
                    if f >= 2:
                        act.wait_ge(merged_ready, 4 * g + f - 1)
                        A(merged[:, bass.ds(4 * g + f - 2, 1), 0], gate_b[:, bass.ds(4 * g + f - 2, 1)], ACT.Copy)\
                            .then_inc(merged_hi, 1)
            nc.scalar.preload_act_table(ACT.Sqrt)
            u0, t0, p0, _ = FIRST_OF["mix"]
            act.wait_ge(tile_empty, t0)
            act.wait_ge(merged_lo, KT)
            with act.Fori(0, 2) as g:
                for n in range(2):
                    tg, pg = t0 + 4 * g + 2 * n, p0 + 6 * g + 3 * n
                    for j in range(2, 8):
                        split_at(u0 + 8 * n, j, tg, pg, 8, 2, g, 16)
                    for t in range(NT):
                        bank = 2 * n + t
                        if t == 1:
                            for j in (8, 9):
                                split_at(u0 + 8 * n, j, tg, pg, 8, 2, g, 16)
                        act.wait_ge(tile_ready, t0 + 4 * g + bank + 1)
                        act.wait_ge(tile_half, t0 + 4 * g + bank)
                        A(junk_m[:, 0:UC], ps[:, bank, :], ACT.Square,
                          accum_out=stat[:, bass.ds(8 + 4 * t + 2 * g + n, 1)]).then_inc(tile_half, 1)
            act.wait_ge(sum_f, 1)
            A(stat[:, 18:20], stat[:, 16:18], ACT.Sqrt, bias=eps_t[:], scale=1.0 / D).then_inc(rms_y, 1)
            for t in range(NT):
                act.wait_ge(x1_ready, t + 1)
                if t:
                    act.wait_ge(ssq_1, t)
                A(junk_m[:], x1[:, t], ACT.Square, accum_out=stat[:, 4 + t:5 + t]).then_inc(ssq_1, 1)
            act.wait_ge(ssq_1, 2)
            A(stat[:, 6:8], stat[:, 4:6], ACT.Sqrt, bias=eps_t[:], scale=1.0 / D).then_inc(rms_1, 1)
            nc.scalar.preload_act_table(ACT.Gelu_apprx_tanh)
            for b in range(0, 8, 2):
                act.wait_ge(x1t_psum, b + 1)
                for k in range(2):
                    kt = 2 * b + k
                    ins = A(h2_f[:, kt], ps[:, b, k * S:(k + 1) * S], ACT.Identity, bias=mod[:, 3, kt:kt + 1],
                            scale=mod[:, 4, kt:kt + 1])
                own.mark(ins)
                act.wait_ge(h2_ready, b // 2 + 1)
                own.wait()
                A(h2t[:, 2 * b:2 * b + 4, 0], h2_f[:, 2 * b:2 * b + 4], ACT.Copy).then_inc(h2_hi, 1)
            u0, t0, p0, _ = FIRST_OF["ffn"]
            with act.Fori(0, 11) as g:
                for part in range(2):
                    tg, pg = t0 + 8 * g + 4 * part, p0 + 6 * g + 3 * part
                    for j in range(2, 8):
                        split_at(u0 + 8 * part, j, tg, pg, 8, 4, g, 16)
                    for f in range(6):
                        if f == 3:
                            split_at(u0 + 8 * part, 8, tg, pg, 8, 4, g, 16)
                        if f < 4:
                            half_tile(tg + f, f)
                        if f == 3:
                            split_at(u0 + 8 * part, 9, tg, pg, 8, 4, g, 16)
                        if 0 <= f - 1 < 4:
                            n = f - 1
                            ft = part * (FF // P) + 4 * g + n
                            act.wait_ge(tile_empty, t0 + 8 * g + 4 * part + n + 1)
                            dst = conv_a[:, n] if part == 0 else conv_v[:, n % 2]
                            if part == 0 and n == 0:
                                act.wait_ge(hid_ready, 4 * g + 1)
                            if part == 1 and n >= 2:
                                act.wait_ge(hid_ready, 4 * g + n)
                            A(dst, conv_in[:, n, 2:S + 2], ACT.Identity,
                              bias=vec[:, bass.ds(V_CB + ft, 1)], scale=vec[:, bass.ds(V_CW + 2 * (2 * FF // P) + ft, 1)])\
                                .then_inc(conv_first, 1)
                        if 0 <= f - 2 < 4:
                            n = f - 2
                            if part == 0:
                                act.wait_ge(conv_done, 8 * g + n + 2)
                                A(conv_a[:, n], conv_a[:, n], ACT.Gelu_apprx_tanh).then_inc(gelu_done, 1)
                            else:
                                act.wait_ge(hid_ready, 4 * g + n + 2)
                                A(hid[:, bass.ds(4 * g + n, 1), 0].rearrange("p o t -> p (o t)"), hid_f[:, n % 2],
                                  ACT.Copy).then_inc(hid_hi, 1)
            nc.scalar.preload_act_table(ACT.Sqrt)
            u0, t0, p0, _ = FIRST_OF["down"]
            for g in range(2):
                for n in range(2):
                    first, tg, pg = u0 + 44 * g + 22 * n, t0 + 4 * g + 2 * n, p0 + 20 * g + 10 * n
                    for j in range(2, 22):
                        split_at(first, j, tg, pg, 22, 2)
                    for t in range(NT):
                        bank = 2 * n + t
                        if t == 1:
                            for j in (22, 23):
                                split_at(first, j, tg, pg, 22, 2)
                        act.wait_ge(tile_ready, t0 + 4 * g + bank + 1)
                        act.wait_ge(tile_half, t0 + 4 * g + bank)
                        A(junk_f[:], ps[:, bank, :], ACT.Square,
                          accum_out=stat[:, 8 + 4 * t + 2 * g + n:9 + 4 * t + 2 * g + n]).then_inc(tile_half, 1)
            act.wait_ge(sum_f, 2)
            A(stat[:, 22:24], stat[:, 20:22], ACT.Sqrt, bias=eps_t[:], scale=1.0 / D).then_inc(rms_f, 1)

        @block.vector
        def _(dve):
            V = nc.vector
            own = Steps(dve, dve_step)

            def chain(ins):
                own.mark(ins)
                own.wait()

            def split(u, slot):
                dve.wait_ge(hi_done, u + 1)
                V.tensor_tensor(w_lo[:, slot], raw[:, slot], w_hi[:, slot].bitcast(F32), ALU.subtract)\
                    .then_inc(lo_done, 1)

            def clear_acc(n):
                if 1 <= n <= 4:
                    dve.wait_ge(mod_psum, n)
                if n == 5:
                    dve.wait_ge(gate_row, 1)
                V.memset(acc[:], 0.0).then_inc(acc_zero, 1)
                dve.wait_ge(acc_zero, n + 1)

            def ada_unit(a, slot, kt, half, loaded, guard=True):
                dve.wait_ge(ada_loaded[slot], loaded)
                if guard:
                    dve.wait_ge(ada_used, a - 1)
                part = acc[:, half * AC:(half + 1) * AC]
                V.scalar_tensor_tensor(part, ada[:, slot], c_act[:, bass.ds(kt, 1)], part, ALU.mult, ALU.add)\
                    .then_inc(ada_used, 1)

            def split_at(u0, j, g=None, per=8):
                u = u0 + 2 + j
                if u < UNITS:
                    split(u if g is None else u + per * g, u % RING)

            def ada_at(a, n, kt, g=None, per=8):
                if a is None:
                    return
                av = a + n if g is None else a + n + (per // 2) * g
                loaded = 16 * ((a + n) // RING + 1)
                if g is not None:
                    loaded = loaded + 16 * (per // 2 // RING) * g
                ada_unit(av, (a + n) % RING, kt + n // 2, n % 2, loaded)

            def inner(u0, nu, a=None, kt=None, g=None, per=8, beside=None):
                for j in range(2, nu):
                    split_at(u0, j, g, per)
                    if j % 2 == 1:
                        ada_at(a, j // 2 - 1, kt, g, per)
                        if beside is not None:
                            beside()

            def features(u0, t0, nu, dst, a=None, kt=None, g=None, per=8, scale=None, beside=None):
                inner(u0, nu, a, kt, g, per, beside)
                for f in range(4):
                    if f == 3:
                        split_at(u0, nu, g, per)
                    sum_tile(t0 + f, f, dst(f), scale)
                split_at(u0, nu + 1, g, per)
                ada_at(a, nu // 2 - 1, kt, g, per)
                if beside is not None:
                    beside()

            def sum_tile(t, bank, dst, scale=None):
                dve.wait_ge(tile_half, t + 1)
                if scale is None:
                    ins = V.tensor_tensor(dst, ps[:, bank, 0:S], cross[:, bank % 2], ALU.add)
                else:
                    ins = V.scalar_tensor_tensor(dst, ps[:, bank, 0:S], scale, cross[:, bank % 2], ALU.mult, ALU.add)
                ins.then_inc(tile_empty, 1)

            dve.wait_ge(const_loaded, 3 * 16)
            chain(V.tensor_copy(pos_f[:], pos_i[:]))
            chain(V.tensor_scalar(ang[:], pos_f[:], inv_freq[:, 0:1], None, ALU.mult))
            round_c = 12582912.0
            V.tensor_scalar(turn[:, 0], ang[:], float(0.5 / np.pi), 0.25, ALU.mult, ALU.add)
            chain(V.tensor_scalar(turn[:, 1], ang[:], float(0.5 / np.pi), None, ALU.mult))
            chain(V.tensor_scalar(turn[:], turn[:], round_c, None, ALU.add))
            chain(V.tensor_scalar(turn[:], turn[:], -round_c, None, ALU.add))
            for n in range(2):
                own.mark(V.scalar_tensor_tensor(red[:, n], turn[:, n], -6.28125, ang[:], ALU.mult, ALU.add))
            own.wait()
            for part in (-0.0019350051879882812, -3.019916050561733e-07):
                chain(V.scalar_tensor_tensor(red[:], turn[:], part, red[:], ALU.mult, ALU.add))
            chain(V.tensor_scalar(red[:, 0], red[:, 0], float(np.pi / 2), None, ALU.add))
            V.tensor_scalar(red[:], red[:], 3.1415925, -3.1415925, ALU.min, ALU.max).then_inc(angle_ready, 1)

            V.tensor_copy(masks[:], masks_i[:])

            dve.wait_ge(rms_x, 1)
            chain(V.reciprocal(stat[:, 2:4], stat[:, 2:4]))
            for t in range(NT):
                V.tensor_scalar(xn_tok[:, t], x_tok[:, t], stat[:, 2 + t:3 + t], None, ALU.mult).then_inc(norm_x, 1)

            dve.wait_ge(c_ready, 1)

            def take_mod(n, dst, base, bank=4):
                dve.wait_ge(mod_psum, n + 1)
                return V.tensor_tensor(mod[:, dst], ps[:, bank, 0:KT], vec[:, base:base + KT], ALU.add)

            def one_plus_times(dst, gain):
                return V.scalar_tensor_tensor(mod[:, dst], mod[:, dst], 1.0, vec[:, gain:gain + KT], ALU.add, ALU.mult)

            for n in range(2):
                clear_acc(n)
                if n == 1:
                    take_mod(0, 0, V_BADA).then_inc(mod_ready, 1)
                a0 = ADA_BLOCK * n
                for r in range(RING):
                    ada_unit(a0 + r, r, r // 2, r % 2, 16 * (a0 // RING + 1), guard=r >= 2)
                with dve.Fori(1, KT // 2) as i:
                    for r in range(RING):
                        ada_unit(a0 + 4 * i + r, r, 2 * i + r // 2, r % 2, 16 * (a0 // RING) + 16 * i + 16)
            for r in range(RING):
                split(r, r)
            chain(take_mod(1, 1, V_BADA + KT))
            one_plus_times(1, V_GPRE).then_inc(mod_ready, 1)
            dve.wait_ge(mod_ready, 2)
            dve.wait_ge(xt_copied, 8)
            for q in range(4):
                for i in range(4):
                    kt = 4 * q + i
                    ins = V.tensor_scalar(h_f[:, kt], xn_t[:, kt], mod[:, 1, kt:kt + 1], mod[:, 0, kt:kt + 1],
                                          ALU.mult, ALU.add)
                ins.then_inc(h_ready, 1)
            for q in range(4):
                dve.wait_ge(h_hi, q + 1)
                ks = slice(4 * q, 4 * q + 4)
                V.tensor_tensor(ht[:, ks, 1], h_f[:, ks], ht[:, ks, 0].bitcast(F32), ALU.subtract).then_inc(h_lo, 1)
            clear_acc(2)
            for name, kt in (("misc", 0), ("qlat", 2)):
                u0, t0, _, a0 = FIRST_OF[name]
                dsts = ([lat[:, 0], lat[:, 1], k_rope_in[:], lr_t[:]] if name == "misc"
                        else [lat[:, 2 + f] for f in range(4)])
                features(u0, t0, 8, lambda f: dsts[f], a0, kt)

            def latents_at(step):
                if step == 0:
                    dve.wait_ge(lat_rms, 1)
                    chain(V.reciprocal(lat_r[:], lat_r[:]))
                if step == 1:
                    for i in range(6):
                        gain = V_GKV + i if i < 2 else V_GQ + i - 2
                        ins = V.scalar_tensor_tensor(lat[:, i], lat[:, i], vec[:, gain:gain + 1],
                                                     lat_r[:, 0 if i < 2 else 1], ALU.mult, ALU.mult)
                    ins.then_inc(lat_normed, 1)
                if step == 3:
                    dve.wait_ge(lat_hi, 1)
                    V.tensor_tensor(lat_s[:, :, 1], lat[:], lat_s[:, :, 0].bitcast(F32), ALU.subtract)\
                        .then_inc(lat_lo, 1)

            u0, t0, _, a0 = FIRST_OF["gq"]
            features(u0, t0, 8, lambda f: q_gla[:, f], a0, 4, scale=GLA_SCALE)
            latents_at(0)
            latent_steps = iter((1, 2, 3, 4))
            features(u0 + 8, t0 + 4, 8, lambda f: q_gla[:, 4 + f], a0 + 4, 6, scale=GLA_SCALE,
                     beside=lambda: latents_at(next(latent_steps)))
            u0, t0, _, _ = FIRST_OF["qup"]
            for g in range(3):
                features(u0 + 2 * g, t0 + 4 * g, 2, lambda f: q_nope[:, 4 * g + f] if g < 2 else q_rope_in[:, f])
            u0, t0, _, _ = FIRST_OF["kup"]
            for n in range(8):
                if n == 7:
                    split_at(u0, 2)
                sum_tile(t0 + n, n % 4, k_nope[:, n])
            split_at(u0, 3)
            u0, t0, _, _ = FIRST_OF["vup"]
            for n in range(4):
                half, t = n // 2, n % 2
                dve.wait_ge(tile_half, t0 + n + 1)
                V.tensor_copy(v_mla[:, t, half * UC:half * UC + S], ps[:, n, 0:S]).then_inc(tile_empty, 1)
                if n >= 2:
                    split_at(u0, n)
            dve.wait_ge(table_ready, 2)
            dve.wait_ge(rot_ready, 1)
            for i in range(4):
                V.tensor_tensor(rope_tmp[:, i % 2], ps[:, 4 + i // 2, (i % 2) * S:(i % 2 + 1) * S], sin_t[:], ALU.mult)
                chain(V.tensor_tensor(q_rope[:, i], q_rope_in[:, i], cos_t[:], ALU.mult))
                V.tensor_tensor(q_rope[:, i], q_rope[:, i], rope_tmp[:, i % 2], ALU.add).then_inc(rope_done, 1)
            V.tensor_tensor(rope_tmp[:, 0], ps[:, 6, 0:S], sin_t[:], ALU.mult)
            chain(V.tensor_tensor(k_rope[:], k_rope_in[:], cos_t[:], ALU.mult))
            V.tensor_tensor(k_rope[:], k_rope[:], rope_tmp[:, 0], ALU.add).then_inc(rope_done, 1)

            def mask_and_max(h):
                dve.wait_ge(scores_ready, h + 1)
                if h >= 3:
                    dve.wait_ge(pt_ready, h - 2)
                k = h % 3

                def diagonal(v):
                    return v.rearrange("p (a b) -> p a b", b=2 * P)[:, :, 0:P]

                V.tensor_copy(probs[:, k, P:2 * P], ps[:, 4, P:2 * P])
                bias = causal[:].rearrange("p (o n) -> p o n", o=1).to_broadcast([P, 2, P])
                chain(V.tensor_tensor(diagonal(probs[:, k]), diagonal(ps[:, 4]), bias, ALU.add))
                V.tensor_reduce(soft[:, k, 0:1], probs[:, k, 0:P], AX, ALU.max)
                chain(V.tensor_reduce(soft[:, k, 1:2], probs[:, k, P:3 * P], AX, ALU.max))
                V.tensor_scalar(soft[:, k, 0:2], soft[:, k, 0:2], -MLA_SCALE, None, ALU.mult).then_inc(max_ready, 1)

            def normalise(h):
                dve.wait_ge(exp_done, 2 * h + 2)
                k = h % 3
                chain(V.reciprocal(soft[:, k, 4:6], soft[:, k, 2:4]))
                V.tensor_scalar(probs[:, k, 0:P], probs[:, k, 0:P], soft[:, k, 4:5], None, ALU.mult)
                V.tensor_scalar(probs[:, k, P:3 * P], probs[:, k, P:3 * P], soft[:, k, 5:6], None, ALU.mult)\
                    .then_inc(probs_ready, 1)

            def context_lo(h):
                dve.wait_ge(ctx_hi, h + 1)
                V.tensor_tensor(ot[:, h, 1], ps[:, 6, 0:S], ot[:, h, 0].bitcast(F32), ALU.subtract).then_inc(ctx_lo, 1)

            def mla_at(step):
                h, odd = step // 2, step % 2
                if odd:
                    if h < H:
                        mask_and_max(h)
                    if 0 <= h - 2 < H:
                        context_lo(h - 2)
                elif 0 <= h - 1 < H:
                    normalise(h - 1)

            def gate_bias(n):
                dve.wait_ge(gate_psum, n + 1)
                for i in range(4):
                    ft = 4 * n + i
                    V.tensor_scalar(suf[:, ft], ps[:, 6 + i // 2, (i % 2) * S:(i % 2 + 1) * S],
                                    vec[:, V_BGLA + ft:V_BGLA + ft + 1], None, ALU.add).then_inc(gate_pre, 1)

            def log_decay():
                dve.wait_ge(gate_soft, 1)
                chain(V.scalar_tensor_tensor(pre[:], suf[:], 0.0, dec[:], ALU.min, ALU.subtract))
                V.tensor_scalar(pre[:], pre[:], 1.0 / TAU, None, ALU.mult)
                V.memset(attn0[:], 0.0)
                V.memset(attn1[:], 0.0)
                V.memset(suf[:], 0.0).then_inc(decay_ready, 1)
                dve.wait_ge(decay_ready, 1)

            def products(lv):
                h = 1 << (lv - 1)
                dve.wait_ge(dec_ready, lv)
                dve.wait_ge(level_ready, lv)
                V.tensor_tensor(halves(qk, h)[1], halves(q_gla, h)[1], halves(dec, h)[1], ALU.mult)
                V.tensor_tensor(halves(qk, h)[0], halves(k_gla, h)[0], halves(dec, h)[0], ALU.mult).then_inc(qk_ready, 1)

            def scan(lv):
                h = 1 << (lv - 1)
                p0, p1 = halves(pre, h)
                s0_, _ = halves(suf, h)
                chain(V.tensor_tensor(s0_, s0_, spread(p1[:, :, h - 1:h], s0_), ALU.add))
                V.tensor_tensor(p1, p1, spread(p0[:, :, h - 1:h], p1), ALU.add).then_inc(scan_ready, 1)
                dve.wait_ge(scan_ready, lv)

            def select(lv):
                dve.wait_ge(level_ready, lv + 1)

                def by_head(b, n=P):
                    return ps[:, b, 0:GH * n].rearrange("p (h n) -> p h n", h=GH)

                if lv == 0:
                    m = masks[:, 0:1, :].to_broadcast([P, GH, P])
                    V.copy_predicated(attn0[:, :, 0:P], m, by_head(6))
                    V.copy_predicated(attn1[:], m, by_head(7)).then_inc(level_taken, 1)
                elif lv < LEVELS - 1:
                    h = 1 << (lv - 1)

                    def second(v):
                        return v.rearrange("p (b s h) -> p b s h", s=2, h=h)[:, :, 1]

                    m = second(masks[:, lv])
                    for b, dst in ((6, attn0[:, :, 0:P]), (7, attn1)):
                        for hd in range(GH):
                            src = ps[:, b, hd * P // 2:(hd + 1) * P // 2].rearrange("p (b h) -> p b h", h=h)
                            ins = V.copy_predicated(second(dst[:, hd]), m, src)
                    ins.then_inc(level_taken, 1)
                else:
                    V.tensor_copy(attn0[:, :, P:S], by_head(6)).then_inc(level_taken, 1)
                dve.wait_ge(level_taken, lv + 1)

            def gla_norm(n):
                if n == 0:
                    dve.wait_ge(og_rms, 1)
                    chain(V.reciprocal(o_r[:], o_r[:]))
                if n in (1, 2):
                    for hd in (2 * n - 2, 2 * n - 1):
                        part = o_gla[:, 4 * hd:4 * hd + 4]
                        own.mark(V.tensor_tensor(part, part, o_r[:, hd:hd + 1].to_broadcast([P, 4, S]), ALU.mult))
                if n in (3, 4):
                    own.wait()
                    dve.wait_ge(og_silu, 1)
                    for i in (2 * n - 6, 2 * n - 5):
                        part, gate = (b[:].rearrange("p (h i) t -> p h i t", i=4)[:, :, i] for b in (o_gla, og))
                        V.scalar_tensor_tensor(part, part, vec[:, V_GOUT + i:V_GOUT + i + 1], gate, ALU.mult, ALU.mult)\
                            .then_inc(og_gated, 1)

            steps = [0]

            def beside():
                step = steps[0]
                steps[0] += 1
                mla_at(step)
                if step in (20, 21):
                    gate_bias(step - 20)
                if step == 22:
                    log_decay()
                if step % 2 == 0 and 1 <= (step - 22) // 2 <= LEVELS - 1:
                    lv = (step - 22) // 2
                    products(lv)
                    if lv < LEVELS - 1:
                        scan(lv)
                if step % 2 == 1 and 0 <= (step - 25) // 2 <= LEVELS - 1:
                    select((step - 25) // 2)
                if 51 <= step <= 55:
                    gla_norm(step - 51)

            def column(buf, n):
                return buf[:, bass.ds(n, 1)].rearrange("p o t -> p (o t)")

            beside()
            u0, t0, _, a0 = FIRST_OF["gk"]
            for g in range(2):
                features(u0 + 8 * g, t0 + 4 * g, 8, lambda f: k_gla[:, 4 * g + f], a0 + 4 * g, 8 + 2 * g, beside=beside)
            u0, t0, _, a0 = FIRST_OF["gv"]
            for g in range(4):
                if g == 2:
                    clear_acc(3)
                    take_mod(2, 3, V_BADA + 3 * KT).then_inc(mod_ready, 1)
                kt = 12 + 2 * g if g < 2 else 2 * g - 4
                inner(u0 + 8 * g, 8, a0 + 4 * g, kt, beside=beside)
                for t in range(NT):
                    n = t0 + 2 * g + t
                    if t == 1:
                        for j in (8, 9):
                            split_at(u0 + 8 * g, j)
                    dve.wait_ge(tile_half, n + 1)
                    V.tensor_copy(v_gla[:, t, g * UC:g * UC + S], ps[:, n % 4, 0:S]).then_inc(tile_empty, 1)
                ada_at(a0 + 4 * g, 3, kt)
                beside()
            u0, t0, _, a0 = FIRST_OF["og"]
            for g in range(4):
                features(u0 + 8 * g, t0 + 4 * g, 8, lambda f: og[:, 4 * g + f], a0 + 4 * g, 4 + 2 * g, beside=beside)
            u0, t0, _, a0 = FIRST_OF["ga"]
            for g in range(4):
                if g == 2:
                    clear_acc(4)
                    chain(take_mod(3, 4, V_BADA + 4 * KT, 6))
                    one_plus_times(4, V_GFFN).then_inc(mod_ready, 1)
                kt = 12 + 2 * g if g < 2 else 2 * g - 4
                features(u0 + 8 * g, t0 + 4 * g, 8, lambda f: gate_a[:, 4 * g + f], a0 + 4 * g, kt, beside=beside)
            with dve.Fori(4, 8) as g:
                features(u0, t0 + 4 * g, 8, lambda f: column(gate_b, 4 * g + f - 16), a0, 2 * g - 4, g)
            for q in range(4):
                dve.wait_ge(og_hi, q + 1)
                ks = slice(4 * q, 4 * q + 4)
                V.tensor_tensor(og_s[:, ks, 1], o_gla[:, ks], og_s[:, ks, 0].bitcast(F32), ALU.subtract)\
                    .then_inc(og_lo, 1)
            u0, t0, _, a0 = FIRST_OF["ba"]
            dve.wait_ge(sig_done, 8)
            n0 = own.n
            with dve.Fori(0, 2) as g:
                own.n = n0 + 8 * g
                for n in range(2):
                    a, kt = a0 + 2 * n, 12 + 2 * g + n
                    inner(u0 + 4 * n, 4, a, kt, g)
                    for f in range(4):
                        if f == 3:
                            split_at(u0 + 4 * n, 4, g)
                        sum_tile(t0 + 8 * g + 4 * n + f, f, ytmp[:, f % 2])
                        dve.wait_ge(tile_empty, t0 + 8 * g + 4 * n + f + 1)
                        dst = column(gate_a, 8 * g + 4 * n + f)
                        own.mark(V.tensor_tensor(dst, dst, ytmp[:, f % 2], ALU.mult))
                    split_at(u0 + 4 * n, 5, g)
                    ada_at(a, 1, kt, g)
            own.n = n0 + 16
            own.wait()

            def gate_gain(n, dst, gpost):
                dve.wait_ge(gate_row, n + 1)
                for b in range(4):
                    cols = slice(b * UC, (b + 1) * UC)
                    ins = V.tensor_tensor(dst[:, cols], ps[:, 4 + b, :], gpost[:, cols], ALU.mult)
                ins.then_inc(gg_ready, 1)

            dve.wait_ge(post_loaded, 16 * 5)
            clear_acc(5)
            gate_gain(0, gg_m, gpost_m)
            u0, t0, _, a0 = FIRST_OF["bb"]
            n0 = own.n
            with dve.Fori(0, 4) as g:
                own.n = n0 + 4 * g
                inner(u0, 8, a0, 2 * g, g)
                for f in range(7):
                    if f == 3:
                        split_at(u0, 8, g)
                    if f < 4:
                        sum_tile(t0 + 4 * g + f, f, ytmp[:, f % 2])
                        dve.wait_ge(tile_empty, t0 + 4 * g + f + 1)
                        y, gb = ytmp[:, f % 2], column(gate_b, 4 * g + f)
                        chain(V.tensor_tensor(y, y, gb, ALU.mult))
                        V.tensor_tensor(gb, y, column(gate_a, 4 * g + f), ALU.add).then_inc(merged_ready, 1)
                    if f == 3:
                        split_at(u0, 9, g)
                        ada_at(a0, 3, 2 * g, g)
                    if f >= 3:
                        kt = 4 * g + f - 3
                        dve.wait_ge(merged_hi, kt + 1)
                        V.tensor_tensor(column(merged[:, :, 1], kt), column(gate_b, kt),
                                        column(merged[:, :, 0], kt).bitcast(F32), ALU.subtract).then_inc(merged_lo, 1)
            own.n = n0 + 16
            u0, t0, _, a0 = FIRST_OF["mix"]
            with dve.Fori(0, 2) as g:
                for n in range(2):
                    a, kt = a0 + 4 * n, 8 + 4 * g + 2 * n
                    inner(u0 + 8 * n, 8, a, kt, g, 16)
                    for t in range(NT):
                        bank = 2 * n + t
                        if t == 1:
                            for j in (8, 9):
                                split_at(u0 + 8 * n, j, g, 16)
                            ada_at(a, 3, kt, g, 16)
                        dve.wait_ge(tile_half, t0 + 4 * g + bank + 1)
                        cols = bass.ds(2 * UC * g + UC * n, UC)
                        V.tensor_tensor(x1[:, t, cols], ps[:, bank, :], gg_m[:, cols], ALU.mult).then_inc(tile_empty, 1)
            V.tensor_reduce(stat[:, 16:18], stat[:, 8:16].rearrange("p (t n) -> p t n", t=2), AX, ALU.add)\
                .then_inc(sum_f, 1)
            dve.wait_ge(rms_y, 1)
            chain(V.reciprocal(stat[:, 18:20], stat[:, 18:20]))
            dve.wait_ge(x_again_loaded, 16)
            dve.wait_ge(tile_empty, FIRST_OF["ffn"][1])
            for t in range(NT):
                V.scalar_tensor_tensor(x1[:, t], x1[:, t], stat[:, 18 + t:19 + t], x_again[:, t], ALU.mult, ALU.add)\
                    .then_inc(x1_ready, 1)
            dve.wait_ge(x1_ready, 2)
            dve.wait_ge(rms_1, 1)
            chain(V.reciprocal(stat[:, 6:8], stat[:, 6:8]))
            for t in range(NT):
                V.tensor_scalar(xn1[:, t], x1[:, t], stat[:, 6 + t:7 + t], None, ALU.mult).then_inc(norm_1, 1)
            for b in range(1, 8, 2):
                dve.wait_ge(x1t_psum, b + 1)
                for k in range(2):
                    kt = 2 * b + k
                    ins = V.tensor_scalar(h2_f[:, kt], ps[:, b, k * S:(k + 1) * S], mod[:, 4, kt:kt + 1],
                                          mod[:, 3, kt:kt + 1], ALU.mult, ALU.add)
                ins.then_inc(h2_ready, 1)
            for q in range(4):
                dve.wait_ge(h2_hi, q + 1)
                ks = slice(4 * q, 4 * q + 4)
                V.tensor_tensor(h2t[:, ks, 1], h2_f[:, ks], h2t[:, ks, 0].bitcast(F32), ALU.subtract).then_inc(h2_lo, 1)
            dve.wait_ge(ada_used, 6 * ADA_BLOCK)
            chain(V.memset(conv_in[:, :, 0:2], 0.0))
            for n, s in enumerate((conv_done, hid_ready, hid_lo)):
                V.memset(hid_f[:, 0, n:n + 1], 0.0).then_inc(s, 1)
            dve.wait_ge(hid_lo, 1)
            u0, t0, _, _ = FIRST_OF["ffn"]
            n0 = own.n
            with dve.Fori(0, FF // UC) as g:
                own.n = n0 + 8 * g
                for part in range(2):
                    inner(u0 + 8 * part, 8, g=g, per=16)
                    for f in range(7 if part else 5):
                        if f == 3:
                            split_at(u0 + 8 * part, 8, g, 16)
                        if f < 4:
                            if part or f == 0:
                                dve.wait_ge(conv_done, 8 * g + (f + 2 if part else 1))
                            sum_tile(t0 + 8 * g + 4 * part + f, f, conv_in[:, f, 2:S + 2])
                        if f == 3:
                            split_at(u0 + 8 * part, 9, g, 16)
                        if 0 <= f - 1 < 4:
                            n = f - 1
                            ft = part * (FF // P) + 4 * g + n
                            dve.wait_ge(conv_first, 8 * g + 4 * part + n + 1)
                            dst = conv_a[:, n] if part == 0 else conv_v[:, n % 2]
                            chain(V.scalar_tensor_tensor(dst, conv_in[:, n, 1:S + 1],
                                                         vec[:, bass.ds(V_CW + 2 * FF // P + ft, 1)], dst,
                                                         ALU.mult, ALU.add))
                            V.scalar_tensor_tensor(dst, conv_in[:, n, 0:S], vec[:, bass.ds(V_CW + ft, 1)], dst,
                                                   ALU.mult, ALU.add).then_inc(conv_done, 1)
                        if part and 0 <= f - 2 < 4:
                            n = f - 2
                            dve.wait_ge(gelu_done, 4 * g + n + 1)
                            dve.wait_ge(hid_lo, 4 * g + max(n, 1))
                            dve.wait_ge(conv_done, 8 * g + 4 + n + 2)
                            V.tensor_tensor(hid_f[:, n % 2], conv_a[:, n], conv_v[:, n % 2], ALU.mult)\
                                .then_inc(hid_ready, 1)
                        if part and 0 <= f - 3 < 4:
                            n = f - 3
                            dve.wait_ge(hid_hi, 4 * g + n + 1)
                            V.tensor_tensor(column(hid[:, :, 1], 4 * g + n), hid_f[:, n % 2],
                                            column(hid[:, :, 0], 4 * g + n).bitcast(F32), ALU.subtract)\
                                .then_inc(hid_lo, 1)
            own.n = n0 + 8 * (FF // UC)
            u0, t0, _, _ = FIRST_OF["down"]
            for g in range(2):
                for n in range(2):
                    first = u0 + 44 * g + 22 * n
                    for j in range(2, 22):
                        split_at(first, j)
                        if g == 0 and n == 0 and j == 5:
                            dve.wait_ge(post_f_loaded, 16)
                            gate_gain(1, gg_f, gpost_f)
                    for t in range(NT):
                        bank = 2 * n + t
                        if t == 1:
                            for j in (22, 23):
                                split_at(first, j)
                        dve.wait_ge(tile_half, t0 + 4 * g + bank + 1)
                        cols = slice((2 * g + n) * UC, (2 * g + n + 1) * UC)
                        V.tensor_tensor(f_tok[:, t, cols], ps[:, bank, :], gg_f[:, cols], ALU.mult)\
                            .then_inc(tile_empty, 1)
            V.tensor_reduce(stat[:, 20:22], stat[:, 8:16].rearrange("p (t n) -> p t n", t=2), AX, ALU.add)\
                .then_inc(sum_f, 1)
            dve.wait_ge(rms_f, 1)
            chain(V.reciprocal(stat[:, 22:24], stat[:, 22:24]))
            dve.wait_ge(tile_empty, FIRST_OF["down"][1] + 8)
            for n in range(4):
                t, c0 = n // 2, (n % 2) * (D // 2)
                part = f_tok[:, t, c0:c0 + D // 2]
                V.scalar_tensor_tensor(part, part, stat[:, 22 + t:23 + t], x1[:, t, c0:c0 + D // 2], ALU.mult, ALU.add)\
                    .then_inc(out_ready, 1)

        @block.gpsimd
        def _(pool):
            nc.gpsimd.memset(eps_t[:], EPS).then_inc(setup_done, 1)
            nc.gpsimd.memset(ones[:], 1.0).then_inc(setup_done, 1)


def kernel(**inputs):
    import concourse.bacc as bacc
    from concourse.bass_utils import run_bass_kernel_spmd

    names = ["x", "c", "positions", "w_ada", "b_ada", "g_pre_mix", "w_in", "g_q_lat", "w_q_up", "g_kv_lat",
             "w_kv_up", "w_gla_gate_up", "b_gla_gate", "g_gla_out", "w_branch_a", "w_branch_b", "w_mix_out",
             "g_post_mix", "g_pre_ffn", "w_ffn_up", "conv_w", "conv_b", "w_ffn_down", "g_post_ffn"]
    nc = bacc.Bacc("TRN2", target_bir_lowering=False, num_devices=1, dynamic_dma_scratch_size=1024)
    arrays = {f"in_{n}": np.ascontiguousarray(inputs[n]) for n in names}
    arrays["in_constants"] = constants()
    arrays["in_masks"] = level_masks()
    args = []
    for n, a in arrays.items():
        t = nc.dram_tensor(n, a.shape, mybir.dt.from_np(a.dtype), kind="ExternalInput").ap()
        args.append(t[0] if n[3:].startswith("w_") else t)
    out = nc.dram_tensor("out", (1, S, D), F32, kind="ExternalOutput").ap()
    build(nc, args, out)
    r = run_bass_kernel_spmd(nc, [arrays], core_ids=[0])
    return r.results[0]["out"]
```

```python
from contextlib import ExitStack

import numpy as np

import concourse.bass as bass
from concourse import mybir

P = 128
F32 = mybir.dt.float32
F32R = mybir.dt.float32r
I32 = mybir.dt.int32
U8 = mybir.dt.uint8
ALU = mybir.AluOpType
ACT = mybir.ActivationFunctionType
AX = mybir.AxisListType.X

D = 2048
S = 256
NT = S // P
H = 8
NOPE, ROPE, VD = 128, 64, 128
QR, KVR = 512, 256
GH = 4
DK, DV = D // 2 // GH, D // GH
GR = 16
TAU = 16.0
FF = 5632
KT = D // P
EPS = 1e-6
THETA = 10000.0

C_Q = 0
C_KV = C_Q + QR
C_KR = C_KV + KVR
C_GQ = C_KR + ROPE
C_GK = C_GQ + GH * DK
C_GV = C_GK + GH * DK
C_LR = C_GV + GH * DV
C_OG = C_LR + GR
C_GA = C_OG + GH * DV
C_GB = C_GA + D

UC = 512
AC = 1024
RING = 4
ADA_BLOCK = D // P * (D // AC)
MLA_SCALE = float(NOPE + ROPE) ** -0.5
GLA_SCALE = float(DK) ** -0.5
LEVELS = 9

V_BADA, V_C, V_GPRE = 0, 96, 112
V_GQ, V_GKV, V_BGLA, V_GOUT, V_GFFN, V_CB = 128, 132, 134, 142, 146, 162
V_CW = 256
V_END = V_CW + 3 * 2 * FF // P

GROUPS = ([("misc", 8, 4), ("qlat", 8, 4)] + [("gq", 8, 4)] * 2
          + [("qup", 2, 4)] * 3 + [("kup", 2, 8)] + [("vup", 2, 4)]
          + [("gk", 8, 4)] * 2 + [("gv", 8, 2)] * 4 + [("og", 8, 4)] * 4
          + [("ga", 8, 4)] * 4 + [("gb", 8, 4)] * 4 + [("ba", 4, 4)] * 4 + [("bb", 8, 4)] * 4
          + [("mix", 8, 2)] * 4 + [("ffn", 8, 4)] * 22 + [("down", 22, 2)] * 4)


def starts(name):
    u = t = p = 0
    a = 2 * ADA_BLOCK
    for kind, nu, nt in GROUPS:
        if kind == name:
            return u, t, p, a
        u, t, p = u + nu, t + nt, p + nu // 2 - 1
        if nu in (4, 8) and a < 6 * ADA_BLOCK:
            a += nu // 2
    return u, t, p, a


UNITS = starts("end")[0]
FIRST_OF = {g[0]: starts(g[0]) for g in GROUPS}


def level_masks():
    j, i = np.arange(P)[:, None], np.arange(P)[None, :]
    out = [i == j]
    for lv in range(1, LEVELS - 1):
        h = 1 << (lv - 1)
        out.append((i // (2 * h) == j // (2 * h)) & (j % (2 * h) < h) & (i % (2 * h) >= h))
    return np.concatenate(out, axis=1).astype(np.int32)


def constants():
    ident = np.eye(P, dtype=np.float32)
    rot = np.zeros((P, P), np.float32)
    for b in (0, ROPE):
        for m in range(ROPE // 2):
            rot[b + m + ROPE // 2, b + m] = -1.0
            rot[b + m, b + m + ROPE // 2] = 1.0
    q, k = np.arange(P)[:, None], np.arange(P)[None, :]
    causal = np.where(k <= q, 0.0, -1e30).astype(np.float32)
    inv = 1.0 / (np.float32(THETA) ** (np.arange(0, ROPE, 2, dtype=np.float32) / np.float32(ROPE)))
    inv = np.tile(inv.astype(np.float32), 4)[:, None]
    return np.ascontiguousarray(np.concatenate([ident, rot, causal, inv], axis=1))


def build(nc, ap, out):
    (x, c, positions, w_ada, b_ada, g_pre_mix, w_in, g_q_lat, w_q_up, g_kv_lat, w_kv_up, w_gla_gate_up,
     b_gla_gate, g_gla_out, w_branch_a, w_branch_b, w_mix_out, g_post_mix, g_pre_ffn, w_ffn_up, conv_w,
     conv_b, w_ffn_down, g_post_ffn, const_f, const_m) = ap
    ctx = ExitStack()
    with ctx:
        def sb(name, shape, dt):
            return ctx.enter_context(nc.sbuf_tensor(name, shape, dt))

        def sem(name):
            return ctx.enter_context(nc.semaphore(name))

        raw = sb("raw", [P, RING, 2, UC], F32)
        w_hi = sb("w_hi", [P, RING, 2, UC], F32R)
        w_lo = sb("w_lo", [P, RING, 2, UC], F32R)
        acc = sb("acc", [P, D], F32)
        fixed = sb("fixed", [P, 3 * P + 1], F32)
        ident, rot, causal = (fixed[:, i * P:(i + 1) * P] for i in range(3))
        inv_freq = fixed[:, 3 * P:3 * P + 1]
        ones = sb("ones", [P, P], F32)
        masks = sb("masks", [P, LEVELS - 1, P], U8)
        cos_t = sb("cos_t", [P, S], F32)
        sin_t = sb("sin_t", [P, S], F32)
        vec = sb("vec", [P, V_END], F32)
        c_act = sb("c_act", [P, KT], F32)
        mod = sb("mod", [P, 6, KT], F32)
        cross = sb("cross", [P, 2, S], F32)
        ytmp = sb("ytmp", [P, 2, S], F32)
        eps_t = sb("eps_t", [P, 1], F32)
        stat = sb("stat", [P, 32], F32)
        cap_kb = 139 * 1024

        def at(kb, name, shape, dt, size_kb):
            words = 1
            for n in shape[1:]:
                words *= n
            assert words * 4 <= size_kb * 1024 and (kb + size_kb) * 1024 <= cap_kb, name
            with nc.sbuf_tensor(name + "_before", [P, max(kb, 0) * 256 + 8], F32):
                with nc.sbuf_tensor(name, shape, dt) as t:
                    pass
            return t

        ada = at(0, "ada", [P, RING, AC], F32, 16)
        conv_in = at(0, "conv_in", [P, 4, S + 2], F32, 5)
        conv_a = at(5, "conv_a", [P, 4, S], F32, 4)
        conv_v = at(9, "conv_v", [P, 4, S], F32, 4)
        hid_f = at(13, "hid_f", [P, 2, S], F32, 2)
        B = 16
        cap_kb = (B + 137) * 1024
        ht = at(B + 0, "ht", [P, KT, 2, S], F32R, 32)
        ot = at(B + 32, "ot", [P, H, 2, S], F32R, 16)
        og = at(B + 48, "og", [P, KT, S], F32, 16)
        v_gla = at(B + 64, "v_gla", [P, NT, GH * DV], F32, 16)
        q_gla = at(B + 80, "q_gla", [P, 8, S], F32, 8)
        k_gla = at(B + 88, "k_gla", [P, 8, S], F32, 8)
        x_tok = at(B + 96, "x_tok", [P, NT, D], F32, 16)
        xn_tok = at(B + 112, "xn_tok", [P, NT, D], F32, 16)
        xn_t = at(B + 48, "xn_t", [P, KT, S], F32, 16)
        h_f = at(B + 64, "h_f", [P, KT, S], F32, 16)
        junk = at(B + 80, "junk", [P, D], F32, 8)
        rows = at(B + 88, "rows", [P, 5, P], F32, 3)
        pos_i = at(B + 32, "pos_i", [P, S], I32, 1)
        pos_f = at(B + 33, "pos_f", [P, S], F32, 1)
        ang = at(B + 34, "ang", [P, S], F32, 1)
        turn = at(B + 35, "turn", [P, 2, S], F32, 2)
        red = at(B + 37, "red", [P, 2, S], F32, 2)
        masks_i = at(B + 39, "masks_i", [P, LEVELS - 1, P], I32, 4)
        acc_2 = at(B + 128, "acc_2", [P, D], F32, 8)
        lat = at(B + 48, "lat", [P, 6, S], F32, 6)
        lat_s = at(B + 54, "lat_s", [P, 6, 2, S], F32R, 12)
        lat_sq = at(B + 66, "lat_sq", [P, 6, S], F32, 6)
        q_rope_in = at(B + 72, "q_rope_in", [P, 4, S], F32, 4)
        rope_tmp = at(B + 76, "rope_tmp", [P, 2, S], F32, 2)
        lat_r = at(B + 78, "lat_r", [P, 2, S], F32, 2)
        q_nope = at(B + 96, "q_nope", [P, H, S], F32, 8)
        k_nope = at(B + 104, "k_nope", [P, H, S], F32, 8)
        v_mla = at(B + 112, "v_mla", [P, NT, H * VD], F32, 8)
        q_rope = at(B + 120, "q_rope", [P, 4, S], F32, 4)
        k_rope = at(B + 124, "k_rope", [P, S], F32, 1)
        probs = at(B + 125, "probs", [P, 3, 4 * P], F32, 6)
        probs_t = at(B + 131, "probs_t", [P, 2, 3 * P], F32, 3)
        k_rope_in = at(B + 134, "k_rope_in", [P, S], F32, 1)
        lr_t = at(B + 135, "lr_t", [P, S], F32, 1)
        soft = at(B + 136, "soft", [P, 3, 8], F32, 1)
        w_gate = at(B + 48, "w_gate", [P, GH * DK], F32, 4)
        pre = at(B + 96, "pre", [P, 8, S], F32, 8)
        suf = at(B + 104, "suf", [P, 8, S], F32, 8)
        dec = at(B + 112, "dec", [P, 8, S], F32, 8)
        qk = at(B + 120, "qk", [P, 8, S], F32, 8)
        attn0 = at(B + 128, "attn0", [P, GH, S], F32, 4)
        attn1 = at(B + 132, "attn1", [P, GH, P], F32, 2)
        o_gla = at(B + 96, "o_gla", [P, KT, S], F32, 16)
        o_sq = at(B + 112, "o_sq", [P, 4, S], F32, 4)
        o_r = at(B + 128, "o_r", [P, GH, S], F32, 4)
        og_s = at(B + 0, "og_s", [P, KT, 2, S], F32R, 32)
        gate_a = at(B + 80, "gate_a", [P, KT, S], F32, 16)
        gate_b = at(B + 112, "gate_b", [P, KT, S], F32, 16)
        merged = at(B + 32, "merged", [P, KT, 2, S], F32R, 32)
        gg_m = at(B + 64, "gg_m", [P, D], F32, 8)
        gpost_m = at(B + 72, "gpost_m", [P, D], F32, 8)
        brow_m = at(B + 128, "brow_m", [P, UC], F32, 2)
        x_again = at(B + 96, "x_again", [P, NT, D], F32, 16)
        x1 = at(B + 121, "x1", [P, NT, D], F32, 16)
        xn1 = at(B + 80, "xn1", [P, NT, D], F32, 16)
        h2_f = at(B + 32, "h2_f", [P, KT, S], F32, 16)
        junk_m = at(B + 112, "junk_m", [P, D], F32, 8)
        h2t = at(B + 0, "h2t", [P, KT, 2, S], F32R, 32)
        hid = at(B + 32, "hid", [P, FF // P, 2, S], F32R, 88)
        f_tok = at(B + 0, "f_tok", [P, NT, D], F32, 16)
        gg_f = at(B + 16, "gg_f", [P, D], F32, 8)
        gpost_f = at(B + 24, "gpost_f", [P, D], F32, 8)
        junk_f = at(5, "junk_f", [P, UC], F32, 2)
        brow_f = ytmp[:].rearrange("p a t -> p (a t)")

        ps = ctx.enter_context(nc.psum_tensor("ps", [P, 8, UC], F32))

        x_loaded, rows_loaded, const_loaded = sem("x_loaded"), sem("rows_loaded"), sem("const_loaded")
        first_rows_loaded, masks_loaded = sem("first_rows_loaded"), sem("masks_loaded")
        gate_w_loaded, post_loaded, x_again_loaded = sem("gate_w_loaded"), sem("post_loaded"), sem("x_again_loaded")
        post_f_loaded, bias_f_loaded, stored = sem("post_f_loaded"), sem("bias_f_loaded"), sem("stored")
        raw_loaded = [sem(f"raw_loaded{r}") for r in range(RING)]
        ada_loaded = [sem(f"ada_loaded{r}") for r in range(RING)]
        hi_done, lo_done = sem("hi_done"), sem("lo_done")
        pairs_used = sem("pairs_used")
        tile_ready = sem("tile_ready")
        tile_half = sem("tile_half")
        tile_empty = sem("tile_empty")
        ada_used = sem("ada_used")
        acc_zero = sem("acc_zero")
        mod_ready, mod_psum = sem("mod_ready"), sem("mod_psum")
        dve_step, act_step, pool_step = sem("dve_step"), sem("act_step"), sem("pool_step")
        setup_done = sem("setup_done")
        rows_t, vec_ready, c_ready = sem("rows_t"), sem("vec_ready"), sem("c_ready")
        ssq_x, rms_x, norm_x, xt_psum, xt_copied = (sem("ssq_x"), sem("rms_x"), sem("norm_x"), sem("xt_psum"),
                                                    sem("xt_copied"))
        recip_x, attn_zero, suffix_ready = sem("recip_x"), sem("attn_zero"), sem("suffix_ready")
        h_ready, h_hi, h_lo = sem("h_ready"), sem("h_hi"), sem("h_lo")
        angle_ready, table_ready = sem("angle_ready"), sem("table_ready")
        lat_squared, lat_summed, lat_rms, lat_normed, lat_hi, lat_lo = (
            sem("lat_squared"), sem("lat_summed"), sem("lat_rms"), sem("lat_normed"), sem("lat_hi"), sem("lat_lo"))
        rot_ready, rope_done = sem("rot_ready"), sem("rope_done")
        scores_ready, max_ready, exp_done, probs_ready = (sem("scores_ready"), sem("max_ready"), sem("exp_done"),
                                                          sem("probs_ready"))
        pt_ready, pt_copied, ctx_ready, ctx_hi, ctx_lo = (sem("pt_ready"), sem("pt_copied"), sem("ctx_ready"),
                                                          sem("ctx_hi"), sem("ctx_lo"))
        gate_psum, gate_pre, gate_soft, decay_ready = (sem("gate_psum"), sem("gate_pre"), sem("gate_soft"),
                                                       sem("decay_ready"))
        dec_ready, qk_ready, scan_ready, level_ready, level_taken = (
            sem("dec_ready"), sem("qk_ready"), sem("scan_ready"), sem("level_ready"), sem("level_taken"))
        og_psum, og_copied, og_squared, og_summed, og_rms, og_silu, og_gated, og_hi, og_lo = (
            sem("og_psum"), sem("og_copied"), sem("og_squared"), sem("og_summed"), sem("og_rms"), sem("og_silu"),
            sem("og_gated"), sem("og_hi"), sem("og_lo"))
        sig_done, mul_done, merged_ready, merged_hi, merged_lo = (
            sem("sig_done"), sem("mul_done"), sem("merged_ready"), sem("merged_hi"), sem("merged_lo"))
        gate_row, gg_ready = sem("gate_row"), sem("gg_ready")
        rms_y, x1_ready, ssq_1, rms_1, norm_1, x1t_psum, h2_ready, h2_hi, h2_lo = (
            sem("rms_y"), sem("x1_ready"), sem("ssq_1"), sem("rms_1"), sem("norm_1"), sem("x1t_psum"),
            sem("h2_ready"), sem("h2_hi"), sem("h2_lo"))
        conv_first, conv_done, gelu_done, hid_ready, hid_hi, hid_lo = (
            sem("conv_first"), sem("conv_done"), sem("gelu_done"), sem("hid_ready"), sem("hid_hi"), sem("hid_lo"))
        sum_f, rms_f, out_ready = sem("sum_f"), sem("rms_f"), sem("out_ready")

        def halves(t, h):
            v = t[:, :, :].rearrange("p d (b s h) -> p (d b) s h", s=2, h=h)
            return v[:, :, 0, :], v[:, :, 1, :]

        def spread(col, like):
            return col.to_broadcast(list(like.shape))

        class Steps:

            def __init__(self, eng, s):
                self.eng, self.s, self.n = eng, s, 0

            def mark(self, ins):
                ins.then_inc(self.s, 1)
                self.n = self.n + 1

            def wait(self):
                self.eng.wait_ge(self.s, self.n)

        block = ctx.enter_context(nc.Block())

        @block.sync
        def _(sp):
            def load_unit(u, r, src):
                if not isinstance(u, int) or u >= RING:
                    sp.wait_ge(lo_done, u - (RING - 1))
                sp.dma_start(raw[:, r], src).then_inc(raw_loaded[r], 16)

            def load_ada(a, r, src):
                if not isinstance(a, int) or a >= RING:
                    sp.wait_ge(ada_used, a - (RING - 1))
                sp.dma_start(ada[:, r], src).then_inc(ada_loaded[r], 16)

            def two_kt(w, row0, col0):
                return w[bass.ds(row0, 2 * P), bass.ds(col0, UC)].rearrange("(k p) n -> p k n", p=P)

            def ada_src(block_no, kt, half):
                return w_ada[bass.ds(kt * P, P), bass.ds(block_no * D + half * AC, AC)]

            def group(u0, nu, src, a0=None, a_block=None, a_kt=None, slot0=0):
                for j in range(nu):
                    load_unit(u0 + j, (slot0 + j) % RING, src(j))
                    if a0 is not None and j % 2 == 1:
                        n = j // 2
                        load_ada(a0 + n, n % RING, ada_src(a_block, a_kt + n // 2, n % 2))

            def small(dst, src, loaded=rows_loaded):
                sp.dma_start(dst, src).then_inc(loaded, 16)

            def as_rows(v):
                return v.rearrange("(r c) -> r c", c=P)

            def first_ada(half, i):
                for r in range(RING):
                    a = 2 * KT * half + 4 * i + r
                    load_ada(a, r, ada_src(r % 2, 2 * i + r // 2, half))

            def load_misc(j):
                r = j % RING
                rs = w_in[j * 2 * P:(j + 1) * 2 * P, :].rearrange("(k p) n -> p k n", p=P)
                if j >= RING:
                    sp.wait_ge(lo_done, j - (RING - 1))
                sp.dma_start(raw[:, r, :, 0:320], rs[:, :, C_KV:C_KV + 320]).then_inc(raw_loaded[r], 16)
                sp.dma_start(raw[:, r, :, 320:384], rs[:, :, C_KR:C_KR + ROPE]).then_inc(raw_loaded[r], 16)
                sp.dma_start(raw[:, r, :, 384:512], rs[:, :, C_LR:C_LR + P]).then_inc(raw_loaded[r], 16)

            for dst0, v in ((96, c[0]), (0, b_ada[0]), (112, g_pre_mix[0])):
                n = v.shape[0] // P
                small(rows[dst0:dst0 + n, 0, :], as_rows(v), first_rows_loaded)
            sp.dma_start(fixed[:], const_f).then_inc(const_loaded, 16)
            sp.dma_start(pos_i[:], positions[0:1, :].to_broadcast([P, S])).then_inc(const_loaded, 16)
            first_ada(0, 0)
            sp.dma_start(x_tok[:], x[0].rearrange("(t p) d -> p t d", p=P)).then_inc(x_loaded, 16)
            for v0, v in ((V_GQ, g_q_lat[0]), (V_GKV, g_kv_lat[0]), (V_BGLA, b_gla_gate[0]), (V_GOUT, g_gla_out[0]),
                          (V_GFFN, g_pre_ffn[0]), (V_CB, conv_b[0])):
                n = v.shape[0] // P
                small(rows[v0 - P:v0 - P + n, 1, :], as_rows(v))
            cw = conv_w[0].rearrange("i (r c) -> (i r) c", c=P)
            for k in range(3):
                n = min(P, cw.shape[0] - k * P)
                small(rows[0:n, 2 + k, :], cw[k * P:k * P + n, :])
            sp.dma_start(masks_i[:, :, :].rearrange("p l n -> p (l n)"), const_m).then_inc(masks_loaded, 16)

            with sp.Fori(1, KT // 2) as i:
                first_ada(0, i)
            for j in range(RING):
                load_misc(j)
            with sp.Fori(0, KT // 2) as i:
                first_ada(1, i)
            _, _, _, a0 = FIRST_OF["misc"]
            for j in range(RING, 8):
                load_misc(j)
                if j >= RING + 1:
                    n = j - RING - 1
                    load_ada(a0 + n, n, ada_src(3, n // 2, n % 2))
            load_ada(a0 + 3, 3, ada_src(3, 1, 1))
            u0, _, _, a0 = FIRST_OF["qlat"]
            group(u0, 8, lambda j: two_kt(w_in, 256 * j, C_Q), a0, 3, 2)
            u0, _, _, a0 = FIRST_OF["gq"]
            with sp.Fori(0, 2) as g:
                group(u0 + 8 * g, 8, lambda j: two_kt(w_in, 256 * j, C_GQ + UC * g), a0 + 4 * g, 3, 4 + 2 * g)
            u0 = FIRST_OF["qup"][0]
            qv = w_q_up.rearrange("(k p) (h e) -> p k h e", p=P, e=NOPE + ROPE)
            for n in range(6):
                g, j = n // 2, n % 2
                r = (u0 + n) % RING
                sp.wait_ge(lo_done, u0 + n - (RING - 1))
                for k in range(2):
                    if g < 2:
                        dst = raw[:, r, k, :].rearrange("p (h e) -> p h e", h=4)
                        sp.dma_start(dst, qv[:, 2 * j + k, 4 * g:4 * g + 4, 0:NOPE]).then_inc(raw_loaded[r], 8 * 2)
                    else:
                        dst = raw[:, r, k, :].rearrange("p (h e) -> p h e", h=H)
                        sp.dma_start(dst, qv[:, 2 * j + k, :, NOPE:NOPE + ROPE]).then_inc(raw_loaded[r], 8 * 2)
            u0 = FIRST_OF["kup"][0]
            kvv = w_kv_up.rearrange("(k p) (h e) -> p k h e", p=P, e=NOPE + VD)
            for n in range(4):
                part, hh = n // 2, n % 2
                r = (u0 + n) % RING
                sp.wait_ge(lo_done, u0 + n - (RING - 1))
                for k in range(2):
                    dst = raw[:, r, k, :].rearrange("p (h e) -> p h e", h=4)
                    sp.dma_start(dst, kvv[:, k, 4 * hh:4 * hh + 4, part * NOPE:part * NOPE + P])\
                        .then_inc(raw_loaded[r], 16)
            s0 = FIRST_OF["gk"][0] % RING
            u0, _, _, a0 = FIRST_OF["gk"]
            with sp.Fori(0, 2) as g:
                group(u0 + 8 * g, 8, lambda j: two_kt(w_in, 256 * j, C_GK + UC * g), a0 + 4 * g, 3, 8 + 2 * g, s0)
            sp.wait_ge(tile_ready, FIRST_OF["gk"][1])
            sp.dma_start(w_gate[0:GR, :], w_gla_gate_up).then_inc(gate_w_loaded, 16)
            u0, _, _, a0 = FIRST_OF["gv"]
            with sp.Fori(0, 2) as g:
                group(u0 + 8 * g, 8, lambda j: two_kt(w_in, 256 * j, C_GV + UC * g), a0 + 4 * g, 3, 12 + 2 * g, s0)
            with sp.Fori(2, 4) as g:
                group(u0 + 8 * g, 8, lambda j: two_kt(w_in, 256 * j, C_GV + UC * g), a0 + 4 * g, 4, 2 * g - 4, s0)
            u0, _, _, a0 = FIRST_OF["og"]
            with sp.Fori(0, 6) as g:
                group(u0 + 8 * g, 8, lambda j: two_kt(w_in, 256 * j, C_OG + UC * g), a0 + 4 * g, 4, 4 + 2 * g, s0)
            with sp.Fori(6, 12) as g:
                group(u0 + 8 * g, 8, lambda j: two_kt(w_in, 256 * j, C_OG + UC * g), a0 + 4 * g, 2, 2 * g - 12, s0)
            sp.wait_ge(og_psum, 8)
            sp.dma_start(gpost_m[:], g_post_mix[0:1, :].to_broadcast([P, D])).then_inc(post_loaded, 16)
            u0, _, _, a0 = FIRST_OF["ba"]
            with sp.Fori(0, 2) as g:
                for n in range(2):
                    group(u0 + 8 * g + 4 * n, 4, lambda j: two_kt(w_branch_a, 256 * j, 2 * UC * g + UC * n),
                          None, None, None, s0)
                    for m in range(2):
                        load_ada(a0 + 4 * g + 2 * n + m, 2 * n + m, ada_src(2, 12 + 2 * g + n, m))
            sp.wait_ge(og_gated, 4)
            for b in range(4):
                c0 = 2 * D + b * UC
                sp.dma_start(brow_m[32 * b:32 * b + 1, :], b_ada[0:1, c0:c0 + UC]).then_inc(post_loaded, 16)
            u0, _, _, a0 = FIRST_OF["bb"]
            with sp.Fori(0, 4) as g:
                group(u0 + 8 * g, 8, lambda j: two_kt(w_branch_b, 256 * j, UC * g), a0 + 4 * g, 5, 2 * g, s0)
            sp.wait_ge(og_lo, 4)
            sp.dma_start(x_again[:], x[0].rearrange("(t p) d -> p t d", p=P)).then_inc(x_again_loaded, 16)
            u0, _, _, a0 = FIRST_OF["mix"]
            with sp.Fori(0, 4) as g:
                group(u0 + 8 * g, 8, lambda j: two_kt(w_mix_out, 256 * j, UC * g), a0 + 4 * g, 5, 8 + 2 * g, s0)
            u0 = FIRST_OF["ffn"][0]
            with sp.Fori(0, 11) as g:
                for part in range(2):
                    group(u0 + 16 * g + 8 * part, 8,
                          lambda j: two_kt(w_ffn_up, 256 * j, part * FF + UC * g), None, None, None, s0)
            for b in range(4):
                c0 = 5 * D + b * UC
                sp.dma_start(brow_f[32 * b:32 * b + 1, :], b_ada[0:1, c0:c0 + UC]).then_inc(bias_f_loaded, 16)
            u0, t0, _, _ = FIRST_OF["down"]
            for n in range(4):
                for j in range(22):
                    load_unit(u0 + 22 * n + j, (s0 + 22 * n + j) % RING, two_kt(w_ffn_down, 256 * j, UC * n))
                    if n == 0 and j == RING:
                        sp.wait_ge(tile_ready, t0)
                        sp.dma_start(gpost_f[:], g_post_ffn[0:1, :].to_broadcast([P, D])).then_inc(post_f_loaded, 16)
            for n in range(4):
                t, c0 = n // 2, (n % 2) * (D // 2)
                sp.wait_ge(out_ready, n + 1)
                sp.dma_start(out[0, t * P:(t + 1) * P, c0:c0 + D // 2], f_tok[:, t, c0:c0 + D // 2])\
                    .then_inc(stored, 16)
            sp.wait_ge(stored, 64)

        @block.tensor
        def _(pe):
            mm = nc.tensor.matmul

            def tile_free(t):
                if not isinstance(t, int) or t >= 4:
                    pe.wait_ge(tile_empty, t - 3)

            def feature_pair(u, t0, kt0, last, moving, slot, first, moving_ready=None):
                pe.wait_ge(lo_done, u + 2)
                if moving_ready is not None:
                    pe.wait_ge(moving_ready, kt0 // 4 + 1)
                for f in range(4):
                    if first:
                        tile_free(t0 + f)
                    for j in range(2):
                        s = (slot + j) % RING
                        for k in range(2):
                            kt = kt0 + 2 * j + k
                            start = first and j == 0 and k == 0
                            stop = last and j == 1 and k == 1
                            cols = slice(f * P, (f + 1) * P)
                            mm(ps[:, f, :], w_hi[:, s, k, cols], moving[:, kt].rearrange("p a t -> p (a t)"),
                               start=start, stop=False)
                            ins = mm(ps[:, f, 0:S], w_lo[:, s, k, cols], moving[:, kt, 0], start=False, stop=stop)
                    if last:
                        ins.then_inc(tile_ready, 1)
                if not last:
                    ins.then_inc(pairs_used, 1)

            def feature_group(u0, t0, nu, moving, slot, kt0=0, moving_ready=None):
                for j in range(0, nu, 2):
                    feature_pair(u0 + j, t0, kt0 + 2 * j, j == nu - 2, moving, (slot + j) % RING, j == 0, moving_ready)

            def token_group(u0, t0, nu, still, slot, bank0, still_lo, base=0):
                for j in range(0, nu, 2):
                    first, last = j == 0, j == nu - 2
                    pe.wait_ge(still_lo, base + 2 * j + 4)
                    pe.wait_ge(lo_done, u0 + j + 2)
                    for t in range(NT):
                        if first:
                            tile_free(t0 + t)
                        o = ps[:, bank0 + t, :]
                        for i in range(2):
                            s = (slot + j + i) % RING
                            for k in range(2):
                                kt = 2 * (j + i) + k
                                tok = slice(t * P, (t + 1) * P)
                                start = first and i == 0 and k == 0
                                mm(o, still[:, kt, 0, tok], w_hi[:, s, k, :], start=start, stop=False)
                                mm(o, still[:, kt, 0, tok], w_lo[:, s, k, :], start=False, stop=False)
                                ins = mm(o, still[:, kt, 1, tok], w_hi[:, s, k, :], start=False,
                                         stop=last and i == 1 and k == 1)
                        if last:
                            ins.then_inc(tile_ready, 1)
                    if not last:
                        ins.then_inc(pairs_used, 1)

            def mod_columns(n_block, used, bank=4):
                pe.wait_ge(ada_used, used)
                if n_block:
                    pe.wait_ge(mod_ready, n_block)
                for i in range(KT):
                    ins = mm(ps[:, bank, i:i + 1], acc[:, i * P:(i + 1) * P], ones[:, 0:1], start=True, stop=True)
                ins.then_inc(mod_psum, 1)

            pe.wait_ge(first_rows_loaded, 3 * 16)
            pe.wait_ge(const_loaded, 2 * 16)
            nc.tensor.transpose(ps[:, 6, 0:P], rows[:, 0, :], ident[:]).then_inc(rows_t, 1)
            pe.wait_ge(rows_loaded, 9 * 16)
            for k in range(1, 5):
                n = (P, P - 6, P, P, V_END - V_CW - 2 * P)[k]
                ins = nc.tensor.transpose(ps[:, 4 + k // 4, (k % 4) * P:(k % 4) * P + n], rows[0:n, k, :],
                                          ident[0:n, 0:n])
            ins.then_inc(rows_t, 1)
            pe.wait_ge(norm_x, 2)
            pe.wait_ge(vec_ready, 1)
            for b in range(8):
                for q in range(4):
                    kt, t = 2 * b + q // 2, q % 2
                    ins = nc.tensor.transpose(ps[:, b, q * P:(q + 1) * P], xn_tok[:, t, kt * P:(kt + 1) * P], ident[:])
                ins.then_inc(xt_psum, 1)
            pe.wait_ge(xt_copied, 8)
            pe.wait_ge(setup_done, 2)
            for half in range(2):
                pe.wait_ge(ada_used, (half + 1) * ADA_BLOCK)
                if half:
                    pe.wait_ge(mod_ready, 1)
                for i in range(KT):
                    src, kt = (acc, acc_2)[i // 8], 8 * half + i % 8
                    ins = mm(ps[:, 4, i:i + 1], src[:, kt * P:(kt + 1) * P], ones[:, 0:1], start=True, stop=True)
                ins.then_inc(mod_psum, 1)
                for j in (4 * half, 4 * half + 2):
                    feature_pair(j, 0, 2 * j, j == 6, ht, j % RING, j == 0, h_lo)
            feature_group(8, 4, 8, ht, 0)
            u0, t0, _, _ = FIRST_OF["gq"]
            feature_group(u0, t0, 8, ht, 0)
            pe.wait_ge(lat_squared, 1)
            pe.wait_ge(mod_ready, 2)
            for n, (f0, nf) in enumerate(((0, 2), (2, 4))):
                for i in range(nf):
                    ins = mm(ps[:, 4, n * S:(n + 1) * S], ones[:], lat_sq[:, f0 + i, :], start=i == 0, stop=i == nf - 1)
            ins.then_inc(lat_summed, 1)
            feature_group(u0 + 8, t0 + 4, 8, ht, 0)
            pe.wait_ge(lat_lo, 1)
            u0, t0, _, _ = FIRST_OF["qup"]
            for g in range(3):
                feature_group(u0 + 2 * g, t0 + 4 * g, 2, lat_s, (u0 + 2 * g) % RING, 2)
            u0, t0, _, _ = FIRST_OF["kup"]
            pe.wait_ge(lo_done, u0 + 2)
            for n in range(8):
                f, s = n % 4, (u0 + n // 4) % RING
                tile_free(t0 + n)
                for k in range(2):
                    cols = slice(f * P, (f + 1) * P)
                    mm(ps[:, f, :], w_hi[:, s, k, cols], lat_s[:, k].rearrange("p a t -> p (a t)"), start=k == 0,
                       stop=False)
                    ins = mm(ps[:, f, 0:S], w_lo[:, s, k, cols], lat_s[:, k, 0], start=False, stop=k == 1)
                ins.then_inc(tile_ready, 1)
            u0, t0, _, _ = FIRST_OF["vup"]
            pe.wait_ge(lo_done, u0 + 2)
            for n in range(4):
                half, t = n // 2, n % 2
                s = (u0 + half) % RING
                tile_free(t0 + n)
                tok = slice(t * P, (t + 1) * P)
                for k in range(2):
                    mm(ps[:, n, :], lat_s[:, k, 0, tok], w_hi[:, s, k, :], start=k == 0, stop=False)
                    mm(ps[:, n, :], lat_s[:, k, 0, tok], w_lo[:, s, k, :], start=False, stop=False)
                    ins = mm(ps[:, n, :], lat_s[:, k, 1, tok], w_hi[:, s, k, :], start=False, stop=k == 1)
                ins.then_inc(tile_ready, 1)

            def rope_rotate():
                pe.wait_ge(tile_empty, FIRST_OF["kup"][1])
                pe.wait_ge(lat_rms, 1)
                for i in range(4):
                    mm(ps[:, 4 + i // 2, (i % 2) * S:(i % 2 + 1) * S], rot[:], q_rope_in[:, i, :], start=True, stop=True)
                mm(ps[:, 6, 0:S], rot[:], k_rope_in[:], start=True, stop=True).then_inc(rot_ready, 1)

            def scores(h):
                if h == 0:
                    pe.wait_ge(rope_done, 5)
                    pe.wait_ge(tile_empty, FIRST_OF["vup"][1])
                else:
                    pe.wait_ge(max_ready, h)
                p0 = ROPE * (h % 2)
                for t in range(NT):
                    o = ps[:, 4, t * P:t * P + (t + 1) * P]
                    tok, keys = slice(t * P, (t + 1) * P), slice(0, (t + 1) * P)
                    mm(o, q_nope[:, h, tok], k_nope[:, h, keys], start=True, stop=False)
                    ins = mm(o, q_rope[p0:p0 + ROPE, h // 2, tok], k_rope[p0:p0 + ROPE, keys], start=False, stop=True)
                ins.then_inc(scores_ready, 1)

            def transpose_probs(h):
                pe.wait_ge(probs_ready, h + 1)
                if h:
                    pe.wait_ge(pt_copied, h)
                for i in range(3):
                    ins = nc.tensor.transpose(ps[:, 5, i * P:(i + 1) * P], probs[:, h % 3, i * P:(i + 1) * P], ident[:])
                ins.then_inc(pt_ready, 1)

            def context(h):
                pe.wait_ge(pt_copied, h + 1)
                if h:
                    pe.wait_ge(ctx_lo, h)
                else:
                    pe.wait_ge(tile_empty, FIRST_OF["gk"][1])
                hv = slice(h * VD, (h + 1) * VD)
                mm(ps[:, 6, 0:S], v_mla[:, 0, hv], probs_t[:, h % 2, 0:S], start=True, stop=False)
                mm(ps[:, 6, P:S], v_mla[:, 1, hv], probs_t[:, h % 2, S:3 * P], start=False, stop=True)\
                    .then_inc(ctx_ready, 1)

            def mla_at(step):
                h, odd = step // 2, step % 2
                if not odd:
                    if h < H:
                        scores(h)
                    if 0 <= h - 2 < H:
                        context(h - 2)
                elif 0 <= h - 1 < H:
                    transpose_probs(h - 1)

            def gate_preact(n):
                if n == 0:
                    pe.wait_ge(ctx_lo, H)
                    pe.wait_ge(gate_w_loaded, 16)
                else:
                    pe.wait_ge(gate_pre, 4)
                for i in range(4):
                    ft = 4 * n + i
                    ins = mm(ps[:, 6 + i // 2, (i % 2) * S:(i % 2 + 1) * S], w_gate[0:GR, ft * P:(ft + 1) * P],
                             lr_t[0:GR, :], start=True, stop=True)
                ins.then_inc(gate_psum, 1)

            def level(lv):
                pe.wait_ge(qk_ready, lv) if lv else pe.wait_ge(gate_pre, 8)
                if lv:
                    pe.wait_ge(level_taken, lv)
                else:
                    pe.wait_ge(tile_empty, FIRST_OF["gv"][1])
                n_q = P if lv in (0, LEVELS - 1) else P // 2
                for t in range(NT if lv < LEVELS - 1 else 1):
                    for hd in range(GH):
                        o = ps[:, 6 + t, hd * n_q:(hd + 1) * n_q]
                        for i in range(2):
                            d = 2 * hd + i
                            keys = slice(t * P, (t + 1) * P)
                            if lv == 0:
                                lhs, rhs = k_gla, q_gla[:, d, keys]
                            elif lv == LEVELS - 1:
                                lhs, rhs = qk, qk[:, d, P:2 * P]
                            else:
                                lhs = qk
                                rhs = qk[:, d, keys].rearrange("p (b s h) -> p b s h", s=2, h=1 << (lv - 1))[:, :, 1]
                            ins = mm(o, lhs[:, d, keys], rhs, start=i == 0, stop=i == 1)
                ins.then_inc(level_ready, 1)

            def gla_out(pr):
                if pr < 2:
                    pe.wait_ge(level_taken, LEVELS)
                    pe.wait_ge(tile_empty, FIRST_OF["og"][1])
                else:
                    pe.wait_ge(og_copied, pr - 1)
                for i in range(2):
                    ft = 2 * pr + i
                    hd = ft // 4
                    fv = slice(ft * P, (ft + 1) * P)
                    o = ps[:, 6 + pr % 2, i * S:(i + 1) * S]
                    mm(o, v_gla[:, 0, fv], attn0[:, hd, :], start=True, stop=False)
                    ins = mm(ps[:, 6 + pr % 2, i * S + P:(i + 1) * S], v_gla[:, 1, fv], attn1[:, hd, :], start=False,
                             stop=True)
                ins.then_inc(og_psum, 1)

            def gla_norm_sum(hd):
                pe.wait_ge(og_squared, hd + 1)
                for i in range(4):
                    ins = mm(ps[:, 4 + hd // 2, (hd % 2) * S:(hd % 2 + 1) * S], ones[:], o_sq[:, i, :],
                             start=i == 0, stop=i == 3)
                ins.then_inc(og_summed, 1)

            rope_rotate()
            s0 = FIRST_OF["gk"][0] % RING
            step = 0
            for g in range(2):
                u0, t0, _, _ = FIRST_OF["gk"]
                for j in range(0, 8, 2):
                    feature_pair(u0 + 8 * g + j, t0 + 4 * g, 2 * j, j == 6, ht, (s0 + j) % RING, j == 0)
                    mla_at(step)
                    step += 1
            u0, t0, _, _ = FIRST_OF["gv"]
            for g in range(4):
                for j in range(0, 8, 2):
                    first, last = j == 0, j == 6
                    pe.wait_ge(lo_done, u0 + 8 * g + j + 2)
                    for t in range(NT):
                        if first:
                            tile_free(t0 + 2 * g + t)
                        o = ps[:, (2 * g + t) % 4, :]
                        for i in range(2):
                            s = (s0 + j + i) % RING
                            for k in range(2):
                                kt = 2 * (j + i) + k
                                tok = slice(t * P, (t + 1) * P)
                                mm(o, ht[:, kt, 0, tok], w_hi[:, s, k, :], start=first and i == 0 and k == 0, stop=False)
                                mm(o, ht[:, kt, 0, tok], w_lo[:, s, k, :], start=False, stop=False)
                                ins = mm(o, ht[:, kt, 1, tok], w_hi[:, s, k, :], start=False,
                                         stop=last and i == 1 and k == 1)
                        if last:
                            ins.then_inc(tile_ready, 1)
                    if not last:
                        ins.then_inc(pairs_used, 1)
                    mla_at(step)
                    if step in (19, 20):
                        gate_preact(step - 19)
                    if step == 22:
                        level(0)
                    if g == 2 and first:
                        pe.wait_ge(max_ready, H)
                        mod_columns(2, 3 * ADA_BLOCK)
                    step += 1
            u0, t0, _, _ = FIRST_OF["og"]
            for g in range(4):
                for j in range(0, 8, 2):
                    feature_pair(u0 + 8 * g + j, t0 + 4 * g, 2 * j, j == 6, ht, (s0 + j) % RING, j == 0)
                    if step % 2 == 1 and 1 <= (step - 23) // 2 <= LEVELS - 1:
                        level((step - 23) // 2)
                    step += 1
            u0, t0, _, _ = FIRST_OF["ga"]
            for g in range(4):
                for j in range(0, 8, 2):
                    feature_pair(u0 + 8 * g + j, t0 + 4 * g, 2 * j, j == 6, ht, (s0 + j) % RING, j == 0)
                    n = step - 40
                    if n < 8:
                        gla_out(n)
                    if n % 2 == 1 and 3 <= n <= 9:
                        if n == 3:
                            pe.wait_ge(mod_ready, 3)
                        gla_norm_sum((n - 3) // 2)
                    if g == 2 and j == 0:
                        pe.wait_ge(og_copied, 7)
                        mod_columns(3, 4 * ADA_BLOCK, 6)
                    step += 1
            pe.wait_ge(og_rms, 1)
            with pe.Fori(4, 8) as g:
                feature_group(u0 + 8 * g, t0 + 4 * g, 8, ht, s0)
            pe.wait_ge(ctx_lo, H)
            u0, t0, _, _ = FIRST_OF["ba"]
            with pe.Fori(0, 4) as g:
                feature_group(u0 + 4 * g, t0 + 4 * g, 4, ot, s0)

            def gate_rows(used, brow):
                pe.wait_ge(ada_used, used)
                for b in range(4):
                    cols = slice(b * UC, (b + 1) * UC)
                    mm(ps[:, 4 + b, :], ones[:], acc[:, cols], start=True, stop=False)
                    row = slice(32 * b, 32 * b + 1)
                    ins = mm(ps[:, 4 + b, :], ones[row, :], brow[row, :], start=False, stop=True)
                ins.then_inc(gate_row, 1)

            pe.wait_ge(mod_ready, 4)
            pe.wait_ge(og_copied, 8)
            pe.wait_ge(post_loaded, 16 * 5)
            gate_rows(5 * ADA_BLOCK, brow_m)
            u0, t0, _, _ = FIRST_OF["bb"]
            with pe.Fori(0, 4) as g:
                feature_group(u0 + 8 * g, t0 + 4 * g, 8, og_s, s0, moving_ready=og_lo)
            u0, t0, _, _ = FIRST_OF["mix"]
            with pe.Fori(0, 2) as g:
                for n in range(2):
                    token_group(u0 + 16 * g + 8 * n, t0 + 4 * g + 2 * n, 8, merged, s0, 2 * n,
                                merged_lo)
            pe.wait_ge(tile_empty, FIRST_OF["ffn"][1])
            pe.wait_ge(gg_ready, 1)
            pe.wait_ge(norm_1, 2)
            for b in range(8):
                for q in range(4):
                    kt, t = 2 * b + q // 2, q % 2
                    ins = nc.tensor.transpose(ps[:, b, q * P:(q + 1) * P], xn1[:, t, kt * P:(kt + 1) * P], ident[:])
                ins.then_inc(x1t_psum, 1)
            pe.wait_ge(h2_hi, 2)
            pe.wait_ge(h2_ready, 2)
            u0, t0, _, _ = FIRST_OF["ffn"]
            with pe.Fori(0, 11) as g:
                for part in range(2):
                    feature_group(u0 + 16 * g + 8 * part, t0 + 8 * g + 4 * part, 8, h2t, s0, moving_ready=h2_lo)
            pe.wait_ge(bias_f_loaded, 16 * 4)
            gate_rows(6 * ADA_BLOCK, brow_f)
            u0, t0, _, _ = FIRST_OF["down"]
            with pe.Fori(0, 2) as g:
                for n in range(2):
                    token_group(u0 + 44 * g + 22 * n, t0 + 4 * g + 2 * n, 22, hid, (s0 + 22 * n) % RING, 2 * n,
                                hid_lo, 1)

        @block.scalar
        def _(act):
            A = nc.scalar.activation
            own = Steps(act, act_step)

            def split(u, slot, loaded, free_sem, free_at):
                act.wait_ge(raw_loaded[slot], loaded)
                if free_sem is not None:
                    act.wait_ge(free_sem, free_at)
                A(w_hi[:, slot], raw[:, slot], ACT.Copy).then_inc(hi_done, 1)

            def loads(u):
                u_q, u_k = FIRST_OF["qup"][0], FIRST_OF["gk"][0]
                return 3 if u < 8 else 2 if u_q <= u < u_k else 1

            total = [0] * (UNITS + 1)
            for u in range(UNITS):
                total[u] = loads(u) * 16 + (total[u - RING] if u >= RING else 0)

            def split_at(u0, j, t0, p0, nu=8, nt=4, g=None, per=8):
                u = u0 + 2 + j
                if u >= UNITS:
                    return
                loaded = total[u] if g is None else total[u] + g * (16 * per // RING)
                free = ((pairs_used, p0 + (j - 2) // 2 + 1) if j < nu else (tile_ready, t0 + nt) if j < nu + 2
                        else (pairs_used, p0 + nu // 2))
                split(u, u % RING, loaded, *free)

            def half_tile(t, bank, scale=1.0):
                act.wait_ge(tile_ready, t + 1)
                if not isinstance(t, int) or t >= 2:
                    act.wait_ge(tile_empty, t - 1)
                A(cross[:, bank % 2], ps[:, bank, S:2 * S], ACT.Copy, scale=scale).then_inc(tile_half, 1)

            nc.scalar.preload_act_table(ACT.Silu)
            act.wait_ge(rows_t, 1)
            own.mark(A(vec[:, 0:P], ps[:, 6, 0:P], ACT.Copy))
            own.wait()
            A(c_act[:], vec[:, V_C:V_C + KT], ACT.Silu).then_inc(c_ready, 1)
            act.wait_ge(x_loaded, 16)
            for t in range(NT):
                A(junk[:], x_tok[:, t], ACT.Square, accum_out=stat[:, t:t + 1]).then_inc(ssq_x, 1)
                act.wait_ge(ssq_x, t + 1)
            act.wait_ge(setup_done, 2)
            A(stat[:, 2:4], stat[:, 0:2], ACT.Sqrt, bias=eps_t[:], scale=1.0 / D).then_inc(rms_x, 1)
            act.wait_ge(rows_t, 2)
            A(vec[:, P:2 * P - 6], ps[:, 4, P:2 * P - 6], ACT.Copy)
            A(vec[:, V_CW:UC], ps[:, 4, V_CW:UC], ACT.Copy)
            A(vec[:, UC:V_END], ps[:, 5, 0:V_END - UC], ACT.Copy).then_inc(vec_ready, 1)
            act.wait_ge(angle_ready, 1)
            A(cos_t[:], red[:, 0], ACT.Sin).then_inc(table_ready, 1)
            A(sin_t[:], red[:, 1], ACT.Sin).then_inc(table_ready, 1)
            act.wait_ge(recip_x, 1)
            for t in range(NT):
                A(xn_tok[:, t], x_tok[:, t], ACT.Copy, scale=stat[:, 2 + t:3 + t]).then_inc(norm_x, 1)
            for b in range(8):
                act.wait_ge(xt_psum, b + 1)
                A(xn_t[:, 2 * b:2 * b + 2, :], ps[:, b, :].rearrange("p (k t) -> p k t", k=2), ACT.Copy)\
                    .then_inc(xt_copied, 1)

            def input_hi(half):
                act.wait_ge(mod_ready, half + 1)
                act.wait_ge(xt_copied, 8)
                for kt in range(8 * half, 8 * half + 8):
                    ins = A(ht[:, kt, 0], xn_t[:, kt], ACT.Identity, bias=mod[:, 0, kt:kt + 1],
                            scale=mod[:, 1, kt:kt + 1])
                    if kt % 4 == 3:
                        ins.then_inc(h_hi, 1)

            for r in range(RING):
                split(r, r, total[r], None, 0)
            input_hi(0)
            for j in (2, 3):
                split_at(0, j, 0, 0)
            input_hi(1)

            def features(u0, t0, p0, nu=8, g=None, per=8, scale=1.0, beside=None, j0=2):
                for j in range(j0, nu):
                    split_at(u0, j, t0, p0, nu, 4, g, per)
                    if beside is not None and j % 2 == 1:
                        beside()
                for f in range(3):
                    half_tile(t0 + f, f, scale)
                split_at(u0, nu, t0, p0, nu, 4, g, per)
                half_tile(t0 + 3, 3, scale)
                split_at(u0, nu + 1, t0, p0, nu, 4, g, per)
                if beside is not None:
                    beside()

            for name in ("misc", "qlat"):
                u0, t0, p0, _ = FIRST_OF[name]
                features(u0, t0, p0, j0=4 if name == "misc" else 2)
            act.wait_ge(tile_empty, 8)
            A(lat_sq[:], lat[:], ACT.Square).then_inc(lat_squared, 1)
            u0, t0, p0, _ = FIRST_OF["gq"]
            features(u0, t0, p0, scale=GLA_SCALE)
            act.wait_ge(lat_summed, 1)
            A(lat_r[:, 0], ps[:, 4, 0:S], ACT.Sqrt, bias=eps_t[:], scale=1.0 / KVR)
            A(lat_r[:, 1], ps[:, 4, S:2 * S], ACT.Sqrt, bias=eps_t[:], scale=1.0 / QR).then_inc(lat_rms, 1)
            for j in range(2, 8):
                split_at(u0 + 8, j, t0 + 4, p0 + 3)
                if j == 5:
                    act.wait_ge(lat_normed, 1)
                    A(lat_s[:, :, 0], lat[:], ACT.Copy).then_inc(lat_hi, 1)
            for f in range(4):
                half_tile(t0 + 4 + f, f, GLA_SCALE)
                if f >= 2:
                    split_at(u0 + 8, 6 + f, t0 + 4, p0 + 3)
            u0, t0, p0, _ = FIRST_OF["qup"]
            for g in range(3):
                features(u0 + 2 * g, t0 + 4 * g, p0, 2)
            u0, t0, p0, _ = FIRST_OF["kup"]
            for f in range(8):
                half_tile(t0 + f, f % 4)
                if f >= 6:
                    split_at(u0, f - 4, t0, p0, 2, 8)
            u0, t0, p0, _ = FIRST_OF["vup"]
            for n in range(4):
                half, t = n // 2, n % 2
                act.wait_ge(tile_ready, t0 + n + 1)
                A(v_mla[:, t, half * UC + S:(half + 1) * UC], ps[:, n, S:UC], ACT.Copy).then_inc(tile_half, 1)
                if n >= 2:
                    split_at(u0, n, t0, p0, 2, 4)

            def exps(h):
                act.wait_ge(max_ready, h + 1)
                k = h % 3
                for t in range(NT):
                    part = probs[:, k, t * P:t * P + (t + 1) * P]
                    ins = A(part, part, ACT.Exp, bias=soft[:, k, t:t + 1], scale=MLA_SCALE,
                            accum_out=soft[:, k, 2 + t:3 + t])
                    ins.then_inc(exp_done, 1)

            def copy_probs(h):
                act.wait_ge(pt_ready, h + 1)
                if h >= 2:
                    act.wait_ge(ctx_ready, h - 1)
                A(probs_t[:, h % 2], ps[:, 5, 0:3 * P], ACT.Copy).then_inc(pt_copied, 1)

            def context_hi(h):
                act.wait_ge(ctx_ready, h + 1)
                A(ot[:, h, 0], ps[:, 6, 0:S], ACT.Copy).then_inc(ctx_hi, 1)

            def mla_at(step):
                h, odd = step // 2, step % 2
                if odd:
                    if h < H:
                        exps(h)
                    if 0 <= h - 2 < H:
                        context_hi(h - 2)
                elif 0 <= h - 2 < H:
                    copy_probs(h - 2)

            def log_gate():
                act.wait_ge(gate_pre, 8)
                own.mark(A(dec[:], suf[:], ACT.Abs))
                own.wait()
                own.mark(A(dec[:], dec[:], ACT.Exp, scale=-1.0))
                own.wait()
                A(dec[:], dec[:], ACT.Ln, bias=ones[:, 0:1]).then_inc(gate_soft, 1)

            def decays(lv):
                h = 1 << (lv - 1)
                if lv > 1:
                    act.wait_ge(scan_ready, lv - 1)
                    act.wait_ge(qk_ready, lv - 1)
                else:
                    act.wait_ge(decay_ready, 1)
                d0, d1 = halves(dec, h)
                A(d1, halves(pre, h)[1], ACT.Exp)
                A(d0, halves(suf, h)[0], ACT.Exp).then_inc(dec_ready, 1)

            def gla_copy(pr):
                act.wait_ge(og_psum, pr + 1)
                A(o_gla[:, 2 * pr:2 * pr + 2, :], ps[:, 6 + pr % 2, :].rearrange("p (k t) -> p k t", k=2), ACT.Copy)\
                    .then_inc(og_copied, 1)

            def gla_square(hd):
                act.wait_ge(og_copied, 2 * hd + 2)
                if hd:
                    act.wait_ge(og_summed, hd)
                A(o_sq[:], o_gla[:, 4 * hd:4 * hd + 4], ACT.Square).then_inc(og_squared, 1)

            steps = [0]

            def beside():
                step = steps[0]
                steps[0] += 1
                mla_at(step)
                if step == 21:
                    log_gate()
                if step % 2 == 1 and 1 <= (step - 21) // 2 <= LEVELS - 1:
                    decays((step - 21) // 2)
                n = step - 40
                if 1 <= n <= 8:
                    gla_copy(n - 1)
                    if n % 2 == 0:
                        gla_square(n // 2 - 1)
                if n == 10:
                    act.wait_ge(og_summed, GH)
                    A(o_r[:].rearrange("p (b h) t -> p b (h t)", b=2), ps[:, 4:6, :], ACT.Sqrt, bias=eps_t[:],
                      scale=1.0 / DV).then_inc(og_rms, 1)
                if n == 11:
                    A(og[:], og[:], ACT.Silu).then_inc(og_silu, 1)

            beside()
            u0, t0, p0, _ = FIRST_OF["gk"]
            for g in range(2):
                features(u0 + 8 * g, t0 + 4 * g, p0 + 3 * g, beside=beside)
            u0, t0, p0, _ = FIRST_OF["gv"]
            for g in range(4):
                for j in range(2, 8):
                    split_at(u0 + 8 * g, j, t0 + 2 * g, p0 + 3 * g, 8, 2)
                    if j % 2 == 1:
                        beside()
                for t in range(NT):
                    n = t0 + 2 * g + t
                    if t == 1:
                        for j in (8, 9):
                            split_at(u0 + 8 * g, j, t0 + 2 * g, p0 + 3 * g, 8, 2)
                    act.wait_ge(tile_ready, n + 1)
                    A(v_gla[:, t, g * UC + S:(g + 1) * UC], ps[:, n % 4, S:UC], ACT.Copy).then_inc(tile_half, 1)
                beside()
            u0, t0, p0, _ = FIRST_OF["og"]
            for g in range(4):
                features(u0 + 8 * g, t0 + 4 * g, p0 + 3 * g, beside=beside)
            u0, t0, p0, _ = FIRST_OF["ga"]
            for g in range(4):
                features(u0 + 8 * g, t0 + 4 * g, p0 + 3 * g, beside=beside)
                act.wait_ge(tile_empty, t0 + 4 * g + 4)
                tiles = gate_a[:, 4 * g:4 * g + 4]
                A(tiles, tiles, ACT.Sigmoid).then_inc(sig_done, 1)
            nc.scalar.preload_act_table(ACT.Sigmoid)
            with act.Fori(4, 8) as g:
                features(u0, t0 + 4 * g, p0 + 3 * g, g=g)
                act.wait_ge(tile_empty, t0 + 4 * g + 4)
                tiles = gate_b[:, bass.ds(4 * g - 16, 4)]
                A(tiles, tiles, ACT.Sigmoid).then_inc(sig_done, 1)
            act.wait_ge(og_gated, 4)
            act.wait_ge(tile_ready, FIRST_OF["ba"][1])
            for q in range(4):
                A(og_s[:, 4 * q:4 * q + 4, 0], o_gla[:, 4 * q:4 * q + 4], ACT.Copy).then_inc(og_hi, 1)
            u0, t0, p0, _ = FIRST_OF["ba"]
            with act.Fori(0, 2) as g:
                for n in range(2):
                    features(u0 + 4 * n, t0 + 8 * g + 4 * n, p0 + 2 * g + n, 4, g)
            u0, t0, p0, _ = FIRST_OF["bb"]
            with act.Fori(0, 4) as g:
                for j in range(2, 8):
                    split_at(u0, j, t0 + 4 * g, p0 + 3 * g, g=g)
                for f in range(6):
                    if f == 3:
                        split_at(u0, 8, t0 + 4 * g, p0 + 3 * g, g=g)
                    if f < 4:
                        half_tile(t0 + 4 * g + f, f)
                    if f == 3:
                        split_at(u0, 9, t0 + 4 * g, p0 + 3 * g, g=g)
                    if f >= 2:
                        act.wait_ge(merged_ready, 4 * g + f - 1)
                        A(merged[:, bass.ds(4 * g + f - 2, 1), 0], gate_b[:, bass.ds(4 * g + f - 2, 1)], ACT.Copy)\
                            .then_inc(merged_hi, 1)
            nc.scalar.preload_act_table(ACT.Sqrt)
            u0, t0, p0, _ = FIRST_OF["mix"]
            act.wait_ge(tile_empty, t0)
            act.wait_ge(merged_lo, KT)
            with act.Fori(0, 2) as g:
                for n in range(2):
                    tg, pg = t0 + 4 * g + 2 * n, p0 + 6 * g + 3 * n
                    for j in range(2, 8):
                        split_at(u0 + 8 * n, j, tg, pg, 8, 2, g, 16)
                    for t in range(NT):
                        bank = 2 * n + t
                        if t == 1:
                            for j in (8, 9):
                                split_at(u0 + 8 * n, j, tg, pg, 8, 2, g, 16)
                        act.wait_ge(tile_ready, t0 + 4 * g + bank + 1)
                        act.wait_ge(tile_half, t0 + 4 * g + bank)
                        A(junk_m[:, 0:UC], ps[:, bank, :], ACT.Square,
                          accum_out=stat[:, bass.ds(8 + 4 * t + 2 * g + n, 1)]).then_inc(tile_half, 1)
            act.wait_ge(sum_f, 1)
            A(stat[:, 18:20], stat[:, 16:18], ACT.Sqrt, bias=eps_t[:], scale=1.0 / D).then_inc(rms_y, 1)
            for t in range(NT):
                act.wait_ge(x1_ready, t + 1)
                if t:
                    act.wait_ge(ssq_1, t)
                A(junk_m[:], x1[:, t], ACT.Square, accum_out=stat[:, 4 + t:5 + t]).then_inc(ssq_1, 1)
            act.wait_ge(ssq_1, 2)
            A(stat[:, 6:8], stat[:, 4:6], ACT.Sqrt, bias=eps_t[:], scale=1.0 / D).then_inc(rms_1, 1)
            nc.scalar.preload_act_table(ACT.Gelu_apprx_tanh)
            for b in range(0, 8, 2):
                act.wait_ge(x1t_psum, b + 1)
                for k in range(2):
                    kt = 2 * b + k
                    ins = A(h2_f[:, kt], ps[:, b, k * S:(k + 1) * S], ACT.Identity, bias=mod[:, 3, kt:kt + 1],
                            scale=mod[:, 4, kt:kt + 1])
                own.mark(ins)
                act.wait_ge(h2_ready, b // 2 + 1)
                own.wait()
                A(h2t[:, 2 * b:2 * b + 4, 0], h2_f[:, 2 * b:2 * b + 4], ACT.Copy).then_inc(h2_hi, 1)
            u0, t0, p0, _ = FIRST_OF["ffn"]
            for j in (2, 3):
                split_at(u0, j, t0, p0)
            with act.Fori(0, FF // UC) as g:

                def split_ffn(part, j):
                    split_at(u0 + 8 * part, j, t0 + 8 * g + 4 * part, p0 + 6 * g + 3 * part, 8, 4, g, 16)

                def tap(part, n):
                    ft = part * (FF // P) + 4 * g + n
                    act.wait_ge(tile_empty, t0 + 8 * g + 4 * part + n + 1)
                    dst = conv_a[:, n] if part == 0 else conv_v[:, n]
                    if part == 0 and n == 0:
                        act.wait_ge(hid_ready, 4 * g + 1)
                    A(dst, conv_in[:, n, 2:S + 2], ACT.Identity, bias=vec[:, bass.ds(V_CB + ft, 1)],
                      scale=vec[:, bass.ds(V_CW + 2 * (2 * FF // P) + ft, 1)]).then_inc(conv_first, 1)

                def gelu(n):
                    act.wait_ge(conv_done, 8 * g + n + 2)
                    A(conv_a[:, n], conv_a[:, n], ACT.Gelu_apprx_tanh).then_inc(gelu_done, 1)

                def hidden_hi(n):
                    act.wait_ge(hid_ready, 4 * g + n + 2)
                    A(hid[:, bass.ds(4 * g + n, 1), 0].rearrange("p o t -> p (o t)"), hid_f[:, n % 2], ACT.Copy)\
                        .then_inc(hid_hi, 1)

                for part in range(2):
                    for j in range(4, 8):
                        split_ffn(part, j)
                    for f in range(4):
                        half_tile(t0 + 8 * g + 4 * part + f, f)
                        if 1 <= f <= 2:
                            tap(part, f - 1)
                    for j in (8, 9):
                        split_ffn(part, j)
                    second = gelu if part == 0 else hidden_hi
                    tap(part, 2)
                    second(0)
                    tap(part, 3)
                    second(1)
                    for j in (10, 11):
                        split_ffn(part, j)
                    second(2)
                    second(3)
            nc.scalar.preload_act_table(ACT.Sqrt)
            u0, t0, p0, _ = FIRST_OF["down"]
            for g in range(2):
                for n in range(2):
                    first, tg, pg = u0 + 44 * g + 22 * n, t0 + 4 * g + 2 * n, p0 + 20 * g + 10 * n
                    for j in range(2 if g or n else 4, 22):
                        split_at(first, j, tg, pg, 22, 2)
                    for t in range(NT):
                        bank = 2 * n + t
                        if t == 1:
                            for j in (22, 23):
                                split_at(first, j, tg, pg, 22, 2)
                        act.wait_ge(tile_ready, t0 + 4 * g + bank + 1)
                        act.wait_ge(tile_half, t0 + 4 * g + bank)
                        A(junk_f[:], ps[:, bank, :], ACT.Square,
                          accum_out=stat[:, 8 + 4 * t + 2 * g + n:9 + 4 * t + 2 * g + n]).then_inc(tile_half, 1)
            act.wait_ge(sum_f, 2)
            A(stat[:, 22:24], stat[:, 20:22], ACT.Sqrt, bias=eps_t[:], scale=1.0 / D).then_inc(rms_f, 1)

        @block.vector
        def _(dve):
            V = nc.vector
            own = Steps(dve, dve_step)

            def chain(ins):
                own.mark(ins)
                own.wait()

            def split(u, slot):
                dve.wait_ge(hi_done, u + 1)
                V.tensor_tensor(w_lo[:, slot], raw[:, slot], w_hi[:, slot].bitcast(F32), ALU.subtract)\
                    .then_inc(lo_done, 1)

            def ada_unit(a, slot, kt, half, loaded, guard=True, dst=acc):
                dve.wait_ge(ada_loaded[slot], loaded)
                if guard:
                    dve.wait_ge(ada_used, a - 1)
                part = dst[:, half * AC:(half + 1) * AC]
                if isinstance(kt, int) and kt == 0:
                    ins = V.tensor_scalar(part, ada[:, slot], c_act[:, 0:1], None, ALU.mult)
                else:
                    ins = V.scalar_tensor_tensor(part, ada[:, slot], c_act[:, bass.ds(kt, 1)], part, ALU.mult, ALU.add)
                ins.then_inc(ada_used, 1)

            def split_at(u0, j, g=None, per=8):
                u = u0 + 2 + j
                if u < UNITS:
                    split(u if g is None else u + per * g, u % RING)

            def ada_at(a, n, kt, g=None, per=8):
                if a is None:
                    return
                av = a + n if g is None else a + n + (per // 2) * g
                loaded = 16 * ((a + n) // RING + 1)
                if g is not None:
                    loaded = loaded + 16 * (per // 2 // RING) * g
                ada_unit(av, (a + n) % RING, kt + n // 2, n % 2, loaded)

            def inner(u0, nu, a=None, kt=None, g=None, per=8, beside=None, j0=2):
                for j in range(j0, nu):
                    split_at(u0, j, g, per)
                    if j % 2 == 1:
                        ada_at(a, j // 2 - 1, kt, g, per)
                        if beside is not None:
                            beside()

            def features(u0, t0, nu, dst, a=None, kt=None, g=None, per=8, scale=None, beside=None,
                         j0=2):
                inner(u0, nu, a, kt, g, per, beside, j0)
                for f in range(4):
                    if f == 3:
                        split_at(u0, nu, g, per)
                    sum_tile(t0 + f, f, dst(f), scale)
                split_at(u0, nu + 1, g, per)
                ada_at(a, nu // 2 - 1, kt, g, per)
                if beside is not None:
                    beside()

            def sum_tile(t, bank, dst, scale=None):
                dve.wait_ge(tile_half, t + 1)
                if scale is None:
                    ins = V.tensor_tensor(dst, ps[:, bank, 0:S], cross[:, bank % 2], ALU.add)
                else:
                    ins = V.scalar_tensor_tensor(dst, ps[:, bank, 0:S], scale, cross[:, bank % 2], ALU.mult, ALU.add)
                ins.then_inc(tile_empty, 1)

            dve.wait_ge(const_loaded, 2 * 16)
            chain(V.tensor_copy(pos_f[:], pos_i[:]))
            chain(V.tensor_scalar(ang[:], pos_f[:], inv_freq[:, 0:1], None, ALU.mult))
            round_c = 12582912.0
            V.tensor_scalar(turn[:, 0], ang[:], float(0.5 / np.pi), 0.25, ALU.mult, ALU.add)
            chain(V.tensor_scalar(turn[:, 1], ang[:], float(0.5 / np.pi), None, ALU.mult))
            chain(V.tensor_scalar(turn[:], turn[:], round_c, None, ALU.add))
            chain(V.tensor_scalar(turn[:], turn[:], -round_c, None, ALU.add))
            for n in range(2):
                own.mark(V.scalar_tensor_tensor(red[:, n], turn[:, n], -6.28125, ang[:], ALU.mult, ALU.add))
            own.wait()
            for part in (-0.0019350051879882812, -3.019916050561733e-07):
                chain(V.scalar_tensor_tensor(red[:], turn[:], part, red[:], ALU.mult, ALU.add))
            chain(V.tensor_scalar(red[:, 0], red[:, 0], float(np.pi / 2), None, ALU.add))
            V.tensor_scalar(red[:], red[:], 3.1415925, -3.1415925, ALU.min, ALU.max).then_inc(angle_ready, 1)

            dve.wait_ge(c_ready, 1)

            def take_mod(n, dst, base, bank=4):
                dve.wait_ge(mod_psum, n + 1)
                return V.tensor_tensor(mod[:, dst], ps[:, bank, 0:KT], vec[:, base:base + KT], ALU.add)

            def one_plus_times(dst, gain):
                return V.scalar_tensor_tensor(mod[:, dst], mod[:, dst], 1.0, vec[:, gain:gain + KT], ALU.add, ALU.mult)

            def first_ada(half, i, r):
                a = ADA_BLOCK * half + 4 * i + r
                ada_unit(a, r, 2 * i + r // 2, half, 16 * (8 * half + i + 1), not isinstance(a, int) or a >= 2,
                         (acc, acc_2)[r % 2])

            def take_first_mod(half):
                dve.wait_ge(mod_psum, half + 1)
                k0 = 8 * half
                for n in range(2):
                    own.mark(V.tensor_tensor(mod[:, n, k0:k0 + 8], ps[:, 4, 8 * n:8 * n + 8],
                                             vec[:, V_BADA + n * KT + k0:V_BADA + n * KT + k0 + 8], ALU.add))
                own.wait()
                V.scalar_tensor_tensor(mod[:, 1, k0:k0 + 8], mod[:, 1, k0:k0 + 8], 1.0,
                                       vec[:, V_GPRE + k0:V_GPRE + k0 + 8], ALU.add, ALU.mult).then_inc(mod_ready, 1)
                dve.wait_ge(mod_ready, half + 1)

            def input_f(q):
                for kt in range(4 * q, 4 * q + 4):
                    ins = V.tensor_scalar(h_f[:, kt], xn_t[:, kt], mod[:, 1, kt:kt + 1], mod[:, 0, kt:kt + 1],
                                          ALU.mult, ALU.add)
                ins.then_inc(h_ready, 1)

            def input_lo(q):
                dve.wait_ge(h_hi, q + 1)
                dve.wait_ge(h_ready, q + 1)
                ks = slice(4 * q, 4 * q + 4)
                V.tensor_tensor(ht[:, ks, 1], h_f[:, ks], ht[:, ks, 0].bitcast(F32), ALU.subtract).then_inc(h_lo, 1)

            for i in range(3):
                for r in range(RING):
                    first_ada(0, i, r)
            dve.wait_ge(rms_x, 1)
            V.reciprocal(stat[:, 2:4], stat[:, 2:4]).then_inc(recip_x, 1)
            dve.wait_ge(masks_loaded, 16)
            V.tensor_copy(masks[:], masks_i[:])
            with dve.Fori(3, KT // 2) as i:
                for r in range(RING):
                    first_ada(0, i, r)
            pieces = [lambda: take_first_mod(0), lambda: input_f(0), lambda: split(0, 0), lambda: split(1, 1),
                      lambda: input_lo(0), lambda: split(2, 2), lambda: split(3, 3), lambda: input_f(1),
                      lambda: input_lo(1)]
            dve.wait_ge(xt_copied, 8)
            for i in range(KT // 2):
                for r in range(RING):
                    first_ada(1, i, r)
                    if i >= 2 and r % 2 == 1 and pieces:
                        pieces.pop(0)()
            for j in (2, 3):
                split_at(0, j)
            take_first_mod(1)
            for q in (2, 3):
                input_f(q)
                input_lo(q)
            for name, kt in (("misc", 0), ("qlat", 2)):
                u0, t0, _, a0 = FIRST_OF[name]
                dsts = ([lat[:, 0], lat[:, 1], k_rope_in[:], lr_t[:]] if name == "misc"
                        else [lat[:, 2 + f] for f in range(4)])
                j0 = 2
                if name == "misc":
                    ada_at(a0, 0, kt)
                    j0 = 4
                features(u0, t0, 8, lambda f: dsts[f], a0, kt, j0=j0)

            def latents_at(step):
                if step == 0:
                    dve.wait_ge(lat_rms, 1)
                    chain(V.reciprocal(lat_r[:], lat_r[:]))
                if step == 1:
                    for i in range(6):
                        gain = V_GKV + i if i < 2 else V_GQ + i - 2
                        ins = V.scalar_tensor_tensor(lat[:, i], lat[:, i], vec[:, gain:gain + 1],
                                                     lat_r[:, 0 if i < 2 else 1], ALU.mult, ALU.mult)
                    ins.then_inc(lat_normed, 1)
                if step == 3:
                    dve.wait_ge(lat_hi, 1)
                    V.tensor_tensor(lat_s[:, :, 1], lat[:], lat_s[:, :, 0].bitcast(F32), ALU.subtract)\
                        .then_inc(lat_lo, 1)

            u0, t0, _, a0 = FIRST_OF["gq"]
            features(u0, t0, 8, lambda f: q_gla[:, f], a0, 4, scale=GLA_SCALE)
            latents_at(0)
            latent_steps = iter((1, 2, 3, 4))
            features(u0 + 8, t0 + 4, 8, lambda f: q_gla[:, 4 + f], a0 + 4, 6, scale=GLA_SCALE,
                     beside=lambda: latents_at(next(latent_steps)))
            u0, t0, _, _ = FIRST_OF["qup"]
            for g in range(3):
                features(u0 + 2 * g, t0 + 4 * g, 2, lambda f: q_nope[:, 4 * g + f] if g < 2 else q_rope_in[:, f])
            u0, t0, _, _ = FIRST_OF["kup"]
            for n in range(8):
                if n == 7:
                    split_at(u0, 2)
                sum_tile(t0 + n, n % 4, k_nope[:, n])
            split_at(u0, 3)
            u0, t0, _, _ = FIRST_OF["vup"]
            for n in range(4):
                half, t = n // 2, n % 2
                dve.wait_ge(tile_half, t0 + n + 1)
                V.tensor_copy(v_mla[:, t, half * UC:half * UC + S], ps[:, n, 0:S]).then_inc(tile_empty, 1)
                if n >= 2:
                    split_at(u0, n)
            dve.wait_ge(table_ready, 2)
            dve.wait_ge(rot_ready, 1)
            for i in range(4):
                V.tensor_tensor(rope_tmp[:, i % 2], ps[:, 4 + i // 2, (i % 2) * S:(i % 2 + 1) * S], sin_t[:], ALU.mult)
                chain(V.tensor_tensor(q_rope[:, i], q_rope_in[:, i], cos_t[:], ALU.mult))
                V.tensor_tensor(q_rope[:, i], q_rope[:, i], rope_tmp[:, i % 2], ALU.add).then_inc(rope_done, 1)
            V.tensor_tensor(rope_tmp[:, 0], ps[:, 6, 0:S], sin_t[:], ALU.mult)
            chain(V.tensor_tensor(k_rope[:], k_rope_in[:], cos_t[:], ALU.mult))
            V.tensor_tensor(k_rope[:], k_rope[:], rope_tmp[:, 0], ALU.add).then_inc(rope_done, 1)

            def mask_and_max(h):
                dve.wait_ge(scores_ready, h + 1)
                if h >= 3:
                    dve.wait_ge(pt_ready, h - 2)
                k = h % 3

                def diagonal(v):
                    return v.rearrange("p (a b) -> p a b", b=2 * P)[:, :, 0:P]

                V.tensor_copy(probs[:, k, P:2 * P], ps[:, 4, P:2 * P])
                bias = causal[:].rearrange("p (o n) -> p o n", o=1).to_broadcast([P, 2, P])
                chain(V.tensor_tensor(diagonal(probs[:, k]), diagonal(ps[:, 4]), bias, ALU.add))
                V.tensor_reduce(soft[:, k, 0:1], probs[:, k, 0:P], AX, ALU.max)
                chain(V.tensor_reduce(soft[:, k, 1:2], probs[:, k, P:3 * P], AX, ALU.max))
                V.tensor_scalar(soft[:, k, 0:2], soft[:, k, 0:2], -MLA_SCALE, None, ALU.mult).then_inc(max_ready, 1)

            def normalise(h):
                dve.wait_ge(exp_done, 2 * h + 2)
                k = h % 3
                chain(V.reciprocal(soft[:, k, 4:6], soft[:, k, 2:4]))
                V.tensor_scalar(probs[:, k, 0:P], probs[:, k, 0:P], soft[:, k, 4:5], None, ALU.mult)
                V.tensor_scalar(probs[:, k, P:3 * P], probs[:, k, P:3 * P], soft[:, k, 5:6], None, ALU.mult)\
                    .then_inc(probs_ready, 1)

            def context_lo(h):
                dve.wait_ge(ctx_hi, h + 1)
                V.tensor_tensor(ot[:, h, 1], ps[:, 6, 0:S], ot[:, h, 0].bitcast(F32), ALU.subtract).then_inc(ctx_lo, 1)

            def mla_at(step):
                h, odd = step // 2, step % 2
                if odd:
                    if h < H:
                        mask_and_max(h)
                    if 0 <= h - 2 < H:
                        context_lo(h - 2)
                elif 0 <= h - 1 < H:
                    normalise(h - 1)

            def gate_bias(n):
                dve.wait_ge(gate_psum, n + 1)
                for i in range(4):
                    ft = 4 * n + i
                    V.tensor_scalar(suf[:, ft], ps[:, 6 + i // 2, (i % 2) * S:(i % 2 + 1) * S],
                                    vec[:, V_BGLA + ft:V_BGLA + ft + 1], None, ALU.add).then_inc(gate_pre, 1)

            def log_decay():
                dve.wait_ge(gate_soft, 1)
                chain(V.scalar_tensor_tensor(pre[:], suf[:], 0.0, dec[:], ALU.min, ALU.subtract))
                V.tensor_scalar(pre[:], pre[:], 1.0 / TAU, None, ALU.mult)
                V.memset(suf[:], 0.0).then_inc(decay_ready, 1)
                dve.wait_ge(decay_ready, 1)

            def products(lv):
                h = 1 << (lv - 1)
                dve.wait_ge(dec_ready, lv)
                dve.wait_ge(level_ready, lv)
                V.tensor_tensor(halves(qk, h)[1], halves(q_gla, h)[1], halves(dec, h)[1], ALU.mult)
                V.tensor_tensor(halves(qk, h)[0], halves(k_gla, h)[0], halves(dec, h)[0], ALU.mult).then_inc(qk_ready, 1)

            def select(lv):
                dve.wait_ge(level_ready, lv + 1)

                def by_head(b, n=P):
                    return ps[:, b, 0:GH * n].rearrange("p (h n) -> p h n", h=GH)

                if lv == 0:
                    dve.wait_ge(attn_zero, 2)
                    m = masks[:, 0:1, :].to_broadcast([P, GH, P])
                    V.copy_predicated(attn0[:, :, 0:P], m, by_head(6))
                    V.copy_predicated(attn1[:], m, by_head(7)).then_inc(level_taken, 1)
                elif lv < LEVELS - 1:
                    h = 1 << (lv - 1)

                    def second(v):
                        return v.rearrange("p (b s h) -> p b s h", s=2, h=h)[:, :, 1]

                    m = second(masks[:, lv])
                    for b, dst in ((6, attn0[:, :, 0:P]), (7, attn1)):
                        for hd in range(GH):
                            src = ps[:, b, hd * P // 2:(hd + 1) * P // 2].rearrange("p (b h) -> p b h", h=h)
                            ins = V.copy_predicated(second(dst[:, hd]), m, src)
                    ins.then_inc(level_taken, 1)
                else:
                    V.tensor_copy(attn0[:, :, P:S], by_head(6)).then_inc(level_taken, 1)
                dve.wait_ge(level_taken, lv + 1)

            def gla_norm(n):
                i = n % 4
                if n < 4:
                    dve.wait_ge(og_rms, 1)
                    own.mark(V.reciprocal(o_r[:, i], o_r[:, i]))
                elif n < 8:
                    own.wait()
                    part = o_gla[:, 4 * i:4 * i + 4]
                    own.mark(V.tensor_tensor(part, part, o_r[:, i:i + 1].to_broadcast([P, 4, S]), ALU.mult))
                else:
                    own.wait()
                    dve.wait_ge(og_silu, 1)
                    part, gate = (b[:].rearrange("p (h i) t -> p h i t", i=4)[:, :, i] for b in (o_gla, og))
                    V.scalar_tensor_tensor(part, part, vec[:, V_GOUT + i:V_GOUT + i + 1], gate, ALU.mult, ALU.mult)\
                        .then_inc(og_gated, 1)

            steps = [0]

            def beside():
                step = steps[0]
                steps[0] += 1
                mla_at(step)
                if step in (20, 21):
                    gate_bias(step - 20)
                if step == 22:
                    log_decay()
                if step % 2 == 0 and 1 <= (step - 22) // 2 <= LEVELS - 1:
                    lv = (step - 22) // 2
                    products(lv)
                if step % 2 == 1 and 0 <= (step - 25) // 2 <= LEVELS - 1:
                    select((step - 25) // 2)
                if 52 <= step < 64:
                    gla_norm(step - 52)

            def column(buf, n):
                return buf[:, bass.ds(n, 1)].rearrange("p o t -> p (o t)")

            beside()
            u0, t0, _, a0 = FIRST_OF["gk"]
            for g in range(2):
                features(u0 + 8 * g, t0 + 4 * g, 8, lambda f: k_gla[:, 4 * g + f], a0 + 4 * g, 8 + 2 * g, beside=beside)
            u0, t0, _, a0 = FIRST_OF["gv"]
            for g in range(4):
                if g == 2:
                    take_mod(2, 3, V_BADA + 3 * KT).then_inc(mod_ready, 1)
                kt = 12 + 2 * g if g < 2 else 2 * g - 4
                inner(u0 + 8 * g, 8, a0 + 4 * g, kt, beside=beside)
                for t in range(NT):
                    n = t0 + 2 * g + t
                    if t == 1:
                        for j in (8, 9):
                            split_at(u0 + 8 * g, j)
                    dve.wait_ge(tile_half, n + 1)
                    V.tensor_copy(v_gla[:, t, g * UC:g * UC + S], ps[:, n % 4, 0:S]).then_inc(tile_empty, 1)
                ada_at(a0 + 4 * g, 3, kt)
                beside()
            u0, t0, _, a0 = FIRST_OF["og"]
            for g in range(4):
                features(u0 + 8 * g, t0 + 4 * g, 8, lambda f: og[:, 4 * g + f], a0 + 4 * g, 4 + 2 * g, beside=beside)
            u0, t0, _, a0 = FIRST_OF["ga"]
            for g in range(4):
                if g == 2:
                    chain(take_mod(3, 4, V_BADA + 4 * KT, 6))
                    one_plus_times(4, V_GFFN).then_inc(mod_ready, 1)
                kt = 12 + 2 * g if g < 2 else 2 * g - 4
                features(u0 + 8 * g, t0 + 4 * g, 8, lambda f: gate_a[:, 4 * g + f], a0 + 4 * g, kt, beside=beside)
            for g in (4, 5):
                features(u0 + 8 * g, t0 + 4 * g, 8, lambda f: gate_b[:, 4 * g + f - 16], a0 + 4 * g, 2 * g - 4,
                         beside=beside)
            with dve.Fori(6, 8) as g:
                features(u0, t0 + 4 * g, 8, lambda f: column(gate_b, 4 * g + f - 16), a0, 2 * g - 4, g)
            for q in range(4):
                dve.wait_ge(og_hi, q + 1)
                ks = slice(4 * q, 4 * q + 4)
                V.tensor_tensor(og_s[:, ks, 1], o_gla[:, ks], og_s[:, ks, 0].bitcast(F32), ALU.subtract)\
                    .then_inc(og_lo, 1)
            u0, t0, _, a0 = FIRST_OF["ba"]
            dve.wait_ge(sig_done, 8)
            n0 = own.n
            with dve.Fori(0, 2) as g:
                own.n = n0 + 8 * g
                for n in range(2):
                    a, kt = a0 + 2 * n, 12 + 2 * g + n
                    inner(u0 + 4 * n, 4, a, kt, g)
                    ada_at(a, 1, kt, g)
                    for f in range(4):
                        if f == 3:
                            split_at(u0 + 4 * n, 4, g)
                        sum_tile(t0 + 8 * g + 4 * n + f, f, ytmp[:, f % 2])
                        dve.wait_ge(tile_empty, t0 + 8 * g + 4 * n + f + 1)
                        dst = column(gate_a, 8 * g + 4 * n + f)
                        own.mark(V.tensor_tensor(dst, dst, ytmp[:, f % 2], ALU.mult))
                    split_at(u0 + 4 * n, 5, g)
            own.n = n0 + 16
            own.wait()

            def gate_gain(n, dst, gpost):
                dve.wait_ge(gate_row, n + 1)
                for b in range(4):
                    cols = slice(b * UC, (b + 1) * UC)
                    ins = V.tensor_tensor(dst[:, cols], ps[:, 4 + b, :], gpost[:, cols], ALU.mult)
                ins.then_inc(gg_ready, 1)

            dve.wait_ge(post_loaded, 16 * 5)
            dve.wait_ge(gate_row, 1)
            V.memset(acc[:], 0.0).then_inc(acc_zero, 1)
            dve.wait_ge(acc_zero, 1)
            gate_gain(0, gg_m, gpost_m)
            u0, t0, _, a0 = FIRST_OF["bb"]
            n0 = own.n
            with dve.Fori(0, 4) as g:
                own.n = n0 + 4 * g
                inner(u0, 8, a0, 2 * g, g)
                for f in range(7):
                    if f == 3:
                        split_at(u0, 8, g)
                    if f < 4:
                        sum_tile(t0 + 4 * g + f, f, ytmp[:, f % 2])
                        dve.wait_ge(tile_empty, t0 + 4 * g + f + 1)
                        y, gb = ytmp[:, f % 2], column(gate_b, 4 * g + f)
                        chain(V.tensor_tensor(y, y, gb, ALU.mult))
                        V.tensor_tensor(gb, y, column(gate_a, 4 * g + f), ALU.add).then_inc(merged_ready, 1)
                    if f == 3:
                        split_at(u0, 9, g)
                        ada_at(a0, 3, 2 * g, g)
                    if f >= 3:
                        kt = 4 * g + f - 3
                        dve.wait_ge(merged_hi, kt + 1)
                        V.tensor_tensor(column(merged[:, :, 1], kt), column(gate_b, kt),
                                        column(merged[:, :, 0], kt).bitcast(F32), ALU.subtract).then_inc(merged_lo, 1)
            own.n = n0 + 16
            u0, t0, _, a0 = FIRST_OF["mix"]
            with dve.Fori(0, 2) as g:
                for n in range(2):
                    a, kt = a0 + 4 * n, 8 + 4 * g + 2 * n
                    inner(u0 + 8 * n, 8, a, kt, g, 16)
                    for t in range(NT):
                        bank = 2 * n + t
                        if t == 1:
                            for j in (8, 9):
                                split_at(u0 + 8 * n, j, g, 16)
                            ada_at(a, 3, kt, g, 16)
                        dve.wait_ge(tile_half, t0 + 4 * g + bank + 1)
                        cols = bass.ds(2 * UC * g + UC * n, UC)
                        V.tensor_tensor(x1[:, t, cols], ps[:, bank, :], gg_m[:, cols], ALU.mult).then_inc(tile_empty, 1)
            V.tensor_reduce(stat[:, 16:18], stat[:, 8:16].rearrange("p (t n) -> p t n", t=2), AX, ALU.add)\
                .then_inc(sum_f, 1)
            dve.wait_ge(rms_y, 1)
            chain(V.reciprocal(stat[:, 18:20], stat[:, 18:20]))
            dve.wait_ge(x_again_loaded, 16)
            dve.wait_ge(tile_empty, FIRST_OF["ffn"][1])
            for t in range(NT):
                V.scalar_tensor_tensor(x1[:, t], x1[:, t], stat[:, 18 + t:19 + t], x_again[:, t], ALU.mult, ALU.add)\
                    .then_inc(x1_ready, 1)
            dve.wait_ge(x1_ready, 2)
            dve.wait_ge(rms_1, 1)
            chain(V.reciprocal(stat[:, 6:8], stat[:, 6:8]))
            for t in range(NT):
                V.tensor_scalar(xn1[:, t], x1[:, t], stat[:, 6 + t:7 + t], None, ALU.mult).then_inc(norm_1, 1)
            for b in range(1, 8, 2):
                dve.wait_ge(x1t_psum, b + 1)
                for k in range(2):
                    kt = 2 * b + k
                    ins = V.tensor_scalar(h2_f[:, kt], ps[:, b, k * S:(k + 1) * S], mod[:, 4, kt:kt + 1],
                                          mod[:, 3, kt:kt + 1], ALU.mult, ALU.add)
                ins.then_inc(h2_ready, 1)
                for q in {1: (), 3: (0,), 5: (1,), 7: (2, 3)}[b]:
                    dve.wait_ge(h2_hi, q + 1)
                    ks = slice(4 * q, 4 * q + 4)
                    V.tensor_tensor(h2t[:, ks, 1], h2_f[:, ks], h2t[:, ks, 0].bitcast(F32), ALU.subtract)\
                        .then_inc(h2_lo, 1)
            dve.wait_ge(ada_used, 6 * ADA_BLOCK)
            chain(V.memset(conv_in[:, :, 0:2], 0.0))
            for n, s in enumerate((conv_done, hid_ready, hid_lo)):
                V.memset(hid_f[:, 0, n:n + 1], 0.0).then_inc(s, 1)
            dve.wait_ge(hid_lo, 1)
            u0, t0, _, _ = FIRST_OF["ffn"]
            n0 = own.n
            for j in (2, 3):
                split_at(u0, j)
            with dve.Fori(0, FF // UC) as g:
                own.n = n0 + 8 * g

                def sum_conv(part, f):
                    if part or f == 0:
                        dve.wait_ge(conv_done, 8 * g + (f + 2 if part else 1))
                    sum_tile(t0 + 8 * g + 4 * part + f, f, conv_in[:, f, 2:S + 2])

                def taps(part, n):
                    ft = part * (FF // P) + 4 * g + n
                    dve.wait_ge(conv_first, 8 * g + 4 * part + n + 1)
                    dst = conv_a[:, n] if part == 0 else conv_v[:, n]
                    chain(V.scalar_tensor_tensor(dst, conv_in[:, n, 1:S + 1],
                                                 vec[:, bass.ds(V_CW + 2 * FF // P + ft, 1)], dst,
                                                 ALU.mult, ALU.add))
                    V.scalar_tensor_tensor(dst, conv_in[:, n, 0:S], vec[:, bass.ds(V_CW + ft, 1)], dst,
                                           ALU.mult, ALU.add).then_inc(conv_done, 1)

                def hidden(n):
                    dve.wait_ge(gelu_done, 4 * g + n + 1)
                    dve.wait_ge(hid_lo, 4 * g + max(n, 1))
                    dve.wait_ge(conv_done, 8 * g + 4 + n + 2)
                    V.tensor_tensor(hid_f[:, n % 2], conv_a[:, n], conv_v[:, n], ALU.mult).then_inc(hid_ready, 1)

                def hidden_lo(n):
                    dve.wait_ge(hid_hi, 4 * g + n + 1)
                    V.tensor_tensor(column(hid[:, :, 1], 4 * g + n), hid_f[:, n % 2],
                                    column(hid[:, :, 0], 4 * g + n).bitcast(F32), ALU.subtract).then_inc(hid_lo, 1)

                for part in range(2):
                    for j in range(4, 8):
                        split_at(u0 + 8 * part, j, g, 16)
                    for f in range(3):
                        sum_conv(part, f)
                        if f >= 1:
                            taps(part, f - 1)
                        if f >= 2 and part:
                            hidden(0)
                    split_at(u0 + 8 * part, 8, g, 16)
                    sum_conv(part, 3)
                    split_at(u0 + 8 * part, 9, g, 16)
                    taps(part, 2)
                    if part:
                        hidden(1)
                        hidden_lo(0)
                    taps(part, 3)
                    if part:
                        hidden(2)
                        hidden_lo(1)
                    split_at(u0 + 8 * part, 10, g, 16)
                    split_at(u0 + 8 * part, 11, g, 16)
                    if part:
                        hidden(3)
                        hidden_lo(2)
                        hidden_lo(3)
            own.n = n0 + 8 * (FF // UC)
            u0, t0, _, _ = FIRST_OF["down"]
            for g in range(2):
                for n in range(2):
                    first = u0 + 44 * g + 22 * n
                    for j in range(2 if g or n else 4, 22):
                        split_at(first, j)
                        if g == 0 and n == 0 and j == 5:
                            dve.wait_ge(post_f_loaded, 16)
                            gate_gain(1, gg_f, gpost_f)
                    for t in range(NT):
                        bank = 2 * n + t
                        if t == 1:
                            for j in (22, 23):
                                split_at(first, j)
                        dve.wait_ge(tile_half, t0 + 4 * g + bank + 1)
                        cols = slice((2 * g + n) * UC, (2 * g + n + 1) * UC)
                        V.tensor_tensor(f_tok[:, t, cols], ps[:, bank, :], gg_f[:, cols], ALU.mult)\
                            .then_inc(tile_empty, 1)
            V.tensor_reduce(stat[:, 20:22], stat[:, 8:16].rearrange("p (t n) -> p t n", t=2), AX, ALU.add)\
                .then_inc(sum_f, 1)
            dve.wait_ge(rms_f, 1)
            chain(V.reciprocal(stat[:, 22:24], stat[:, 22:24]))
            dve.wait_ge(tile_empty, FIRST_OF["down"][1] + 8)
            for n in range(4):
                t, c0 = n // 2, (n % 2) * (D // 2)
                part = f_tok[:, t, c0:c0 + D // 2]
                V.scalar_tensor_tensor(part, part, stat[:, 22 + t:23 + t], x1[:, t, c0:c0 + D // 2], ALU.mult, ALU.add)\
                    .then_inc(out_ready, 1)

        @block.gpsimd
        def _(pool):
            nc.gpsimd.memset(eps_t[:], EPS).then_inc(setup_done, 1)
            nc.gpsimd.memset(ones[:], 1.0).then_inc(setup_done, 1)
            pool.wait_ge(gate_psum, 1)
            nc.gpsimd.memset(attn0[:], 0.0).then_inc(attn_zero, 1)
            nc.gpsimd.memset(attn1[:], 0.0).then_inc(attn_zero, 1)
            for lv in range(1, LEVELS - 1):
                h = 1 << (lv - 1)
                p0, p1 = halves(pre, h)
                s0, _ = halves(suf, h)
                pool.wait_ge(dec_ready, lv)
                nc.gpsimd.tensor_tensor(s0, s0, spread(p1[:, :, h - 1:h], s0), ALU.add).then_inc(suffix_ready, 1)
                pool.wait_ge(suffix_ready, lv)
                nc.gpsimd.tensor_tensor(p1, p1, spread(p0[:, :, h - 1:h], p1), ALU.add).then_inc(scan_ready, 1)
                pool.wait_ge(scan_ready, lv)


def kernel(**inputs):
    import concourse.bacc as bacc
    from concourse.bass_utils import run_bass_kernel_spmd

    names = ["x", "c", "positions", "w_ada", "b_ada", "g_pre_mix", "w_in", "g_q_lat", "w_q_up", "g_kv_lat",
             "w_kv_up", "w_gla_gate_up", "b_gla_gate", "g_gla_out", "w_branch_a", "w_branch_b", "w_mix_out",
             "g_post_mix", "g_pre_ffn", "w_ffn_up", "conv_w", "conv_b", "w_ffn_down", "g_post_ffn"]
    nc = bacc.Bacc("TRN2", target_bir_lowering=False, num_devices=1, dynamic_dma_scratch_size=1024)
    arrays = {f"in_{n}": np.ascontiguousarray(inputs[n]) for n in names}
    arrays["in_constants"] = constants()
    arrays["in_masks"] = level_masks()
    args = []
    for n, a in arrays.items():
        t = nc.dram_tensor(n, a.shape, mybir.dt.from_np(a.dtype), kind="ExternalInput").ap()
        args.append(t[0] if n[3:].startswith("w_") else t)
    out = nc.dram_tensor("out", (1, S, D), F32, kind="ExternalOutput").ap()
    build(nc, args, out)
    r = run_bass_kernel_spmd(nc, [arrays], core_ids=[0])
    return r.results[0]["out"]
```
